# Optimizing a Trainium2 kernel written in Bass

```python
import math
import jax, jax.numpy as jnp
from jax import lax
import numpy as np

D_MODEL = 1024
BATCH = 1
SEQ = 512
DEPTH = 2

SSM_WIDTH = D_MODEL // 4
MLSTM_WIDTH = D_MODEL // 4
NSA_WIDTH = D_MODEL // 2
D_MIX = SSM_WIDTH + MLSTM_WIDTH + NSA_WIDTH
SSM_GROUP = 16
SSM_GROUPS = SSM_WIDTH // SSM_GROUP
SSM_STATE = 64
DT_MIN = 1e-3
DT_MAX = 1e-1
MLSTM_HEADS = 4
MLSTM_HEAD_DIM = MLSTM_WIDTH // MLSTM_HEADS
MLSTM_CHUNK = 128
MLSTM_CONV = 4
NSA_HEAD_DIM = 64
NSA_HEADS = NSA_WIDTH // NSA_HEAD_DIM
NSA_KV_GROUPS = 2
NSA_KV_WIDTH = NSA_KV_GROUPS * NSA_HEAD_DIM
CMP_BLOCK = 32
CMP_STRIDE = 16
CMP_HIDDEN = 256
SEL_BLOCK = 64
SEL_TOPN = 8
WINDOW = 256
Q_BLOCK = 128
FORCE_SCORE = 1e4
NEG_INF = -1e30
ROPE_THETA = 500000.0
ROPE_DIMS = NSA_HEAD_DIM // 4
D_FF = 4 * D_MODEL
EPS = 1e-6

IN_SPLITS = (SSM_WIDTH,
             MLSTM_WIDTH, MLSTM_WIDTH, MLSTM_WIDTH, MLSTM_WIDTH, MLSTM_HEADS, MLSTM_HEADS,
             NSA_WIDTH, NSA_KV_WIDTH, NSA_KV_WIDTH, NSA_KV_WIDTH, NSA_KV_WIDTH, NSA_KV_WIDTH, NSA_KV_WIDTH,
             3 * NSA_HEADS)
D_IN = SSM_WIDTH + 4 * MLSTM_WIDTH + 2 * MLSTM_HEADS + NSA_WIDTH + 6 * NSA_KV_WIDTH + 3 * NSA_HEADS

kernel_name = 'hybrid_s5_mlstm_nsa_sandwich'

F32 = jnp.float32

def _rmsnorm(x, g):
    xf = x.astype(F32)
    y = xf * lax.rsqrt(jnp.mean(xf * xf, axis=-1, keepdims=True) + EPS)
    return (y * g).astype(x.dtype)

def _group_rmsnorm(y, g, n_groups):
    shp = y.shape
    yf = y.astype(F32).reshape(*shp[:-1], n_groups, shp[-1] // n_groups)
    yf = yf * lax.rsqrt(jnp.mean(yf * yf, axis=-1, keepdims=True) + EPS)
    return yf.reshape(shp) * g

def _rope_tables(positions):
    inv = ROPE_THETA ** (-jnp.arange(0, ROPE_DIMS, 2, dtype=F32) / ROPE_DIMS)
    ang = positions.astype(F32)[..., None] * inv
    return jnp.cos(ang)[:, :, None, :], jnp.sin(ang)[:, :, None, :]

def _rope(x, cos, sin):
    half = ROPE_DIMS // 2
    x1 = x[..., :half]
    x2 = x[..., half:ROPE_DIMS]
    rot = jnp.concatenate([x1 * cos - x2 * sin, x2 * cos + x1 * sin], axis=-1)
    return jnp.concatenate([rot.astype(x.dtype), x[..., ROPE_DIMS:]], axis=-1)

def _masked_softmax(s, mask):
    s = jnp.where(mask, s.astype(F32), NEG_INF)
    p = jax.nn.softmax(s, axis=-1)
    return jnp.where(mask, p, 0.0)

def _causal_dwconv(x, w):
    K = w.shape[0]
    S = x.shape[1]
    xp = jnp.pad(x, ((0, 0), (K - 1, 0), (0, 0)))
    out = xp[:, 0:S] * w[0]
    for j in range(1, K):
        out = out + xp[:, j:j + S] * w[j]
    return out

def _s5_mixer(u, lam_re, lam_im, b_re, b_im, c_re, c_im, d_skip, log_dt, w_glu):
    Bsz, S, _ = u.shape
    uf = u.astype(F32).reshape(Bsz, S, SSM_GROUPS, SSM_GROUP)
    dt = jnp.exp(log_dt.astype(F32))[:, None]
    lr = lam_re.astype(F32)
    li = lam_im.astype(F32)
    mag = jnp.exp(lr * dt)
    ang = li * dt
    ab_re = mag * jnp.cos(ang)
    ab_im = mag * jnp.sin(ang)
    den = lr * lr + li * li
    g_re = ((ab_re - 1.0) * lr + ab_im * li) / den
    g_im = (ab_im * lr - (ab_re - 1.0) * li) / den
    br = b_re.astype(F32)
    bi = b_im.astype(F32)
    bb_re = g_re[..., None] * br - g_im[..., None] * bi
    bb_im = g_re[..., None] * bi + g_im[..., None] * br
    bu_re = jnp.einsum('bsgh,gph->bsgp', uf, bb_re)
    bu_im = jnp.einsum('bsgh,gph->bsgp', uf, bb_im)
    a_re = jnp.broadcast_to(ab_re, bu_re.shape)
    a_im = jnp.broadcast_to(ab_im, bu_im.shape)

    def combine(e1, e2):
        a1r, a1i, b1r, b1i = e1
        a2r, a2i, b2r, b2i = e2
        return (a2r * a1r - a2i * a1i,
                a2r * a1i + a2i * a1r,
                a2r * b1r - a2i * b1i + b2r,
                a2r * b1i + a2i * b1r + b2i)

    _, _, xr, xi = lax.associative_scan(combine, (a_re, a_im, bu_re, bu_im), axis=1)
    y = (jnp.einsum('bsgp,ghp->bsgh', xr, c_re.astype(F32))
         - jnp.einsum('bsgp,ghp->bsgh', xi, c_im.astype(F32))
         + d_skip.astype(F32).reshape(SSM_GROUPS, SSM_GROUP) * uf)
    y = jax.nn.gelu(y.reshape(Bsz, S, SSM_WIDTH))
    return y * jax.nn.sigmoid(y @ w_glu.astype(F32))

def _mlstm_mixer(q, k, v, o_pre, i_pre, f_pre, conv_w, b_i, b_f):
    Bsz, S, _ = q.shape
    H, Dh, L = MLSTM_HEADS, MLSTM_HEAD_DIM, MLSTM_CHUNK
    nc = S // L
    qk = jax.nn.silu(_causal_dwconv(jnp.concatenate([q, k], axis=-1), conv_w))
    q, k = jnp.split(qk, 2, axis=-1)

    def heads(t):
        return t.astype(F32).reshape(Bsz, nc, L, H, Dh).transpose(1, 0, 3, 2, 4)

    def gates(t):
        return t.reshape(Bsz, nc, L, H).transpose(1, 0, 3, 2)

    qh = heads(q)
    kh = heads(k) * (Dh ** -0.5)
    vh = heads(v)
    ig = gates(i_pre.astype(F32) + b_i.astype(F32))
    lf = gates(jax.nn.log_sigmoid(f_pre.astype(F32) + b_f.astype(F32)))
    causal = jnp.tril(jnp.ones((L, L), dtype=bool))

    def step(carry, xs):
        C, n, m = carry
        qc, kc, vc, ic, fc = xs
        b = jnp.cumsum(fc, axis=-1)
        dmat = b[..., :, None] - b[..., None, :] + ic[..., None, :]
        dmat = jnp.where(causal, dmat, -jnp.inf)
        inter = b + m[..., None]
        m_t = jnp.maximum(inter, jnp.max(dmat, axis=-1))
        w_intra = jnp.exp(dmat - m_t[..., None])
        w_inter = jnp.exp(inter - m_t)
        s = jnp.einsum('bhtd,bhsd->bhts', qc, kc) * w_intra
        num = (w_inter[..., None] * jnp.einsum('bhtd,bhde->bhte', qc, C)
               + jnp.einsum('bhts,bhse->bhte', s, vc))
        den = w_inter * jnp.einsum('bhtd,bhd->bht', qc, n) + jnp.sum(s, axis=-1)
        h = num / jnp.maximum(jnp.abs(den), jnp.exp(-m_t))[..., None]
        bL = b[..., -1]
        logw = bL[..., None] - b + ic
        m_new = jnp.maximum(bL + m, jnp.max(logw, axis=-1))
        wk = jnp.exp(logw - m_new[..., None])
        decay = jnp.exp(bL + m - m_new)
        C_new = decay[..., None, None] * C + jnp.einsum('bhs,bhsd,bhse->bhde', wk, kc, vc)
        n_new = decay[..., None] * n + jnp.einsum('bhs,bhsd->bhd', wk, kc)
        return (C_new, n_new, m_new), h

    init = (jnp.zeros((Bsz, H, Dh, Dh), F32), jnp.zeros((Bsz, H, Dh), F32), jnp.zeros((Bsz, H), F32))
    _, hs = lax.scan(step, init, (qh, kh, vh, ig, lf))
    h = hs.transpose(1, 0, 3, 2, 4).reshape(Bsz, S, MLSTM_WIDTH)
    return jax.nn.sigmoid(o_pre.astype(F32)) * h

def _compress(t, pe, w1, w2):
    Bsz, S, G, Dh = t.shape
    r = CMP_BLOCK // CMP_STRIDE
    ch = t.reshape(Bsz, S // CMP_STRIDE, CMP_STRIDE, G, Dh)
    n = S // CMP_STRIDE - (r - 1)
    blocks = jnp.concatenate([ch[:, j:j + n] for j in range(r)], axis=2)
    blocks = blocks + pe[None, None, :, None, :]
    flat = blocks.transpose(0, 1, 3, 2, 4).reshape(Bsz, n, G, CMP_BLOCK * Dh)
    return jax.nn.gelu(flat @ w1) @ w2

def _cmp_to_sel_overlap(n_cmp, n_sel):
    i = np.arange(n_cmp)[:, None]
    j = np.arange(n_sel)[None, :]
    lo = np.maximum(i * CMP_STRIDE, j * SEL_BLOCK)
    hi = np.minimum(i * CMP_STRIDE + CMP_BLOCK, (j + 1) * SEL_BLOCK)
    return jnp.asarray(np.maximum(hi - lo, 0) / CMP_STRIDE, dtype=F32)

def _nsa_mixer(q, k_c, v_c, k_s, v_s, k_w, v_w, g_pre, cos, sin,
               pe_k, w1_k, w2_k, pe_v, w1_v, w2_v):
    Bsz, S, _ = q.shape
    H, G, Dh = NSA_HEADS, NSA_KV_GROUPS, NSA_HEAD_DIM
    R = H // G
    scale = Dh ** -0.5
    t_idx = jnp.arange(S)
    qh = _rope(q.reshape(Bsz, S, H, Dh), cos, sin)
    qg = qh.reshape(Bsz, S, G, R, Dh)

    def kv(t):
        return t.reshape(Bsz, S, G, Dh)

    k_c = _rope(kv(k_c), cos, sin)
    k_s = _rope(kv(k_s), cos, sin)
    k_w = _rope(kv(k_w), cos, sin)
    v_c, v_s, v_w = kv(v_c), kv(v_s), kv(v_w)

    kcmp = _compress(k_c, pe_k, w1_k, w2_k)
    vcmp = _compress(v_c, pe_v, w1_v, w2_v)
    n_cmp = kcmp.shape[1]
    cmp_end = jnp.arange(n_cmp) * CMP_STRIDE + CMP_BLOCK - 1
    cmask = cmp_end[None, :] <= t_idx[:, None]
    sc = jnp.einsum('bsgrd,bngd->bgrsn', qg, kcmp) * scale
    p_c = _masked_softmax(sc, cmask)
    o_c = jnp.einsum('bgrsn,bngd->bsgrd', p_c, vcmp).reshape(Bsz, S, H, Dh)

    n_sel = S // SEL_BLOCK
    n_top = min(SEL_TOPN, n_sel)
    imp = jnp.einsum('bgrsn,nj->bgsj', p_c, _cmp_to_sel_overlap(n_cmp, n_sel))
    blk = jnp.arange(n_sel)
    valid = blk[None, :] * SEL_BLOCK <= t_idx[:, None]
    forced = (blk[None, :] == 0) | (blk[None, :] == (t_idx // SEL_BLOCK)[:, None])
    imp = jnp.where(forced, FORCE_SCORE, jnp.where(valid, imp, -FORCE_SCORE))
    _, sel_idx = lax.top_k(imp, n_top)

    nq = S // Q_BLOCK
    ks_blocks = k_s.reshape(Bsz, n_sel, SEL_BLOCK, G, Dh).transpose(0, 3, 1, 2, 4)
    vs_blocks = v_s.reshape(Bsz, n_sel, SEL_BLOCK, G, Dh).transpose(0, 3, 1, 2, 4)
    q_blk = qg.reshape(Bsz, nq, Q_BLOCK, G, R, Dh).transpose(1, 0, 3, 2, 4, 5)
    idx_blk = sel_idx.reshape(Bsz, G, nq, Q_BLOCK, n_top).transpose(2, 0, 1, 3, 4)
    t_blk = t_idx.reshape(nq, Q_BLOCK)
    b_ix = jnp.arange(Bsz)[:, None, None]
    g_ix = jnp.arange(G)[None, :, None]
    kk = n_top * SEL_BLOCK

    def sel_block(args):
        qb, ib, tb = args
        flat = ib.reshape(Bsz, G, Q_BLOCK * n_top)
        kg = ks_blocks[b_ix, g_ix, flat].reshape(Bsz, G, Q_BLOCK, kk, Dh)
        vg = vs_blocks[b_ix, g_ix, flat].reshape(Bsz, G, Q_BLOCK, kk, Dh)
        kpos = (ib[..., None] * SEL_BLOCK + jnp.arange(SEL_BLOCK)).reshape(Bsz, G, Q_BLOCK, kk)
        mask = kpos <= tb[None, None, :, None]
        s = jnp.einsum('bgtrd,bgtkd->bgrtk', qb, kg) * scale
        p = _masked_softmax(s, mask[:, :, None])
        return jnp.einsum('bgrtk,bgtkd->btgrd', p, vg)

    o_s = lax.map(sel_block, (q_blk, idx_blk, t_blk))
    o_s = o_s.transpose(1, 0, 2, 3, 4, 5).reshape(Bsz, S, H, Dh)

    nb = S // Q_BLOCK
    nprev = WINDOW // Q_BLOCK

    def band(t):
        tb = t.reshape(Bsz, nb, Q_BLOCK, G, Dh)
        tp = jnp.pad(tb, ((0, 0), (nprev, 0), (0, 0), (0, 0), (0, 0)))
        return jnp.concatenate([tp[:, j:j + nb] for j in range(nprev + 1)], axis=2)

    kwb = band(k_w)
    vwb = band(v_w)
    qpos = t_idx.reshape(nb, Q_BLOCK)
    kpos = (jnp.arange(nb)[:, None] - nprev) * Q_BLOCK + jnp.arange((nprev + 1) * Q_BLOCK)[None, :]
    wmask = ((kpos[:, None, :] >= 0) & (kpos[:, None, :] <= qpos[:, :, None])
             & (qpos[:, :, None] - kpos[:, None, :] < WINDOW))
    qw = qg.reshape(Bsz, nb, Q_BLOCK, G, R, Dh)
    sw = jnp.einsum('bitgrd,bikgd->bigrtk', qw, kwb) * scale
    p_w = _masked_softmax(sw, wmask[None, :, None, None])
    o_w = jnp.einsum('bigrtk,bikgd->bitgrd', p_w, vwb).reshape(Bsz, S, H, Dh)

    g = jax.nn.sigmoid(g_pre.astype(F32)).reshape(Bsz, S, H, 3)
    o = g[..., 0:1] * o_c + g[..., 1:2] * o_s + g[..., 2:3] * o_w
    return o.reshape(Bsz, S, NSA_WIDTH)

def _split_points():
    return [int(v) for v in np.cumsum(IN_SPLITS)[:-1]]

def setup_inputs(seed: int = 0) -> dict:
    key = jax.random.key(seed)
    ks = jax.random.split(key, 40)
    L, D, G, P, Hc = DEPTH, D_MODEL, SSM_GROUPS, SSM_STATE, SSM_GROUP

    def nrm(k, shape, scale):
        return scale * jax.random.normal(k, shape, F32)

    def gain(k, shape):
        return 1.0 + 0.05 * jax.random.normal(k, shape, F32)

    x = jax.random.normal(ks[0], (BATCH, SEQ, D), F32)
    offs = jax.random.randint(ks[1], (BATCH, 1), 0, SEQ, dtype=jnp.int32)
    positions = offs + jnp.arange(SEQ, dtype=jnp.int32)[None, :]
    return {
        'x': x,
        'positions': positions,
        'ln_mix_pre': gain(ks[2], (L, D)),
        'ln_mix_post': gain(ks[3], (L, D)),
        'ln_mlp_pre': gain(ks[4], (L, D)),
        'ln_mlp_post': gain(ks[5], (L, D)),
        'w_in': nrm(ks[6], (L, D, D_IN), D ** -0.5),
        'w_out': nrm(ks[7], (L, D_MIX, D), D_MIX ** -0.5),
        'ssm_lambda_re': -0.5 + 0.01 * jax.random.normal(ks[8], (L, G, P), F32),
        'ssm_lambda_im': math.pi * jnp.arange(P, dtype=F32) + 0.01 * jax.random.normal(ks[9], (L, G, P), F32),
        'ssm_b_re': nrm(ks[10], (L, G, P, Hc), (2 * Hc) ** -0.5),
        'ssm_b_im': nrm(ks[11], (L, G, P, Hc), (2 * Hc) ** -0.5),
        'ssm_c_re': nrm(ks[12], (L, G, Hc, P), P ** -0.5),
        'ssm_c_im': nrm(ks[13], (L, G, Hc, P), P ** -0.5),
        'ssm_d': nrm(ks[14], (L, SSM_WIDTH), 1.0),
        'ssm_log_dt': jax.random.uniform(ks[15], (L, G), F32, math.log(DT_MIN), math.log(DT_MAX)),
        'ssm_w_glu': nrm(ks[16], (L, SSM_WIDTH, SSM_WIDTH), SSM_WIDTH ** -0.5),
        'mlstm_conv': nrm(ks[17], (L, MLSTM_CONV, 2 * MLSTM_WIDTH), MLSTM_CONV ** -0.5),
        'mlstm_b_i': nrm(ks[18], (L, MLSTM_HEADS), 0.1),
        'mlstm_b_f': jax.random.uniform(ks[19], (L, MLSTM_HEADS), F32, 3.0, 6.0),
        'cmp_pe_k': nrm(ks[20], (L, CMP_BLOCK, NSA_HEAD_DIM), 0.1),
        'cmp_w1_k': nrm(ks[21], (L, CMP_BLOCK * NSA_HEAD_DIM, CMP_HIDDEN), (CMP_BLOCK * NSA_HEAD_DIM) ** -0.5),
        'cmp_w2_k': nrm(ks[22], (L, CMP_HIDDEN, NSA_HEAD_DIM), CMP_HIDDEN ** -0.5),
        'cmp_pe_v': nrm(ks[23], (L, CMP_BLOCK, NSA_HEAD_DIM), 0.1),
        'cmp_w1_v': nrm(ks[24], (L, CMP_BLOCK * NSA_HEAD_DIM, CMP_HIDDEN), (CMP_BLOCK * NSA_HEAD_DIM) ** -0.5),
        'cmp_w2_v': nrm(ks[25], (L, CMP_HIDDEN, NSA_HEAD_DIM), CMP_HIDDEN ** -0.5),
        'gn_ssm': gain(ks[26], (L, SSM_WIDTH)),
        'gn_mlstm': gain(ks[27], (L, MLSTM_WIDTH)),
        'gn_nsa': gain(ks[28], (L, NSA_WIDTH)),
        'mlp_w1': nrm(ks[29], (L, D, D_FF), D ** -0.5),
        'mlp_w2': nrm(ks[30], (L, D_FF, D), D_FF ** -0.5),
    }

def reference(x, positions, ln_mix_pre, ln_mix_post, ln_mlp_pre, ln_mlp_post, w_in, w_out,
              ssm_lambda_re, ssm_lambda_im, ssm_b_re, ssm_b_im, ssm_c_re, ssm_c_im, ssm_d,
              ssm_log_dt, ssm_w_glu, mlstm_conv, mlstm_b_i, mlstm_b_f,
              cmp_pe_k, cmp_w1_k, cmp_w2_k, cmp_pe_v, cmp_w1_v, cmp_w2_v,
              gn_ssm, gn_mlstm, gn_nsa, mlp_w1, mlp_w2):
    cos, sin = _rope_tables(positions)
    h = x
    for l in range(DEPTH):
        u = _rmsnorm(h, ln_mix_pre[l])
        z = u @ w_in[l]
        (s_u, m_q, m_k, m_v, m_o, m_i, m_f,
         a_q, c_k, c_v, s_k, s_v, w_k, w_v, a_g) = jnp.split(z, _split_points(), axis=-1)
        y_ssm = _s5_mixer(s_u, ssm_lambda_re[l], ssm_lambda_im[l], ssm_b_re[l], ssm_b_im[l],
                          ssm_c_re[l], ssm_c_im[l], ssm_d[l], ssm_log_dt[l], ssm_w_glu[l])
        y_mls = _mlstm_mixer(m_q, m_k, m_v, m_o, m_i, m_f, mlstm_conv[l], mlstm_b_i[l], mlstm_b_f[l])
        y_nsa = _nsa_mixer(a_q, c_k, c_v, s_k, s_v, w_k, w_v, a_g, cos, sin,
                           cmp_pe_k[l], cmp_w1_k[l], cmp_w2_k[l], cmp_pe_v[l], cmp_w1_v[l], cmp_w2_v[l])
        y = jnp.concatenate([_group_rmsnorm(y_ssm, gn_ssm[l], SSM_GROUPS),
                             _group_rmsnorm(y_mls, gn_mlstm[l], MLSTM_HEADS),
                             _group_rmsnorm(y_nsa, gn_nsa[l], NSA_HEADS)], axis=-1).astype(h.dtype)
        h = h + _rmsnorm(y @ w_out[l], ln_mix_post[l])
        u = _rmsnorm(h, ln_mlp_pre[l])
        f = jnp.square(jax.nn.relu(u @ mlp_w1[l])) @ mlp_w2[l]
        h = h + _rmsnorm(f, ln_mlp_post[l])
    return h


_drawn_inputs = setup_inputs


def setup_inputs(seed=0):
    import zlib

    import numpy as np

    out = dict(_drawn_inputs(seed))
    spreads = {}
    factors = {'ssm_lambda_re': 8.0, 'mlstm_b_i': 8.0, 'cmp_pe_k': 5.65, 'gn_ssm': 2.693}
    for name, (base, spread) in spreads.items():
        noise = np.random.default_rng([zlib.crc32(name.encode()), seed]).standard_normal(out[name].shape)
        drawn = base * np.exp(spread * noise) if base else spread * noise
        out[name] = __import__('jax').numpy.asarray(drawn.astype(out[name].dtype))
    for name, factor in factors.items():
        out[name] = (out[name] * factor).astype(out[name].dtype)
    return out
```

```python
from contextlib import ExitStack

import concourse.bass as bass
from concourse import mybir

F32 = mybir.dt.float32
F32R = mybir.dt.float32r
I32 = mybir.dt.int32
ALU = mybir.AluOpType
ACT = mybir.ActivationFunctionType
AX = mybir.AxisListType.X

P = 128
DEPTH, D, T = 2, 1024, 512
NT = T // P
KD = D // P
SSM, MLS, NSA = D // 4, D // 4, D // 2
NG, GH, NP_ = 16, 16, 64
NJ = NG * NP_ // P
L = P
MH, HD, KCONV = 4, 64, 4
NH, NGR = NSA // HD, 2
R = NH // NGR
CB, CS_, CHID = 32, 16, 256
NCMP = T // CS_ - CB // CS_ + 1
WIN = 256
FF = 4 * D
EPS = 1e-6
NEG = -1e30
THETA, ROT = 500000.0, HD // 8
D_IN = SSM + 4 * MLS + 2 * MH + NSA + 6 * NGR * HD + 3 * NH

ZF = SSM + 2 * MLS
ZT = D_IN - ZF
ZV, ZO, ZI, ZFG, ZQ = 0, MLS, 2 * MLS, 2 * MLS + MH, 2 * MLS + 2 * MH
ZKC = ZQ + NSA
GW = NGR * HD
ZVC, ZKS, ZVS, ZKW, ZVW = (ZKC + n * GW for n in range(1, 6))
ZG = ZKC + 6 * GW

R_PRE, R_MLP, R_GN, R_D, R_CONV = 0, 8, 16, 24, 26
R_PEK, R_PEV = R_CONV + 4 * KCONV, R_CONV + 4 * KCONV + CB // 2
R_LR = R_PEV + CB // 2
R_LI = R_LR + NJ
R_DT = 96
NROW = R_DT + NJ

TWO_PI = 6.283185307179586
C1 = 6.28125
C2 = round((TWO_PI - C1) * 2 ** 22) / 2 ** 22
C3 = TWO_PI - C1 - C2
ROUND = 1.5 * 2.0 ** 23
ROUND13 = 1.5 * 2.0 ** 10
PI_IN = 3.1415925

NRAW, NSPLIT = 6, 4


(S_DT, S_X, S_MAG, S_TH, S_R, S_ABS, S_SIN, S_COS, S_ARE, S_AIM, S_DEN, S_RDEN, S_E, S_GRE, S_GIM, S_RHI, S_RLO,
 S_IRE, S_IIM, S_T0, S_T1, S_T2, S_T3) = range(23)
N_PARAMS = 23


def spans(i):
    return (896, NCMP), (0, (i + 1) * P), (512, min(i + 1, WIN // P + 1) * P)


def reduce_angle(dve, link, out, angle, whole):
    link(dve.tensor_scalar(whole, angle, 1.0 / TWO_PI, ROUND, ALU.mult, ALU.add))
    link(dve.tensor_scalar(whole, whole, ROUND, None, ALU.subtract))
    for c in (C1, C2, C3):
        link(dve.scalar_tensor_tensor(out, whole, -c, angle, ALU.mult, ALU.add))
        angle = out
    link(dve.tensor_scalar(out, out, PI_IN, -PI_IN, ALU.min, ALU.max))


def absolute(dve, out, x):
    return dve.scalar_tensor_tensor(out, x, -1.0, x, ALU.mult, ALU.max)


def low(dve, g, fl, fh, sq_t, s):
    dve.wait_ge(s["f_hi"], g + 1)
    dve.tensor_tensor(fl[:, g % 16], sq_t[:, g % 2], fh[:, g % 16].bitcast(F32), ALU.subtract).then_inc(s["f_lo"], 1)


def weight_units(t, layer):
    units = []
    cols = [(0, 512), (512, ZF)] + [(ZF + a, min(ZF + a + 512, D_IN)) for a in range(0, ZT, 512)]
    for a, b in cols:
        for k in range(KD):
            units.append((t["w_in"][layer, k * P:(k + 1) * P, a:b], "split", b - a))
    for name in ("cmp_w1_k", "cmp_w1_v"):
        for j in range(CB // 4):
            src = t[name][layer, 2 * j * P:(2 * j + 2) * P, :].rearrange("(j p) c -> p j c", p=P)
            units.append((src, "whole", 2 * CHID))
    for half in range(2):
        for k in range(KD):
            units.append((t["w_out"][layer, k * P:(k + 1) * P, half * 512:half * 512 + 512], "split", 512))
    for part in range(2):
        for c in range(4):
            for k in range(KD):
                a = part * FF // 2 + c * 512
                units.append((t["mlp_w1"][layer, k * P:(k + 1) * P, a:a + 512], "split", 512))
        for half in range(2):
            for k in range(FF // 2 // P):
                a = part * FF // 2 + k * P
                units.append((t["mlp_w2"][layer, a:a + P, half * 512:half * 512 + 512], "split", 512))
    return units, [b - a for a, b in cols]


def build(nc, t, out):
    ctx = ExitStack()
    with ctx:
        at = [nc.sbuf_base]
        place = {}

        def over(name, shape, under, dt=F32):
            return nc.alloc_sbuf_tensor_at(name, shape, dt, offset=place[under])

        def sb(name, shape, dt=F32):
            place[name] = at[0]
            size = 4
            for n in shape[1:]:
                size *= n
            size = (size + 31) // 32 * 32
            tensor = nc.alloc_sbuf_tensor_at(name, shape, dt, offset=at[0])
            at[0] += size
            return tensor

        at[0] = (at[0] + 31) // 32 * 32
        h = sb("h", [P, NT, D])
        xh = sb("xh", [P, KD, T], F32R)
        xl = sb("xl", [P, KD, T], F32R)
        raw = sb("raw", [P, NRAW, 512])
        wh = sb("wh", [P, NSPLIT, 512], F32R)
        wl = sb("wl", [P, NSPLIT, 512], F32R)
        fbuf = sb("fbuf", [P, NT, D])
        gpost = sb("gpost", [P, 2, D])
        junk = over("junk", [P, D], "xl")
        ident = sb("ident", [P, P])
        mask = sb("mask", [P, 512])
        wmask = sb("wmask", [P, 384])
        cmask = sb("cmask", [P, NT, 32])
        cvalid = sb("cvalid", [P, 32])
        maskT = sb("maskT", [P, P])
        bones = sb("bones", [P, P])
        par = sb("par", [P, 4])
        sel = sb("sel", [MH, MH, P])
        sel2 = sb("sel2", [MH, 2, P])
        keep = sb("keep", [MH, T])
        steps = sb("steps", [P, L + 1])
        stepi = sb("stepi", [P, L + 1], I32)
        consts = sb("consts", [P, 2])
        posi = sb("posi", [P, NT], I32)
        posf = sb("posf", [P, NT])
        cosr = sb("cosr", [P, NT, ROT])
        sinr = sb("sinr", [P, NT, ROT])
        prow = sb("prow", [NROW, P])
        pcol = sb("pcol", [P, NROW])
        dt8 = sb("dt8", [NROW, 2])
        gateb = sb("gateb", [MH, 2])
        wglu = sb("wglu", [P, 2, SSM])
        w2c = sb("w2c", [P, 2, 2, HD])
        bnat = sb("bnat", [P, 2, NJ, GH])
        cnat = sb("cnat", [P, 2, 2, NP_])
        stat = sb("stat", [P, 3, NT])
        small = sb("small", [P, 24, NJ])
        shared = at[0]
        z = sb("z", [P, NT, ZT])
        su = sb("su", [P, 2, T])
        qkr = sb("qkr", [P, 4, KCONV - 1 + T])
        ytok = over("ytok", [P, NT, MLS + NSA], "fbuf")
        work = at[0]
        vr = sb("vr", [P, NJ, T])
        vi = over("vi", [P, NJ, T], "fbuf")
        ctab = sb("ctab", [P, NJ, L + 1])
        stab = sb("stab", [P, NJ, L + 1])
        bd = sb("bd", [P, 2, NJ, 32])
        bT = sb("bT", [P, 4, P])
        cb = sb("cb", [P, 2, 2, P])
        cT = sb("cT", [P, 2, 2, P])
        tmp = sb("tmp", [P, 4, T])
        s5_end = at[0]
        at[0] = work
        tang = sb("tang", [P, NJ, L + 1])
        tnum = sb("tnum", [P, NJ, L + 1])
        assert at[0] <= work + NJ * T * 4
        tred = over("tred", [P, NJ, L + 1], "fbuf")
        at[0] = work
        qk = sb("qk", [P, 4, T])
        wT = sb("wT", [P, MH, T])
        kw = sb("kw", [P, NT, MH, HD])
        va = sb("va", [P, NT, MH, HD + 1])
        nu = sb("nu", [P, NT, MH, HD + 1])
        so = sb("so", [P, NT, MLS])
        rows = over("rows", [MH, 8, T], "xl")
        msr = sb("msr", [MH, NT])
        colt = sb("colt", [P, 4, NT, MH])
        cst = sb("cst", [P, 2, HD + 1])
        dec = sb("dec", [P, 2, NT])
        mden = sb("mden", [P, 2, NT, MH])
        mtmp = sb("mtmp", [P, MH, HD + 1])
        mls_end = at[0]
        at[0] = work
        qa = over("qa", [P, NT, R, NGR, HD], "xh")
        qT = sb("qT", [P, R, T])
        ksT = sb("ksT", [P, T])
        kwT = sb("kwT", [P, T])
        flat = sb("flat", [P, 2, CB // 2, NGR, NCMP])
        hg = sb("hg", [P, 4, NGR * NCMP])
        kcT = sb("kcT", [P, NCMP])
        vcm = sb("vcm", [NCMP, NGR, HD])
        sm = sb("sm", [P, 2, 928])
        pt = sb("pt", [P, 2, 1024])
        gate = sb("gate", [P, NT, 3 * NH])
        am = sb("am", [P, 2, 16])
        rtmp = sb("rtmp", [P, 4, NT * NH * ROT])
        gsq = over("gsq", [P, NT, MLS + NSA], "qT")
        gst = sb("gst", [P, 3, NT, 12])
        nsa_end = at[0]
        at[0] = shared
        fh = sb("fh", [P, FF // 2 // P, T], F32R)
        fl = sb("fl", [P, FF // 2 // P, T], F32R)
        act_t = sb("act_t", [P, 2, T])
        sq_t = sb("sq_t", [P, 2, T])
        mlp_end = at[0]
        ps = [ctx.enter_context(nc.psum_tensor(f"ps{n}", [P, 512], F32)) for n in range(8)]


        def sems(text):
            made = {name: ctx.enter_context(nc.semaphore(name)) for name in text.split()}
            numbers = [x.num for x in made.values()]
            assert numbers == list(range(numbers[0], numbers[0] + len(numbers)))
            return made, range(numbers[0], numbers[0] + len(numbers))

        once, _ = sems("x_landed pool_made rope_ready rope_trig setup_steps stored")
        s, layer_sems = sems("""
            params_landed raw_landed0 raw_landed1 raw_landed2 raw_landed3 raw_landed4 raw_landed5
            w_hi w_lo w_used whole_used evacuated evac_added
            act_steps dve_steps cols_turned cols_ready ssq msq rms normed turned x_hi x_lo h_new
            f_relu f_sq f_hi f_lo
            s5_dt s5_ang s5_trig s5_phase s5_table s5_nat s5_natT s5_mats s5_bu s5_rot s5_x s5_y
            s5_ypre s5_gelu s5_glu s5_sig s5_sq s5_ms s5_rt
            m_pad m_conv m_qk m_gateT m_fx m_ln m_rows m_exp m_colT m_bc m_cols m_arg m_w m_s m_p m_kT m_kw
            m_va m_chunk m_state m_nu m_so m_out
            n_rope n_qa n_qT n_q n_kT n_k n_flat n_hid n_kcT n_kc n_gate
            n_score n_max n_exp n_p n_pT n_pa n_pd n_av n_o
            g_sq g_ms g_rt g_y""")
        raw_landed = [s[f"raw_landed{n}"] for n in range(NRAW)]

        def chain(engine, semaphore):
            count = [0]

            def link(instruction):
                count[0] += 1
                instruction.then_inc(semaphore, 1)
                engine.wait_ge(semaphore, count[0])
            return link

        with nc.Block() as block:
            @block.sync
            def _(sp):
                sp.dma_start(h[:], t["x"][0].rearrange("(i p) d -> p i d", p=P)).then_inc(once["x_landed"], 16)
                sp.dma_start(posi[:], t["positions"][0].rearrange("(i p) -> p i", p=P),
                             allow_slow_non_contiguous=True).then_inc(once["x_landed"], 16)
                sp.wait_ge(once["x_landed"], 32)

            @block.gpsimd
            def _(pool):
                link = chain(pool, once["pool_made"])

                def keep_where(tile, pattern, base, mult, fill, op=ALU.is_ge):
                    link(pool.affine_select(out=tile, in_=tile, pattern=pattern, base=base,
                                            channel_multiplier=mult, compare_op=op, fill=fill))

                for tile, value in ((ident, 0.0), (mask, 0.0), (wmask, 0.0), (cmask, 0.0), (cvalid, 1.0),
                                    (maskT, 0.0), (bones, 1.0 / GH), (sel, 0.0), (sel2, 0.0), (keep, 1.0),
                                    (prow, 0.0)):
                    link(pool.memset(tile[:], value))
                link(pool.memset(consts[:, 0:1], TWO_PI / 4))
                link(pool.memset(consts[:, 1:2], EPS))
                for n in range(ROT):
                    link(pool.memset(small[:, 0, n:n + 1], THETA ** (-2.0 * n / (2 * ROT))))
                keep_where(ident[:], [[-1, P]], 0, 1, 1.0, ALU.not_equal)
                keep_where(mask[:, 384:512], [[-1, P]], 0, 1, NEG)
                keep_where(wmask[:, 256:384], [[-1, P]], 0, 1, NEG)
                keep_where(wmask[:, 0:128], [[1, P]], -1, -1, NEG)
                keep_where(cmask[:], [[P, NT], [-CS_, 32]], 1 - CB, 1, NEG)
                keep_where(cvalid[:], [[-CS_, 32]], 1 - CB, 1, 0.0)
                keep_where(maskT[:], [[1, P]], 0, -1, NEG)
                keep_where(bones[:].rearrange("p (b c) -> p b c", c=GH), [[-GH, P // GH], [0, GH]], 0, 1, 0.0)
                keep_where(bones[:].rearrange("p (b c) -> p b c", c=GH), [[GH, P // GH], [0, GH]], GH - 1, -1, 0.0)
                keep_where(sel[:], [[-1, MH], [0, P]], 0, 1, 1.0, ALU.not_equal)
                keep_where(sel2[:].rearrange("k a (b c) -> k a b c", b=2), [[-2, 2], [-1, 2], [0, HD]], 0, 1, 1.0,
                           ALU.not_equal)
                keep_where(keep[:].rearrange("k (a b) -> k a b", b=L), [[0, NT], [1, L]], 0, 0, 0.0, ALU.not_equal)
                link(pool.iota(stepi[:], [[1, L + 1]], base=0, channel_multiplier=0))

            N_POOL = 11 + 2 + ROT + 12 + 1

            @block.vector
            def _(dve):
                link = chain(dve, once["setup_steps"])
                dve.wait_ge(once["pool_made"], N_POOL)
                link(dve.tensor_copy(steps[:], stepi[:]))
                for parity in range(2):
                    link(dve.tensor_reduce(par[:, parity:parity + 1], bones[:, GH * parity:P:2 * GH], AX, ALU.add))
                link(dve.tensor_scalar(par[:, 0:2], par[:, 0:2], float(GH), None, ALU.mult))
                link(dve.tensor_scalar(par[:, 2:4], par[:, 0:2], -1.0, None, ALU.mult))
                dve.wait_ge(once["x_landed"], 32)
                link(dve.tensor_copy(posf[:], posi[:]))
                link(dve.tensor_tensor(sinr[:], posf[:].unsqueeze(2).to_broadcast([P, NT, ROT]),
                                       small[:, 0:1, :].to_broadcast([P, NT, ROT]), ALU.mult))
                reduce_angle(dve, link, sinr[:], sinr[:], cosr[:])
                absolute(dve, cosr[:], sinr[:]).then_inc(once["rope_ready"], 1)

            @block.scalar
            def _(act):
                act.wait_ge(once["rope_ready"], 1)
                act.activation(cosr[:], cosr[:], ACT.Sin, bias=consts[:, 0:1], scale=-1.0).then_inc(once["rope_trig"], 1)
                act.activation(sinr[:], sinr[:], ACT.Sin).then_inc(once["rope_trig"], 1)
                act.wait_ge(once["rope_trig"], 2)

        with nc.Fori(0, DEPTH) as layer:
            with nc.Block() as block:
                units, widths = weight_units(t, layer)
                splits = [n for n, unit in enumerate(units) if unit[1] == "split"]
                wholes = [n for n, unit in enumerate(units) if unit[1] == "whole"]
                order = {n: k for kind in (splits, wholes) for k, n in enumerate(kind)}
                N_SPLIT = len(splits)

                def unit_tile(n, ring=None):
                    return raw[:, n % NRAW, 0:units[n][2]]

                def landed(engine, n):
                    engine.wait_ge(raw_landed[n % NRAW], 16 * (n // NRAW + 1))

                blocks = []
                first = 0
                for n, width in enumerate(widths):
                    blocks.append((first, KD, n < 2, width))
                    first += KD
                for part in (("out",), ("up", "down"), ("up", "down")):
                    for what in part:
                        for _ in range(4 if what == "up" else 2):
                            deep = FF // 2 // P if what == "down" else KD
                            blocks.append((first, deep, what == "up", 512))
                            first += deep
                assert first == N_SPLIT
                B_IN, B_OUT = 0, 6
                B_UP, B_DOWN = (8, 14), (12, 18)
                N_IN = 6 * KD

                @block.sync
                def _(sp):
                    def load(tile, src, slow=False):
                        params.append(sp.dma_start(tile, src, allow_slow_non_contiguous=slow).then_inc(s["params_landed"], 16))

                    params = []
                    for row, src in (
                        (R_PRE, t["ln_mix_pre"][layer].rearrange("(k p) -> k p", p=P)),
                        (R_MLP, t["ln_mlp_pre"][layer].rearrange("(k p) -> k p", p=P)),
                        (R_GN, t["gn_ssm"][layer].rearrange("(k p) -> k p", p=P)),
                        (R_GN + 2, t["gn_mlstm"][layer].rearrange("(k p) -> k p", p=P)),
                        (R_GN + 4, t["gn_nsa"][layer].rearrange("(k p) -> k p", p=P)),
                        (R_D, t["ssm_d"][layer].rearrange("(k p) -> k p", p=P)),
                        (R_CONV, t["mlstm_conv"][layer].rearrange("k (c p) -> (k c) p", p=P)),
                        (R_PEK, t["cmp_pe_k"][layer].rearrange("(j q) d -> j (q d)", q=2)),
                        (R_PEV, t["cmp_pe_v"][layer].rearrange("(j q) d -> j (q d)", q=2)),
                        (R_LR, t["ssm_lambda_re"][layer].rearrange("(j g) p -> j (g p)", g=2)),
                        (R_LI, t["ssm_lambda_im"][layer].rearrange("(j g) p -> j (g p)", g=2)),
                    ):
                        load(prow[row:row + src.shape[0], :], src)
                    load(dt8[R_DT:R_DT + NJ, :], t["ssm_log_dt"][layer].rearrange("(j g) -> j g", g=2), True)
                    load(bnat[:, 0], t["ssm_b_re"][layer].rearrange("(j g) p h -> (g p) j h", g=2))
                    load(bnat[:, 1], t["ssm_b_im"][layer].rearrange("(j g) p h -> (g p) j h", g=2))
                    load(cnat[:, 0], t["ssm_c_re"][layer].rearrange("(c g) h p -> (g h) c p", c=2))
                    load(cnat[:, 1], t["ssm_c_im"][layer].rearrange("(c g) h p -> (g h) c p", c=2))
                    load(gateb[:, 0:1], t["mlstm_b_i"][layer].unsqueeze(1), True)
                    load(gateb[:, 1:2], t["mlstm_b_f"][layer].unsqueeze(1), True)
                    load(wglu[:], t["ssm_w_glu"][layer].rearrange("(c p) n -> p c n", p=P))
                    load(w2c[:, 0], t["cmp_w2_k"][layer].rearrange("(c p) n -> p c n", p=P))
                    load(w2c[:, 1], t["cmp_w2_v"][layer].rearrange("(c p) n -> p c n", p=P))
                    load(gpost[:, 0], t["ln_mix_post"][layer].partition_broadcast(P))
                    load(gpost[:, 1], t["ln_mlp_post"][layer].partition_broadcast(P))
                    assert len(params) == N_PARAMS
                    for n, (src, kind, width) in enumerate(units):
                        if n >= NRAW:
                            before = n - NRAW
                            sp.wait_ge(s["w_lo" if units[before][1] == "split" else "whole_used"], order[before] + 1)
                        tile = unit_tile(n)
                        if kind == "whole":
                            tile = tile.rearrange("p (j c) -> p j c", j=2)
                        sp.dma_start(tile, src).then_inc(raw_landed[n % NRAW], 16)

                @block.gpsimd
                def _(pool):
                    def split_low(k):
                        pool.wait_ge(s["w_hi"], k + 1)
                        n = splits[k]
                        width = units[n][2]
                        pool.tensor_tensor(wl[:, k % NSPLIT, 0:width], unit_tile(n), wh[:, k % NSPLIT, 0:width].bitcast(F32),
                                           ALU.subtract).then_inc(s["w_lo"], 1)

                    pool.memset(qkr[:, :, 0:KCONV - 1], 0.0).then_inc(s["m_pad"], 1)
                    for k in range(N_IN):
                        split_low(k)
                    pool.wait_ge(s["s5_ypre"], 2)
                    pool.wait_ge(s["evacuated"], 6)
                    pool.memset(va[:], 1.0).then_inc(s["m_va"], 1)
                    pool.wait_ge(s["m_va"], 1)
                    for i in range(NT):
                        pool.tensor_copy(va[:, i, :, 0:HD], z[:, i, ZV:ZV + MLS].rearrange("p (h d) -> p h d", h=MH)).then_inc(
                            s["m_va"], 1)
                    for k in range(N_IN, N_SPLIT):
                        split_low(k)

                @block.scalar
                def _(act):
                    link = chain(act, s["act_steps"])

                    def split_high(k):
                        n = splits[k]
                        width = units[n][2]
                        landed(act, n)
                        if k >= NSPLIT:
                            act.wait_ge(s["w_used"], k - NSPLIT + 1)
                        act.activation(wh[:, k % NSPLIT, 0:width], unit_tile(n), ACT.Copy).then_inc(s["w_hi"], 1)

                    def splits_for(block_numbers, evacuate, hooks=()):
                        start = blocks[block_numbers[0]][0]
                        end = blocks[block_numbers[-1]][0] + blocks[block_numbers[-1]][1]
                        after = {blocks[b][0] + blocks[b][1] + NSPLIT - 1: b for b in block_numbers}
                        hooks = dict(hooks)
                        for k in range(start, end):
                            split_high(k)
                            if k in after:
                                evacuate(after.pop(k))
                            if k - start in hooks:
                                hooks[k - start]()
                        for k in sorted(after):
                            evacuate(after[k])

                    def product_done(engine, b):
                        engine.wait_ge(s["w_used"], blocks[b][0] + blocks[b][1])

                    def mean_squares(n, src):
                        for i in range(NT):
                            if n or i:
                                act.wait_ge(s["ssq"], NT * n + i)
                            act.activation(junk[:], src[:, i], ACT.Square, accum_out=stat[:, 0, i:i + 1]).then_inc(s["ssq"], 1)
                        act.wait_ge(s["msq"], n + 1)
                        act.activation(stat[:, 2, :], stat[:, 1, :], ACT.Sqrt).then_inc(s["rms"], 1)

                    def turned_high(first, gains, count0):
                        for k in range(KD):
                            act.wait_ge(s["turned"], first + k + 1)
                            act.activation(xh[:, k], ps[k][:], ACT.Identity, scale=pcol[:, gains + k:gains + k + 1]).then_inc(
                                s["x_hi"], 1)

                    def take_in(b):
                        product_done(act, b)
                        group = 4 * (b % 2)
                        last = None
                        if b == 0:
                            for n in range(2):
                                act.activation(su[:, n], ps[group + n][:], ACT.Copy)
                            for n in range(2):
                                last = act.activation(qkr[:, n, KCONV - 1:], ps[group + 2 + n][:], ACT.Copy)
                        elif b == 1:
                            for n in range(2):
                                last = act.activation(qkr[:, 2 + n, KCONV - 1:], ps[group + n][:], ACT.Copy)
                        else:
                            a = (b - 2) * 512
                            for i in range(NT):
                                last = act.activation(z[:, i, a:a + widths[b]], ps[group + i][:, 0:widths[b]], ACT.Copy)
                        last.then_inc(s["evacuated"], 1)

                    def take_half(b):
                        product_done(act, b)
                        for i in range(NT):
                            last = act.activation(fbuf[:, i, 512 * (b % 2):512 * (b % 2) + 512], ps[4 * (b % 2) + i][:], ACT.Copy)
                        last.then_inc(s["evacuated"], 1)

                    def s5_dt():
                        act.wait_ge(s["cols_ready"], 1)
                        act.activation(small[:, S_DT], pcol[:, R_DT:R_DT + NJ], ACT.Exp).then_inc(s["s5_dt"], 1)
                        act.wait_ge(s["s5_ang"], 1)
                        act.activation(small[:, S_MAG], small[:, S_X], ACT.Exp)
                        act.activation(small[:, S_SIN], small[:, S_R], ACT.Sin)
                        act.activation(small[:, S_COS], small[:, S_ABS], ACT.Sin, bias=consts[:, 0:1], scale=-1.0).then_inc(
                            s["s5_trig"], 1)

                    def s5_tables():
                        act.wait_ge(s["s5_phase"], 2)
                        act.activation(stab[:], tred[:], ACT.Sin).then_inc(s["s5_table"], 1)
                        act.activation(ctab[:], tang[:], ACT.Sin, bias=consts[:, 0:1], scale=-1.0).then_inc(s["s5_table"], 1)

                    mean_squares(0, h)
                    act.wait_ge(s["cols_ready"], 1)
                    turned_high(0, R_PRE, 0)
                    splits_for(range(B_IN, B_OUT), take_in, {14: s5_dt, 22: s5_tables})

                    for n in range(2):
                        act.wait_ge(s["s5_ypre"], n + 1)
                        act.activation(tmp[:, 2 + n], tmp[:, n], ACT.Gelu_apprx_tanh).then_inc(s["s5_gelu"], 1)
                    for n in range(2):
                        act.wait_ge(s["s5_glu"], n + 1)
                        act.activation(tmp[:, n], ps[6 + n][:], ACT.Sigmoid).then_inc(s["s5_sig"], 1)
                    for n in range(2):
                        act.wait_ge(s["s5_ms"], n + 1)
                        act.activation(tmp[:, n], ps[4 + n][:], ACT.Sqrt, bias=consts[:, 1:2]).then_inc(s["s5_rt"], 1)

                    for n in range(4):
                        act.wait_ge(s["m_conv"], n + 1)
                        act.activation(qk[:, n], qk[:, n], ACT.Silu).then_inc(s["m_qk"], 1)
                    act.activation(so[:], z[:, :, ZO:ZO + MLS], ACT.Sigmoid).then_inc(s["m_so"], 1)
                    act.wait_ge(s["m_fx"], 1)
                    link(act.activation(rows[:, 6], rows[:, 6], ACT.Exp, scale=-1.0))
                    act.activation(rows[:, 6], rows[:, 6], ACT.Ln, bias=1.0).then_inc(s["m_ln"], 1)
                    act.wait_ge(s["m_rows"], 1)
                    act.activation(rows[:, 5:8], rows[:, 5:8], ACT.Exp).then_inc(s["m_exp"], 1)
                    for head in range(MH):
                        act.wait_ge(s["m_arg"], head + 1)
                        act.activation(wT[:, head], wT[:, head], ACT.Exp).then_inc(s["m_w"], 1)

                    act.wait_ge(s["n_rope"], 1)
                    act.activation(gate[:], z[:, :, ZG:ZG + 3 * NH], ACT.Sigmoid).then_inc(s["n_gate"], 1)
                    for i in range(NT):
                        act.activation(qa[:, i].rearrange("p r g d -> p g r d"),
                                       z[:, i, ZQ:ZQ + NSA].rearrange("p (g r d) -> p g r d", g=NGR, r=R),
                                       ACT.Copy).then_inc(s["n_qa"], 1)
                    for r in range(R):
                        act.wait_ge(s["n_qT"], r + 1)
                        act.activation(qT[:, r], ps[r][:], ACT.Copy).then_inc(s["n_q"], 1)
                    for n in range(4):
                        act.wait_ge(s["whole_used"], len(wholes) // 2 * (n // 2 + 1))
                        act.activation(hg[:, n], ps[n][:, 0:NGR * NCMP], ACT.Gelu_apprx_tanh).then_inc(s["n_hid"], 1)

                    def exps(u):
                        i, slot = u // NH, u % 2
                        act.wait_ge(s["n_max"], u + 1)
                        for kind, (a, width) in enumerate(spans(i)):
                            last = act.activation(sm[:, slot, a:a + width], sm[:, slot, a:a + width], ACT.Exp,
                                                  bias=am[:, slot, 3 + kind:4 + kind], scale=HD ** -0.5,
                                                  accum_out=am[:, slot, 6 + kind:7 + kind])
                        last.then_inc(s["n_exp"], 1)

                    def take_turned(u):
                        i, slot = u // NH, u % 2
                        act.wait_ge(s["n_pT"], u + 1)
                        if u >= 2:
                            act.wait_ge(s["n_av"], u - 1)
                        act.activation(pt[:, slot, 0:(i + 1) * P], ps[4][:, 0:(i + 1) * P], ACT.Copy).then_inc(s["n_pa"], 1)

                    def take_tile(i):
                        act.wait_ge(s["n_av"], NH * (i + 1))
                        act.activation(ytok[:, i, MLS:], ps[6 + i % 2][:], ACT.Copy).then_inc(s["n_o"], 1)

                    for u in range(NT * NH + 2):
                        if u < NT * NH:
                            exps(u)
                        if 1 <= u <= NT * NH:
                            take_turned(u - 1)
                        if u >= 2 and (u - 1) % NH == 0:
                            take_tile((u - 1) // NH - 1)
                    act.wait_ge(s["n_o"], NT)
                    for i in range(NT):
                        act.activation(gsq[:, i], ytok[:, i], ACT.Square).then_inc(s["g_sq"], 1)
                    act.wait_ge(s["g_ms"], 1)
                    act.activation(gst[:, 1], gst[:, 0], ACT.Sqrt).then_inc(s["g_rt"], 1)
                    for k in range(2):
                        act.activation(xh[:, k], su[:, k], ACT.Copy).then_inc(s["x_hi"], 1)
                    for k in range(2, KD):
                        act.wait_ge(s["turned"], KD + k - 1)
                        act.activation(xh[:, k], ps[k][:], ACT.Identity, scale=pcol[:, R_GN + k:R_GN + k + 1]).then_inc(
                            s["x_hi"], 1)

                    splits_for(range(B_OUT, B_OUT + 2), take_half)
                    act.wait_ge(s["evacuated"], 8)
                    mean_squares(1, fbuf)
                    act.wait_ge(s["h_new"], NT)
                    mean_squares(2, h)
                    turned_high(2 * KD - 2, R_MLP, 0)

                    def take_up(part):
                        def take(b):
                            product_done(act, b)
                            for n in range(4):
                                f = 4 * (b - B_UP[part]) + n
                                g = 16 * part + f
                                if g >= 2:
                                    act.wait_ge(s["f_sq"], g - 1)
                                act.activation(act_t[:, g % 2], ps[4 * (b % 2) + n][:], ACT.Relu).then_inc(s["f_relu"], 1)
                                if g >= 1 and f >= 1:
                                    high(g - 1)
                            if b == B_UP[part] + 3:
                                high(16 * part + 15)
                        return take

                    def high(g):
                        act.wait_ge(s["f_sq"], g + 1)
                        if g == 16:
                            product_done(act, B_DOWN[0] + 1)
                        act.activation(fh[:, g % 16], sq_t[:, g % 2], ACT.Copy).then_inc(s["f_hi"], 1)

                    def nothing(b):
                        pass

                    for part in range(2):
                        splits_for(range(B_UP[part], B_UP[part] + 4), take_up(part))
                        splits_for(range(B_DOWN[part], B_DOWN[part] + 2), take_half if part == 0 else nothing)
                    act.wait_ge(s["evac_added"], 2)
                    mean_squares(3, fbuf)

                @block.vector
                def _(dve):
                    link = chain(dve, s["dve_steps"])

                    def tt(out_, a, b, op):
                        return dve.tensor_tensor(out_, a, b, op)

                    def root_mean(n):
                        dve.wait_ge(s["ssq"], NT * (n + 1))
                        dve.tensor_scalar(stat[:, 1, :], stat[:, 0, :], 1.0 / D, EPS, ALU.mult, ALU.add).then_inc(s["msq"], 1)
                        dve.wait_ge(s["rms"], n + 1)
                        link(dve.reciprocal(stat[:, 1, :], stat[:, 2, :]))

                    def pre_norm(n):
                        root_mean(n)
                        for i in range(NT):
                            dve.tensor_scalar(fbuf[:, i], h[:, i], stat[:, 1, i:i + 1], None, ALU.mult).then_inc(s["normed"], 1)

                    def turned_low(first, gains):
                        for k in range(KD):
                            dve.wait_ge(s["x_hi"], first + k + 1)
                            dve.scalar_tensor_tensor(xl[:, k], ps[k][:], pcol[:, gains + k:gains + k + 1], xh[:, k].bitcast(F32),
                                                     ALU.mult, ALU.subtract).then_inc(s["x_lo"], 1)

                    def post_norm(n, which):
                        root_mean(n)
                        for i in range(NT):
                            link(dve.scalar_tensor_tensor(fbuf[:, i], fbuf[:, i], stat[:, 1, i:i + 1], gpost[:, which],
                                                          ALU.mult, ALU.mult))
                            tt(h[:, i], h[:, i], fbuf[:, i], ALU.add).then_inc(s["h_new"], 1)

                    def sm_(n):
                        return small[:, n]

                    dve.wait_ge(s["params_landed"], 16 * N_PARAMS)
                    dve.tensor_copy(prow[R_DT:R_DT + NJ, :].rearrange("j (g p) -> j g p", g=2),
                                    dt8[R_DT:R_DT + NJ, :].unsqueeze(2).to_broadcast([NJ, 2, NP_])).then_inc(s["cols_turned"], 1)
                    pre_norm(0)
                    dve.wait_ge(s["cols_turned"], 2)
                    dve.tensor_copy(pcol[:], ps[7][:, 0:NROW]).then_inc(s["cols_ready"], 1)
                    dve.wait_ge(s["cols_ready"], 1)
                    turned_low(0, R_PRE)

                    lr, li = pcol[:, R_LR:R_LR + NJ], pcol[:, R_LI:R_LI + NJ]
                    dve.wait_ge(s["s5_dt"], 1)
                    link(tt(sm_(S_X), lr, sm_(S_DT), ALU.mult))
                    link(tt(sm_(S_TH), li, sm_(S_DT), ALU.mult))
                    reduce_angle(dve, link, sm_(S_R), sm_(S_TH), sm_(S_T0))
                    absolute(dve, sm_(S_ABS), sm_(S_R)).then_inc(s["s5_ang"], 1)
                    link(dve.tensor_scalar(sm_(S_RHI), sm_(S_R), ROUND13, None, ALU.add))
                    link(dve.tensor_scalar(sm_(S_RHI), sm_(S_RHI), ROUND13, None, ALU.subtract))
                    link(tt(sm_(S_RLO), sm_(S_R), sm_(S_RHI), ALU.subtract))
                    table = [P, NJ, L + 1]
                    stepb = steps[:].unsqueeze(1).to_broadcast(table)
                    link(tt(tang[:], sm_(S_RHI).unsqueeze(2).to_broadcast(table), stepb, ALU.mult))
                    reduce_angle(dve, link, tred[:], tang[:], tnum[:])
                    link(tt(tang[:], sm_(S_RLO).unsqueeze(2).to_broadcast(table), stepb, ALU.mult))
                    link(tt(tred[:], tred[:], tang[:], ALU.add))
                    dve.tensor_scalar(tred[:], tred[:], PI_IN, -PI_IN, ALU.min, ALU.max).then_inc(s["s5_phase"], 1)
                    dve.wait_ge(s["s5_phase"], 1)
                    absolute(dve, tang[:], tred[:]).then_inc(s["s5_phase"], 1)
                    dve.wait_ge(s["s5_trig"], 1)
                    link(tt(sm_(S_ARE), sm_(S_MAG), sm_(S_COS), ALU.mult))
                    link(tt(sm_(S_AIM), sm_(S_MAG), sm_(S_SIN), ALU.mult))
                    link(tt(sm_(S_T0), lr, lr, ALU.mult))
                    link(tt(sm_(S_T1), li, li, ALU.mult))
                    link(tt(sm_(S_DEN), sm_(S_T0), sm_(S_T1), ALU.add))
                    link(dve.reciprocal(sm_(S_RDEN), sm_(S_DEN)))
                    link(dve.tensor_scalar(sm_(S_E), sm_(S_ARE), 1.0, None, ALU.subtract))
                    for out_, (a, b), op in ((S_GRE, (lr, li), ALU.add), (S_GIM, (li, lr), ALU.subtract)):
                        link(tt(sm_(S_T0), sm_(S_E), a, ALU.mult))
                        link(tt(sm_(S_T1), sm_(S_AIM), b, ALU.mult))
                        link(tt(sm_(S_T0), sm_(S_T0), sm_(S_T1), op))
                        link(tt(sm_(out_), sm_(S_T0), sm_(S_RDEN), ALU.mult))
                    link(dve.memset(bd[:], 0.0))
                    wide = [P, NJ, GH]
                    gre, gim = (sm_(n).unsqueeze(2).to_broadcast(wide) for n in (S_GRE, S_GIM))
                    t0 = tmp[:, 0, 0:NJ * GH].rearrange("p (j c) -> p j c", j=NJ)
                    t1 = tmp[:, 1, 0:NJ * GH].rearrange("p (j c) -> p j c", j=NJ)
                    for part, (a, b), op in ((0, (0, 1), ALU.add), (1, (1, 0), ALU.subtract)):
                        link(tt(t0, gre, bnat[:, a], ALU.mult))
                        link(tt(t1, gim, bnat[:, b], ALU.mult))
                        for g in range(2):
                            rows_ = slice(g * NP_, (g + 1) * NP_)
                            link(tt(bd[rows_, part, :, g * GH:(g + 1) * GH], t0[rows_], t1[rows_], op))
                    for part in range(2):
                        for c in range(2):
                            for g in range(2):
                                mine = par[:, 2 * part + g:2 * part + g + 1]
                                last = dve.tensor_scalar(cb[:, part, c, g * NP_:(g + 1) * NP_], cnat[:, part, c], mine, None,
                                                         ALU.mult)
                                if (part, c, g) != (1, 1, 1):
                                    link(last)
                    last.then_inc(s["s5_nat"], 1)
                    dve.wait_ge(s["s5_natT"], 2)
                    link(dve.tensor_copy(bT[:], ps[0][:].rearrange("p (n c) -> p n c", n=4)))
                    dve.tensor_copy(cT[:], ps[1][:].rearrange("p (a b c) -> p a b c", a=2, b=2)).then_inc(s["s5_mats"], 1)

                    dve.wait_ge(s["s5_table"], 2)
                    chunked = [P, NT, L]

                    def by_chunk(ap):
                        return ap.rearrange("p (c l) -> p c l", c=NT)

                    def cos_sin(j):
                        return (ctab[:, j, 0:L].unsqueeze(1).to_broadcast(chunked),
                                stab[:, j, 0:L].unsqueeze(1).to_broadcast(chunked))

                    for j in range(NJ):
                        cos_, sin_ = cos_sin(j)
                        dve.wait_ge(s["s5_bu"], j + 1)
                        re_, im_ = by_chunk(ps[2 * (j % 2)][:]), by_chunk(ps[2 * (j % 2) + 1][:])
                        tt(by_chunk(tmp[:, 0]), re_, cos_, ALU.mult)
                        tt(by_chunk(tmp[:, 1]), im_, sin_, ALU.mult)
                        tt(by_chunk(tmp[:, 2]), im_, cos_, ALU.mult)
                        tt(by_chunk(tmp[:, 3]), re_, sin_, ALU.mult).then_inc(s["s5_rot"], 1)
                        dve.wait_ge(s["s5_rot"], j + 1)
                        tt(vr[:, j], tmp[:, 0], tmp[:, 1], ALU.add)
                        link(tt(vi[:, j], tmp[:, 2], tmp[:, 3], ALU.subtract))
                    last_cos, last_sin = ctab[:, :, L], stab[:, :, L]
                    for c in range(NT):
                        for j in range(NJ):
                            decay = sm_(S_MAG)[:, j:j + 1].to_broadcast([P, L])
                            for v, start in ((vr, S_IRE), (vi, S_IIM)):
                                part = v[:, j, c * L:(c + 1) * L]
                                last = dve.tensor_tensor_scan(part, decay, part,
                                                              sm_(start)[:, j:j + 1] if c else 0.0, ALU.mult, ALU.add)
                        link(last)
                        if c < NT - 1:
                            er, ei = vr[:, :, (c + 1) * L - 1], vi[:, :, (c + 1) * L - 1]
                            tt(sm_(S_T0), last_cos, er, ALU.mult)
                            tt(sm_(S_T1), last_sin, ei, ALU.mult)
                            tt(sm_(S_T2), last_cos, ei, ALU.mult)
                            link(tt(sm_(S_T3), last_sin, er, ALU.mult))
                            tt(sm_(S_IRE), sm_(S_T0), sm_(S_T1), ALU.subtract)
                            link(tt(sm_(S_IIM), sm_(S_T2), sm_(S_T3), ALU.add))
                    for j in range(NJ):
                        cos_, sin_ = cos_sin(j)
                        re_, im_ = by_chunk(vr[:, j]), by_chunk(vi[:, j])
                        tt(by_chunk(tmp[:, 0]), re_, cos_, ALU.mult)
                        tt(by_chunk(tmp[:, 1]), im_, sin_, ALU.mult)
                        tt(by_chunk(tmp[:, 2]), im_, cos_, ALU.mult)
                        link(tt(by_chunk(tmp[:, 3]), re_, sin_, ALU.mult))
                        link(tt(vr[:, j], tmp[:, 0], tmp[:, 1], ALU.subtract))
                        tt(vi[:, j], tmp[:, 2], tmp[:, 3], ALU.add).then_inc(s["s5_x"], 1)
                        dve.wait_ge(s["s5_x"], j + 1)
                    dve.wait_ge(s["s5_x"], NJ)
                    for n in range(2):
                        dve.wait_ge(s["s5_y"], n + 1)
                        dve.scalar_tensor_tensor(tmp[:, n], su[:, n], pcol[:, R_D + n:R_D + n + 1], ps[4 + n][:], ALU.mult,
                                                 ALU.add).then_inc(s["s5_ypre"], 1)
                    for n in range(2):
                        dve.wait_ge(s["s5_sig"], n + 1)
                        link(tt(su[:, n], tmp[:, 2 + n], tmp[:, n], ALU.mult))
                        tt(tmp[:, n], su[:, n], su[:, n], ALU.mult).then_inc(s["s5_sq"], 1)
                    for n in range(2):
                        dve.wait_ge(s["s5_rt"], n + 1)
                        link(dve.reciprocal(tmp[:, 2 + n], tmp[:, n]))
                        link(dve.scalar_tensor_tensor(su[:, n], su[:, n], pcol[:, R_GN + n:R_GN + n + 1], tmp[:, 2 + n],
                                                      ALU.mult, ALU.mult))

                    dve.wait_ge(s["m_pad"], 1)
                    for n in range(4):
                        tap = lambda k: pcol[:, R_CONV + 4 * k + n:R_CONV + 4 * k + n + 1]
                        link(dve.tensor_scalar(qk[:, n], qkr[:, n, 0:T], tap(0), None, ALU.mult))
                        for k in range(1, KCONV):
                            last = dve.scalar_tensor_tensor(qk[:, n], qkr[:, n, k:k + T], tap(k), qk[:, n], ALU.mult, ALU.add)
                            if k < KCONV - 1:
                                link(last)
                        last.then_inc(s["m_conv"], 1)
                    dve.wait_ge(s["m_gateT"], 1)
                    link(dve.tensor_scalar(rows[:, 0], ps[0][0:MH, :], gateb[:, 0:1], None, ALU.add))
                    link(dve.tensor_scalar(rows[:, 5], ps[1][0:MH, :], gateb[:, 1:2], None, ALU.add))
                    absolute(dve, rows[:, 6], rows[:, 5]).then_inc(s["m_fx"], 1)
                    dve.wait_ge(s["m_ln"], 1)
                    link(dve.scalar_tensor_tensor(rows[:, 1], rows[:, 5], 0.0, rows[:, 6], ALU.min, ALU.subtract))
                    dve.tensor_tensor_scan(rows[:, 2], keep[:], rows[:, 1], 0.0, ALU.mult, ALU.add)
                    link(dve.tensor_tensor_scan(rows[:, 3], rows[:, 1], rows[:, 0], 0.0, ALU.add, ALU.max))
                    tt(rows[:, 4], rows[:, 2], rows[:, 3], ALU.subtract)
                    tt(rows[:, 0], rows[:, 0], rows[:, 2], ALU.subtract)
                    dve.memset(msr[:, 0:1], 0.0)
                    link(dve.tensor_copy(msr[:, 1:NT], rows[:, 3, L - 1:T - 1:L]))
                    crow = [MH, NT, L]
                    tt(by_chunk(rows[:, 5]), by_chunk(rows[:, 4]), msr[:].unsqueeze(2).to_broadcast(crow), ALU.add)
                    tt(by_chunk(rows[:, 6]), by_chunk(rows[:, 0]),
                       by_chunk(rows[:, 4])[:, :, L - 1:L].to_broadcast(crow), ALU.add)
                    dve.tensor_scalar(rows[:, 7], rows[:, 3], -1.0, None, ALU.mult).then_inc(s["m_rows"], 1)
                    dve.wait_ge(s["m_colT"], 1)
                    dve.tensor_copy(dec[:], ps[3][:, 0:2 * NT].rearrange("p (a c) -> p a c", a=2))
                    link(dve.tensor_copy(colt[:], ps[2][:, 0:4 * NT * MH].rearrange("p (a c n) -> p a c n", a=4, c=NT)))
                    dve.tensor_scalar(colt[:, 2], colt[:, 2], HD ** -0.5, None, ALU.mult).then_inc(s["m_cols"], 1)
                    dve.wait_ge(s["m_cols"], 1)
                    for head in range(MH):
                        dve.wait_ge(s["m_bc"], head + 1)
                        for c in range(NT):
                            span = slice(c * L, (c + 1) * L)
                            last = dve.scalar_tensor_tensor(wT[:, head, span], ps[4 + head][:, span],
                                                            colt[:, 0, c, head:head + 1], maskT[:], ALU.add, ALU.add)
                        last.then_inc(s["m_arg"], 1)
                    for n in range(2):
                        dve.wait_ge(s["m_kT"], n + 1)
                        tt(kw[:, :, 2 * n:2 * n + 2], ps[n][:].rearrange("p (c a d) -> p c a d", c=NT, a=2),
                           colt[:, 2, :, 2 * n:2 * n + 2].unsqueeze(3).to_broadcast([P, NT, 2, HD]), ALU.mult).then_inc(s["m_kw"], 1)
                    for head in range(MH):
                        dve.wait_ge(s["m_s"], head + 1)
                        dve.wait_ge(s["m_w"], head + 1)
                        dve.scalar_tensor_tensor(wT[:, head], ps[4 + head][:], HD ** -0.5, wT[:, head], ALU.mult,
                                                 ALU.mult).then_inc(s["m_p"], 1)
                    W1 = HD + 1
                    for c in range(NT):
                        dve.wait_ge(s["m_chunk"], c + 1)
                        if c == 0:
                            dve.tensor_copy(cst[:], ps[2][:, 0:2 * W1].rearrange("p (a d) -> p a d", a=2)).then_inc(s["m_state"], 1)
                            dve.tensor_copy(nu[:, 0], ps[0][:, 0:MH * W1].rearrange("p (n d) -> p n d", n=MH)).then_inc(s["m_nu"], 1)
                            continue
                        if c < NT - 1:
                            dve.wait_ge(s["m_state"], 2 * c - 1)
                            for a in range(2):
                                dve.scalar_tensor_tensor(cst[:, a], cst[:, a], dec[:, a, c:c + 1], ps[2][:, a * W1:(a + 1) * W1],
                                                         ALU.mult, ALU.add).then_inc(s["m_state"], 1)
                        for odd in range(2):
                            link(tt(mtmp[:, odd::2], ps[1 + 2 * odd][:, 0:2 * W1].rearrange("p (n d) -> p n d", n=2),
                                    colt[:, 1, c, odd::2].unsqueeze(2).to_broadcast([P, 2, W1]), ALU.mult))
                        tt(nu[:, c], mtmp[:], ps[0][:, 0:MH * W1].rearrange("p (n d) -> p n d", n=MH), ALU.add).then_inc(
                            s["m_nu"], 1)
                    dve.wait_ge(s["m_nu"], NT)
                    link(absolute(dve, mden[:, 0], nu[:, :, :, HD]))
                    link(tt(mden[:, 0], mden[:, 0], colt[:, 3], ALU.max))
                    link(dve.reciprocal(mden[:, 1], mden[:, 0]))
                    dve.wait_ge(s["m_so"], 1)
                    for i in range(NT):
                        yt = ytok[:, i, 0:MLS].rearrange("p (n d) -> p n d", n=MH)
                        link(tt(yt, nu[:, i, :, 0:HD], mden[:, 1, i].unsqueeze(2).to_broadcast([P, MH, HD]), ALU.mult))
                    for i in range(NT):
                        last = tt(ytok[:, i, 0:MLS], ytok[:, i, 0:MLS], so[:, i], ALU.mult)
                    link(last)

                    def rope(x, heads):
                        shape = [P, NT, heads, ROT]
                        size = NT * heads * ROT
                        ts = [rtmp[:, n, 0:size].rearrange("p (i a c) -> p i a c", i=NT, a=heads) for n in range(4)]
                        cos_, sin_ = (v[:].unsqueeze(2).to_broadcast(shape) for v in (cosr, sinr))
                        x1, x2 = x[:, :, :, 0:ROT], x[:, :, :, ROT:2 * ROT]
                        tt(ts[0], x1, cos_, ALU.mult)
                        tt(ts[1], x2, sin_, ALU.mult)
                        tt(ts[2], x2, cos_, ALU.mult)
                        link(tt(ts[3], x1, sin_, ALU.mult))
                        tt(x1, ts[0], ts[1], ALU.subtract)
                        return tt(x2, ts[2], ts[3], ALU.add)

                    link(rope(z[:, :, ZQ:ZQ + NSA].rearrange("p i (a d) -> p i a d", d=HD), NH))
                    for a in (ZKC, ZKS, ZKW):
                        last = rope(z[:, :, a:a + GW].rearrange("p i (a d) -> p i a d", d=HD), NGR)
                        if a != ZKW:
                            link(last)
                    last.then_inc(s["n_rope"], 1)
                    dve.wait_ge(s["n_kT"], 2)
                    dve.tensor_copy(ksT[:], ps[4][:]).then_inc(s["n_k"], 1)
                    dve.tensor_copy(kwT[:], ps[5][:]).then_inc(s["n_k"], 1)
                    for kv, pe_row in ((0, R_PEK), (1, R_PEV)):
                        dve.wait_ge(s["n_kT"], 3 + kv)
                        for g in range(NGR):
                            src = ps[6 + kv][g * HD:(g + 1) * HD, :].rearrange("p (m q) -> p q m", q=CS_)
                            for q in range(2):
                                to = slice(q * HD, (q + 1) * HD)
                                for half in range(2):
                                    js = slice(half * 8, half * 8 + 8)
                                    last = tt(flat[to, kv, js, g, :], src[:, q::2, half:half + NCMP],
                                              pcol[to, pe_row + half * 8:pe_row + half * 8 + 8].unsqueeze(2).to_broadcast(
                                                  [HD, 8, NCMP]), ALU.add)
                        last.then_inc(s["n_flat"], 1)
                    dve.wait_ge(s["n_kcT"], 1)
                    dve.tensor_copy(kcT[:, 0:NCMP], ps[4][:, 0:NCMP])
                    dve.tensor_copy(vcm[0:NCMP], ps[5][0:NCMP, 0:GW].rearrange("p (g d) -> p g d", g=NGR)).then_inc(s["n_kc"], 1)
                    dve.wait_ge(s["n_gate"], 1)

                    def masked(u):
                        i, slot = u // NH, u % 2
                        dve.wait_ge(s["n_score"], u + 1)
                        if u >= 2:
                            dve.wait_ge(s["n_pT"], u - 1)
                        sc, wc = ps[2 * slot], ps[2 * slot + 1]
                        n_win = min(i + 1, WIN // P + 1)
                        for kind, (src, msk) in enumerate((
                            (wc[:, 384:384 + NCMP], cmask[:, i, 0:NCMP]),
                            (sc[:, 0:(i + 1) * P], mask[:, 512 - (i + 1) * P:512]),
                            (wc[:, 0:n_win * P], wmask[:, 384 - n_win * P:384]),
                        )):
                            a, width = spans(i)[kind]
                            last = dve.tensor_tensor_reduce(sm[:, slot, a:a + width], src, msk, 1.0, 3 * NEG, ALU.add, ALU.max,
                                                            am[:, slot, kind:kind + 1])
                        link(last)
                        dve.tensor_scalar(am[:, slot, 3:6], am[:, slot, 0:3], -HD ** -0.5, None, ALU.mult).then_inc(s["n_max"], 1)

                    def weigh(u):
                        i, slot, head = u // NH, u % 2, u % NH
                        dve.wait_ge(s["n_exp"], u + 1)
                        if i == 0:
                            a, width = spans(i)[0]
                            tt(sm[:, slot, a:a + width], sm[:, slot, a:a + width], cvalid[:, 0:NCMP], ALU.mult)
                        link(dve.reciprocal(am[:, slot, 9:12], am[:, slot, 6:9]))
                        link(tt(am[:, slot, 12:15], am[:, slot, 9:12], gate[:, i, 3 * head:3 * head + 3], ALU.mult))
                        for kind, (a, width) in enumerate(spans(i)):
                            last = dve.tensor_scalar(sm[:, slot, a:a + width], sm[:, slot, a:a + width],
                                                     am[:, slot, 12 + kind:13 + kind], None, ALU.mult)
                        last.then_inc(s["n_p"], 1)

                    def take_turned(u):
                        i, slot = u // NH, u % 2
                        n_win = min(i + 1, WIN // P + 1)
                        dve.wait_ge(s["n_pT"], u + 1)
                        if u >= 2:
                            dve.wait_ge(s["n_av"], u - 1)
                        dve.tensor_copy(pt[0:NCMP, slot, 896:1024], ps[5][0:NCMP, 384:512])
                        dve.tensor_copy(pt[:, slot, 512:512 + n_win * P], ps[5][:, 0:n_win * P]).then_inc(s["n_pd"], 1)

                    for u in range(NT * NH + 1):
                        if u < NT * NH:
                            masked(u)
                        if u >= 1:
                            weigh(u - 1)
                        if u >= 2:
                            take_turned(u - 2)
                    take_turned(NT * NH - 1)

                    heads = MH + NH
                    for i in range(NT):
                        dve.wait_ge(s["g_sq"], i + 1)
                        last = dve.tensor_reduce(gst[:, 2, i], gsq[:, i].rearrange("p (n d) -> p n d", d=HD), AX, ALU.add)
                    link(last)
                    dve.tensor_scalar(gst[:, 0], gst[:, 2], 1.0 / HD, EPS, ALU.mult, ALU.add).then_inc(s["g_ms"], 1)
                    dve.wait_ge(s["g_rt"], 1)
                    link(dve.reciprocal(gst[:, 2], gst[:, 1]))
                    for i in range(NT):
                        yt = ytok[:, i].rearrange("p (n d) -> p n d", d=HD)
                        tt(yt, yt, gst[:, 2, i].unsqueeze(2).to_broadcast([P, heads, HD]), ALU.mult).then_inc(s["g_y"], 1)
                    for k in range(2):
                        dve.wait_ge(s["x_hi"], KD + k + 1)
                        tt(xl[:, k], su[:, k], xh[:, k].bitcast(F32), ALU.subtract).then_inc(s["x_lo"], 1)
                    for k in range(2, KD):
                        dve.wait_ge(s["x_hi"], KD + k + 1)
                        dve.scalar_tensor_tensor(xl[:, k], ps[k][:], pcol[:, R_GN + k:R_GN + k + 1], xh[:, k].bitcast(F32),
                                                 ALU.mult, ALU.subtract).then_inc(s["x_lo"], 1)

                    post_norm(1, 0)
                    dve.wait_ge(s["h_new"], NT)
                    pre_norm(2)
                    turned_low(2 * KD, R_MLP)
                    for part in range(2):
                        for g in range(16 * part, 16 * part + 16):
                            b, n = B_UP[part] + g % 16 // 4, g % 4
                            dve.wait_ge(s["f_relu"], g + 1)
                            if g >= 2:
                                dve.wait_ge(s["f_lo"], g - 1)
                            dve.scalar_tensor_tensor(sq_t[:, g % 2], ps[4 * (b % 2) + n][:], 0.0, act_t[:, g % 2], ALU.max,
                                                     ALU.mult).then_inc(s["f_sq"], 1)
                            if g % 16:
                                low(dve, g - 1, fl, fh, sq_t, s)
                        low(dve, 16 * part + 15, fl, fh, sq_t, s)
                    for half in range(2):
                        b = B_DOWN[1] + half
                        dve.wait_ge(s["w_used"], blocks[b][0] + blocks[b][1])
                        for i in range(NT):
                            into = fbuf[:, i, 512 * half:512 * half + 512]
                            last = tt(into, into, ps[4 * (b % 2) + i][:], ALU.add)
                        last.then_inc(s["evac_added"], 1)
                    post_norm(3, 1)

                @block.tensor
                def _(pe):
                    def product(b):
                        first, deep, on_features, width = blocks[b]
                        group = 4 * (b % 2)
                        hi, lo = (fh, fl) if b in (B_DOWN[0], B_DOWN[0] + 1, B_DOWN[1], B_DOWN[1] + 1) else (xh, xl)
                        for k in range(deep):
                            unit = first + k
                            slot = unit % NSPLIT
                            pe.wait_ge(s["w_lo"], unit + 1)
                            if on_features:
                                for n in range(width // P):
                                    cols = slice(n * P, (n + 1) * P)
                                    for m, (w, x) in enumerate(((wh, hi), (wh, lo), (wl, hi))):
                                        last = pe.matmul(ps[group + n][:], w[:, slot, cols], x[:, k], start=k == 0 and m == 0,
                                                         stop=k == deep - 1 and m == 2)
                            else:
                                for i in range(NT):
                                    rows_ = slice(i * P, (i + 1) * P)
                                    for m, (x, w) in enumerate(((hi, wh), (hi, wl), (lo, wh))):
                                        last = pe.matmul(ps[group + i][:, 0:width], x[:, k, rows_], w[:, slot, 0:width],
                                                         start=k == 0 and m == 0, stop=k == deep - 1 and m == 2)
                            last.then_inc(s["w_used"], 1)

                    def turn(src, k0, count, used):
                        for k in range(count):
                            for i in range(NT):
                                last = pe.transpose(ps[k0 + k][:, i * P:(i + 1) * P], src[:, i, k * P:(k + 1) * P], ident[:])
                            last.then_inc(s["turned"], 1)

                    pe.wait_ge(s["cols_turned"], 1)
                    pe.transpose(ps[7][:, 0:NROW], prow[:], ident[0:NROW, 0:NROW]).then_inc(s["cols_turned"], 1)
                    pe.wait_ge(s["normed"], NT)
                    turn(fbuf, 0, KD - 1, 0)
                    pe.wait_ge(s["cols_ready"], 1)
                    for i in range(NT):
                        last = pe.transpose(ps[7][:, i * P:(i + 1) * P], fbuf[:, i, 7 * P:8 * P], ident[:])
                    last.then_inc(s["turned"], 1)
                    pe.wait_ge(s["x_lo"], KD)
                    for b in range(B_OUT):
                        if b >= 2:
                            pe.wait_ge(s["evacuated"], b - 1)
                        product(b)

                    pe.wait_ge(s["evacuated"], B_OUT)
                    pe.wait_ge(s["s5_nat"], 1)
                    for n in range(4):
                        last = pe.transpose(ps[0][:, n * P:(n + 1) * P],
                                            bd[:, n // 2, 4 * (n % 2):4 * (n % 2) + 4].rearrange("p j c -> p (j c)"), ident[:])
                    last.then_inc(s["s5_natT"], 1)
                    for n in range(4):
                        last = pe.transpose(ps[1][:, n * P:(n + 1) * P], cb[:, n // 2, n % 2], ident[:])
                    last.then_inc(s["s5_natT"], 1)
                    pe.wait_ge(s["s5_mats"], 1)
                    for j in range(NJ):
                        if j >= 2:
                            pe.wait_ge(s["s5_rot"], j - 1)
                        rows_ = slice(32 * (j % 4), 32 * (j % 4) + 32)
                        for part in range(2):
                            last = pe.matmul(ps[2 * (j % 2) + part][:], bT[rows_, 2 * part + j // 4], su[rows_, j // 4],
                                             start=True, stop=True)
                        last.then_inc(s["s5_bu"], 1)
                    for n in range(2):
                        for q in range(4):
                            rows_ = slice(32 * q, 32 * q + 32)
                            pe.wait_ge(s["s5_x"], 4 * n + q + 1)
                            for part, v in enumerate((vr, vi)):
                                last = pe.matmul(ps[4 + n][rows_, :], cT[:, part, n, rows_], v[:, 4 * n + q], start=part == 0,
                                                 stop=part == 1)
                        last.then_inc(s["s5_y"], 1)
                    pe.wait_ge(s["s5_gelu"], 2)
                    for m in range(2):
                        for c in range(2):
                            last = pe.matmul(ps[6 + m][:], wglu[:, c, m * P:(m + 1) * P], tmp[:, 2 + c], start=c == 0, stop=c == 1)
                        last.then_inc(s["s5_glu"], 1)
                    for m in range(2):
                        pe.wait_ge(s["s5_sq"], m + 1)
                        pe.matmul(ps[4 + m][:], bones[:], tmp[:, m], start=True, stop=True).then_inc(s["s5_ms"], 1)

                    for n, a in enumerate((ZI, ZFG)):
                        for i in range(NT):
                            last = pe.transpose(ps[n][0:MH, i * P:(i + 1) * P], z[:, i, a:a + MH], ident[:])
                    last.then_inc(s["m_gateT"], 1)
                    pe.wait_ge(s["m_exp"], 1)
                    for a, row in enumerate((0, 5, 6, 7)):
                        for c in range(NT):
                            col = (a * NT + c) * MH
                            pe.transpose(ps[2][:, col:col + MH], rows[:, row, c * L:(c + 1) * L], ident[0:MH, 0:MH])
                    for a in range(2):
                        last = pe.matmul(ps[3][:, a * NT:(a + 1) * NT], sel2[:, a], rows[:, 5, L - 1:T:L], start=True, stop=True)
                    last.then_inc(s["m_colT"], 1)
                    pe.wait_ge(s["s5_rt"], 2)
                    for head in range(MH):
                        pe.matmul(ps[4 + head][:], sel[:, head], rows[:, 4], start=True, stop=True).then_inc(s["m_bc"], 1)
                    pe.wait_ge(s["m_qk"], 4)
                    for n in range(2):
                        for c in range(NT):
                            last = pe.transpose(ps[n][:, c * L:(c + 1) * L], qk[:, 2 + n, c * L:(c + 1) * L], ident[:])
                        last.then_inc(s["m_kT"], 1)
                    for head in range(MH):
                        pe.wait_ge(s["m_arg"], head + 1)
                        rows_ = slice(HD * (head % 2), HD * (head % 2) + HD)
                        for c in range(NT):
                            span = slice(c * L, (c + 1) * L)
                            last = pe.matmul(ps[4 + head][:, span], qk[rows_, 2 + head // 2, span], qk[rows_, head // 2, span],
                                             start=True, stop=True)
                        last.then_inc(s["m_s"], 1)
                    W1 = HD + 1
                    pe.wait_ge(s["m_kw"], 2)
                    pe.wait_ge(s["m_va"], 1 + NT)
                    pe.wait_ge(s["m_cols"], 1)
                    for c in range(NT):
                        span = slice(c * L, (c + 1) * L)
                        if c:
                            pe.wait_ge(s["m_nu"], c)
                            pe.wait_ge(s["m_state"], 2 * c - 1)
                        for head in range(MH):
                            if c == 0:
                                pe.wait_ge(s["m_p"], head + 1)
                            rows_ = slice(HD * (head % 2), HD * (head % 2) + HD)
                            cols = slice(head * W1, (head + 1) * W1)
                            last = pe.matmul(ps[0][:, cols], wT[:, head, span], va[:, c, head], start=True, stop=True)
                            if c:
                                cols = slice(head // 2 * W1, (head // 2 + 1) * W1)
                                last = pe.matmul(ps[1 + 2 * (head % 2)][:, cols], qk[rows_, head // 2, span],
                                                 cst[rows_, head // 2], start=True, stop=True)
                            if c < NT - 1:
                                a = head // 2
                                last = pe.matmul(ps[2][rows_, a * W1:(a + 1) * W1], kw[:, c, head], va[:, c, head], start=True,
                                                 stop=True)
                        last.then_inc(s["m_chunk"], 1)

                    pe.wait_ge(s["n_rope"], 1)
                    for r in range(R):
                        for i in range(NT):
                            if r == 0:
                                pe.wait_ge(s["n_qa"], i + 1)
                            last = pe.transpose(ps[r][:, i * P:(i + 1) * P], qa[:, i, r].rearrange("p g d -> p (g d)"), ident[:])
                        last.then_inc(s["n_qT"], 1)
                    for n, a in enumerate((ZKS, ZKW, ZKC, ZVC)):
                        for i in range(NT):
                            last = pe.transpose(ps[4 + n][:, i * P:(i + 1) * P], z[:, i, a:a + GW], ident[:])
                        last.then_inc(s["n_kT"], 1)
                    for k, n in enumerate(wholes):
                        kv, j0 = k // (len(wholes) // 2), 2 * (k % (len(wholes) // 2))
                        pe.wait_ge(raw_landed[n % NRAW], 16 * (n // NRAW + 1))
                        if j0 == 0:
                            pe.wait_ge(s["n_flat"], kv + 1)
                            pe.wait_ge(s["n_q"], 2 * kv + 2)
                        for jj in range(2):
                            for c in range(2):
                                last = pe.matmul(ps[2 * kv + c][:, 0:NGR * NCMP],
                                                 raw[:, n % NRAW, jj * CHID + c * P:jj * CHID + (c + 1) * P],
                                                 flat[:, kv, j0 + jj].rearrange("p g n -> p (g n)"),
                                                 start=j0 + jj == 0, stop=j0 + jj == CB // 2 - 1)
                        last.then_inc(s["whole_used"], 1)
                    pe.wait_ge(s["n_hid"], 4)
                    pe.wait_ge(s["n_k"], 2)
                    for g in range(NGR):
                        blocks_ = slice(g * NCMP, (g + 1) * NCMP)
                        for c in range(2):
                            pe.matmul(ps[4][g * HD:(g + 1) * HD, 0:NCMP], w2c[:, 0, c], hg[:, c, blocks_], start=c == 0, stop=c == 1)
                        for c in range(2):
                            last = pe.matmul(ps[5][0:NCMP, g * HD:(g + 1) * HD], hg[:, 2 + c, blocks_], w2c[:, 1, c],
                                             start=c == 0, stop=c == 1)
                    last.then_inc(s["n_kcT"], 1)
                    pe.wait_ge(s["n_kc"], 1)

                    def scores(u):
                        i, slot, head = u // NH, u % 2, u % NH
                        g, r = head // R, head % R
                        n_win = min(i + 1, WIN // P + 1)
                        if u >= 2:
                            pe.wait_ge(s["n_max"], u - 1)
                        rows_ = slice(g * HD, (g + 1) * HD)
                        q = qT[rows_, r, i * P:(i + 1) * P]
                        pe.matmul(ps[2 * slot][:, 0:(i + 1) * P], q, ksT[rows_, 0:(i + 1) * P], start=True, stop=True)
                        pe.matmul(ps[2 * slot + 1][:, 0:n_win * P], q, kwT[rows_, (i + 1 - n_win) * P:(i + 1) * P], start=True,
                                  stop=True)
                        pe.matmul(ps[2 * slot + 1][:, 384:384 + NCMP], q, kcT[rows_, 0:NCMP], start=True, stop=True).then_inc(
                            s["n_score"], 1)

                    def turn_weights(u):
                        i, slot = u // NH, u % 2
                        n_win = min(i + 1, WIN // P + 1)
                        pe.wait_ge(s["n_p"], u + 1)
                        if u:
                            pe.wait_ge(s["n_pa"], u)
                            pe.wait_ge(s["n_pd"], u)
                        for n in range(i + 1):
                            pe.transpose(ps[4][:, n * P:(n + 1) * P], sm[:, slot, n * P:(n + 1) * P], ident[:])
                        pe.transpose(ps[5][0:NCMP, 384:512], sm[:, slot, 896:896 + NCMP], ident[:])
                        for n in range(n_win):
                            last = pe.transpose(ps[5][:, n * P:(n + 1) * P], sm[:, slot, 512 + n * P:512 + (n + 1) * P], ident[:])
                        last.then_inc(s["n_pT"], 1)

                    def combine(u):
                        i, slot, head = u // NH, u % 2, u % NH
                        g = head // R
                        n_win = min(i + 1, WIN // P + 1)
                        o = ps[6 + i % 2][:, head * HD:(head + 1) * HD]
                        if i >= 2 and head == 0:
                            pe.wait_ge(s["n_o"], i - 1)
                        pe.wait_ge(s["n_pd"], u + 1)
                        pe.wait_ge(s["n_pa"], u + 1)
                        pe.matmul(o, pt[0:NCMP, slot, 896:1024], vcm[0:NCMP, g], start=True, stop=False)
                        for n in range(n_win):
                            a = ZVW + g * HD
                            pe.matmul(o, pt[:, slot, 512 + n * P:512 + (n + 1) * P], z[:, i + 1 - n_win + n, a:a + HD],
                                      start=False, stop=False)
                        for n in range(i + 1):
                            a = ZVS + g * HD
                            last = pe.matmul(o, pt[:, slot, n * P:(n + 1) * P], z[:, n, a:a + HD], start=False, stop=n == i)
                        last.then_inc(s["n_av"], 1)

                    for u in range(NT * NH + 2):
                        if u < NT * NH:
                            scores(u)
                        if 1 <= u <= NT * NH:
                            turn_weights(u - 1)
                        if u >= 2:
                            combine(u - 2)

                    pe.wait_ge(s["g_y"], NT)
                    turn(ytok, 2, KD - 2, 0)
                    pe.wait_ge(s["x_lo"], 2 * KD)
                    for b in range(B_OUT, B_OUT + 2):
                        product(b)
                    pe.wait_ge(s["normed"], 2 * NT)
                    turn(fbuf, 0, KD, 0)
                    pe.wait_ge(s["x_lo"], 3 * KD)
                    for part in range(2):
                        for n in range(4):
                            b = B_UP[part] + n
                            if part and n < 2:
                                pe.wait_ge(s["evacuated"], 9 + n)
                            elif n >= 2:
                                pe.wait_ge(s["f_sq"], 16 * part + 4 * (n - 1))
                            product(b)
                        pe.wait_ge(s["f_lo"], 16 * (part + 1))
                        for b in (B_DOWN[part], B_DOWN[part] + 1):
                            product(b)
            nc.multi_engine_barrier(list(nc.engines), sems_to_clear=layer_sems)

        with nc.Block() as block:
            @block.sync
            def _(sp):
                sp.dma_start(out[0].rearrange("(i p) d -> p i d", p=P), h[:]).then_inc(once["stored"], 16)
                sp.wait_ge(once["stored"], 16)


def kernel(**inputs):
    import concourse.bacc as bacc
    import numpy as np
    from concourse.bass_utils import run_bass_kernel_spmd

    nc = bacc.Bacc("TRN2", target_bir_lowering=False, num_devices=1)
    arrays, tensors = {}, {}
    for name, value in inputs.items():
        a = np.ascontiguousarray(value)
        arrays[f"in_{name}"] = a
        tensors[name] = nc.dram_tensor(f"in_{name}", a.shape, mybir.dt.from_np(a.dtype), kind="ExternalInput").ap()
    out = nc.dram_tensor("out", (1, T, D), F32, kind="ExternalOutput").ap()
    build(nc, tensors, out)
    result = run_bass_kernel_spmd(nc, [arrays], core_ids=[0])
    return result.results[0]["out"]
```

```python
from contextlib import ExitStack

import concourse.bass as bass
from concourse import mybir

F32 = mybir.dt.float32
F32R = mybir.dt.float32r
I32 = mybir.dt.int32
ALU = mybir.AluOpType
ACT = mybir.ActivationFunctionType
AX = mybir.AxisListType.X

P = 128
DEPTH, D, T = 2, 1024, 512
NT = T // P
KD = D // P
SSM, MLS, NSA = D // 4, D // 4, D // 2
NG, GH, NP_ = 16, 16, 64
NJ = NG * NP_ // P
L = P
MH, HD, KCONV = 4, 64, 4
NH, NGR = NSA // HD, 2
R = NH // NGR
CB, CS_, CHID = 32, 16, 256
NCMP = T // CS_ - CB // CS_ + 1
WIN = 256
FF = 4 * D
EPS = 1e-6
NEG = -2.0 ** 99
THETA, ROT = 500000.0, HD // 8
D_IN = SSM + 4 * MLS + 2 * MH + NSA + 6 * NGR * HD + 3 * NH

ZF = SSM + 2 * MLS
ZT = D_IN - ZF
ZV, ZO, ZI, ZFG, ZQ = 0, MLS, 2 * MLS, 2 * MLS + MH, 2 * MLS + 2 * MH
ZKC = ZQ + NSA
GW = NGR * HD
ZVC, ZKS, ZVS, ZKW, ZVW = (ZKC + n * GW for n in range(1, 6))
ZG = ZKC + 6 * GW

R_PRE, R_MLP, R_GN, R_D, R_CONV = 0, 8, 16, 24, 26
R_PEK, R_PEV = R_CONV + 4 * KCONV, R_CONV + 4 * KCONV + CB // 2
R_LR = R_PEV + CB // 2
R_LI = R_LR + NJ
R_DT = 96
NROW = R_DT + NJ

TWO_PI = 6.283185307179586
C1 = 6.28125
C2 = round((TWO_PI - C1) * 2 ** 22) / 2 ** 22
C3 = TWO_PI - C1 - C2
ROUND = 1.5 * 2.0 ** 23
ROUND13 = 1.5 * 2.0 ** 10
PI_IN = 3.1415925

NRAW, NSPLIT = 6, 4


(S_DT, S_X, S_MAG, S_TH, S_R, S_ABS, S_SIN, S_COS, S_ARE, S_AIM, S_DEN, S_RDEN, S_E, S_GRE, S_GIM, S_RHI, S_RLO,
 S_IRE, S_IIM, S_T0, S_T1, S_T2, S_T3) = range(23)
N_PARAMS = 23
COMPRESSED, SELECTED, WINDOW = range(3)


def key_tiles(i):
    return ([(SELECTED, n) for n in range(i + 1)] + [(WINDOW, n) for n in range(max(0, i - WIN // P), i + 1)]
            + [(COMPRESSED, 0)])


def reduce_angle(dve, link, out, angle, whole):
    link(dve.tensor_scalar(whole, angle, 1.0 / TWO_PI, ROUND, ALU.mult, ALU.add))
    link(dve.tensor_scalar(whole, whole, ROUND, None, ALU.subtract))
    for c in (C1, C2, C3):
        link(dve.scalar_tensor_tensor(out, whole, -c, angle, ALU.mult, ALU.add))
        angle = out
    link(dve.tensor_scalar(out, out, PI_IN, -PI_IN, ALU.min, ALU.max))


def absolute(dve, out, x):
    return dve.scalar_tensor_tensor(out, x, -1.0, x, ALU.mult, ALU.max)


def low(dve, g, fl, fh, sq_t, s):
    dve.wait_ge(s["f_hi"], g + 1)
    dve.tensor_tensor(fl[:, g % 16], sq_t[:, g % 2], fh[:, g % 16].bitcast(F32), ALU.subtract).then_inc(s["f_lo"], 1)


def weight_units(t, layer):
    units = []
    cols = [(0, 512), (512, ZF)] + [(ZF + a, min(ZF + a + 512, D_IN)) for a in range(0, ZT, 512)]
    for a, b in cols:
        for k in range(KD):
            units.append((t["w_in"][layer, k * P:(k + 1) * P, a:b], "split", b - a))
    for name in ("cmp_w1_k", "cmp_w1_v"):
        for j in range(CB // 4):
            src = t[name][layer, 2 * j * P:(2 * j + 2) * P, :].rearrange("(j p) c -> p j c", p=P)
            units.append((src, "whole", 2 * CHID))
    for half in range(2):
        for k in range(KD):
            units.append((t["w_out"][layer, k * P:(k + 1) * P, half * 512:half * 512 + 512], "split", 512))
    for part in range(2):
        for c in range(4):
            for k in range(KD):
                a = part * FF // 2 + c * 512
                units.append((t["mlp_w1"][layer, k * P:(k + 1) * P, a:a + 512], "split", 512))
        for half in range(2):
            for k in range(FF // 2 // P):
                a = part * FF // 2 + k * P
                units.append((t["mlp_w2"][layer, a:a + P, half * 512:half * 512 + 512], "split", 512))
    return units, [b - a for a, b in cols]


def build(nc, t, out):
    ctx = ExitStack()
    with ctx:
        at = [nc.sbuf_base]
        place = {}

        def over(name, shape, under, dt=F32):
            return nc.alloc_sbuf_tensor_at(name, shape, dt, offset=place[under])

        def sb(name, shape, dt=F32):
            place[name] = at[0]
            size = 4
            for n in shape[1:]:
                size *= n
            size = (size + 31) // 32 * 32
            tensor = nc.alloc_sbuf_tensor_at(name, shape, dt, offset=at[0])
            at[0] += size
            return tensor

        at[0] = (at[0] + 31) // 32 * 32
        h = sb("h", [P, NT, D])
        xh = sb("xh", [P, KD, T], F32R)
        xl = sb("xl", [P, KD, T], F32R)
        raw = sb("raw", [P, NRAW, 512])
        wh = sb("wh", [P, NSPLIT, 512], F32R)
        wl = sb("wl", [P, NSPLIT, 512], F32R)
        fbuf = sb("fbuf", [P, NT, D])
        gpost = sb("gpost", [P, 2, D])
        junk = over("junk", [P, D], "xl")
        ident = sb("ident", [P, P])
        mask = sb("mask", [P, 512])
        wmask = sb("wmask", [P, 384])
        cmask = sb("cmask", [P, NT, 32])
        cvalid = sb("cvalid", [P, 1])
        nident = sb("nident", [P, P])
        identr = sb("identr", [P, P], F32R)
        onesr = sb("onesr", [P, P], F32R)
        wmaskT = sb("wmaskT", [P, 3, P], F32R)
        cmaskT = sb("cmaskT", [P, NT, P], F32R)
        maskT = sb("maskT", [P, P])
        bones = sb("bones", [P, P])
        par = sb("par", [P, 4])
        sel = sb("sel", [MH, MH, P])
        sel2 = sb("sel2", [MH, 2, P])
        keep = sb("keep", [MH, T])
        steps = sb("steps", [P, L + 1])
        stepi = sb("stepi", [P, L + 1], I32)
        consts = sb("consts", [P, 2])
        posi = sb("posi", [P, NT], I32)
        posf = sb("posf", [P, NT])
        cosr = sb("cosr", [P, NT, ROT])
        sinr = sb("sinr", [P, NT, ROT])
        prow = sb("prow", [NROW, P])
        pcol = sb("pcol", [P, NROW])
        dt8 = sb("dt8", [NROW, 2])
        gateb = sb("gateb", [MH, 2])
        wglu = sb("wglu", [P, 2, SSM])
        w2c = sb("w2c", [P, 2, 2, HD])
        bnat = sb("bnat", [P, 2, NJ, GH])
        cnat = sb("cnat", [P, 2, 2, NP_])
        stat = sb("stat", [P, 4, NT])
        small = sb("small", [P, 24, NJ])
        shared = at[0]
        z = sb("z", [P, NT, ZT])
        su = sb("su", [P, 2, T])
        qkr = sb("qkr", [P, 4, KCONV - 1 + T])
        ytok = over("ytok", [P, NT, MLS + NSA], "fbuf")
        work = at[0]
        vr = sb("vr", [P, NJ, T])
        vi = over("vi", [P, NJ, T], "fbuf")
        ctab = sb("ctab", [P, NJ, L + 1])
        stab = sb("stab", [P, NJ, L + 1])
        bd = sb("bd", [P, 2, NJ, 32])
        bT = sb("bT", [P, 4, P])
        cb = sb("cb", [P, 2, 2, P])
        cT = sb("cT", [P, 2, 2, P])
        tmp = sb("tmp", [P, 4, T])
        s5_end = at[0]
        at[0] = work
        tang = sb("tang", [P, NJ, L + 1])
        tnum = sb("tnum", [P, NJ, L + 1])
        assert at[0] <= work + NJ * T * 4
        tred = over("tred", [P, NJ, L + 1], "fbuf")
        at[0] = work
        qk = sb("qk", [P, 4, T])
        wT = sb("wT", [P, MH, T])
        kw = sb("kw", [P, NT, MH, HD])
        va = sb("va", [P, NT, MH, HD + 1])
        nu = sb("nu", [P, NT, MH, HD + 1])
        so = sb("so", [P, NT, MLS])
        rows = over("rows", [MH, 8, T], "xl")
        msr = sb("msr", [MH, NT])
        colt = sb("colt", [P, 4, NT, MH])
        cst = sb("cst", [P, 2, HD + 1])
        dec = sb("dec", [P, 2, NT])
        mden = sb("mden", [P, 2, NT, MH])
        mtmp = sb("mtmp", [P, MH, HD + 1])
        mls_end = at[0]
        at[0] = work
        qa = over("qa", [P, NT, R, NGR, HD], "xh")
        flat = over("flat", [P, 2, CB // 2, NGR, NCMP], "xl")
        qh = sb("qh", [P, R, T], F32R)
        ql = sb("ql", [P, R, T], F32R)
        ksh = over("ksh", [P, 2, NGR, T], "qkr", F32R)
        ksl = sb("ksl", [P, 2, NGR, T], F32R)
        vsw = sb("vsw", [P, 2, NT, NGR, HD + 1])
        vca = sb("vca", [P, NGR, HD + 1])
        rtmp = sb("rtmp", [P, 4, NT * NH * ROT])
        hg = sb("hg", [P, 4, NGR * NCMP])
        gate = sb("gate", [P, NT, 3 * NH])
        am = sb("am", [P, 4, 12])
        cf = sb("cf", [P, 2, 12])
        diag = over("diag", [P, 2, 3, R, P], "xl", F32R)
        place["behind diag"] = place["xl"] + 2 * 3 * R * P * 4
        kch = over("kch", [P, NGR, P], "behind diag", F32R)
        place["behind kch"] = place["behind diag"] + NGR * P * 4
        kcl = over("kcl", [P, NGR, P], "behind kch", F32R)
        pT = over("pT", [P, 4, R, P], "xh")
        prod = sb("prod", [P, 2, R, 3, HD])
        junkz = over("junkz", [P, 512], "z")
        gsq = over("gsq", [P, NT, MLS + NSA], "z")
        gst = over("gst", [P, 3, NT, 12], "mtmp")
        nsa_end = at[0]
        at[0] = shared
        fh = sb("fh", [P, FF // 2 // P, T], F32R)
        fl = sb("fl", [P, FF // 2 // P, T], F32R)
        act_t = sb("act_t", [P, 2, T])
        sq_t = sb("sq_t", [P, 2, T])
        mlp_end = at[0]
        ps = [ctx.enter_context(nc.psum_tensor(f"ps{n}", [P, 512], F32)) for n in range(8)]


        def sems(text):
            made = {name: ctx.enter_context(nc.semaphore(name)) for name in text.split()}
            numbers = [x.num for x in made.values()]
            assert numbers == list(range(numbers[0], numbers[0] + len(numbers)))
            return made, range(numbers[0], numbers[0] + len(numbers))

        once, _ = sems("x_landed pool_made rope_ready rope_trig setup_steps stored")
        s, layer_sems = sems("""
            params_landed raw_landed0 raw_landed1 raw_landed2 raw_landed3 raw_landed4 raw_landed5
            w_hi w_lo w_used whole_used evacuated f_sum f_gain
            act_steps dve_steps cols_turned cols_ready ssq msq rms normed turned x_hi x_lo h_new
            f_relu f_sq f_hi f_lo
            s5_dt s5_ang s5_trig s5_phase s5_table s5_nat s5_natT s5_mats s5_bu s5_rot s5_x s5_y
            s5_ypre s5_gelu s5_glu s5_sig s5_sq s5_ms s5_rt
            m_pad m_conv m_qk m_gateT m_fx m_ln m_rows m_exp m_colT m_bc m_cols m_arg m_w m_s m_p m_kT m_kw
            m_va n_va m_chunk m_state m_nu m_so m_out
            n_rope n_qa n_qT n_q n_ql n_kT n_kh n_k n_flat n_hid n_kcT n_kch n_kc n_gate
            n_score n_max n_diag n_diag_rest n_shifted n_exp n_av n_o n_y
            g_sq g_ms g_rt g_y""")
        raw_landed = [s[f"raw_landed{n}"] for n in range(NRAW)]

        def chain(engine, semaphore):
            count = [0]

            def link(instruction):
                count[0] += 1
                instruction.then_inc(semaphore, 1)
                engine.wait_ge(semaphore, count[0])
            return link

        wmaskT_f = over("wmaskT_f", [P, 3, P], "z")
        cmaskT_f = over("cmaskT_f", [P, NT, P], "su")
        with nc.Block() as block:
            @block.sync
            def _(sp):
                sp.dma_start(h[:], t["x"][0].rearrange("(i p) d -> p i d", p=P)).then_inc(once["x_landed"], 16)
                sp.dma_start(posi[:], t["positions"][0].rearrange("(i p) -> p i", p=P),
                             allow_slow_non_contiguous=True).then_inc(once["x_landed"], 16)
                sp.wait_ge(once["x_landed"], 32)

            @block.gpsimd
            def _(pool):
                link = chain(pool, once["pool_made"])

                def keep_where(tile, pattern, base, mult, fill, op=ALU.is_ge):
                    link(pool.affine_select(out=tile, in_=tile, pattern=pattern, base=base,
                                            channel_multiplier=mult, compare_op=op, fill=fill))

                for tile, value in ((ident, 0.0), (mask, 0.0), (wmask, 0.0), (cmask, 0.0), (cvalid, 1.0), (nident, 0.0),
                                    (maskT, 0.0), (bones, 1.0 / GH), (sel, 0.0), (sel2, 0.0), (keep, 1.0),
                                    (prow, 0.0), (wmaskT_f, 0.0), (cmaskT_f, 0.0)):
                    link(pool.memset(tile[:], value))
                link(pool.memset(consts[:, 0:1], TWO_PI / 4))
                link(pool.memset(consts[:, 1:2], EPS))
                for n in range(ROT):
                    link(pool.memset(small[:, 0, n:n + 1], THETA ** (-2.0 * n / (2 * ROT))))
                keep_where(ident[:], [[-1, P]], 0, 1, 1.0, ALU.not_equal)
                keep_where(mask[:, 384:512], [[-1, P]], 0, 1, NEG)
                keep_where(wmask[:, 256:384], [[-1, P]], 0, 1, NEG)
                keep_where(wmask[:, 0:128], [[1, P]], -1, -1, NEG)
                keep_where(cmask[:], [[P, NT], [-CS_, 32]], 1 - CB, 1, NEG)
                keep_where(cvalid[:], [[0, 1]], 1 - CB, 1, 0.0)
                keep_where(nident[:], [[-1, P]], 0, 1, -1.0, ALU.not_equal)
                keep_where(wmaskT_f[:, 0], [[-1, P]], -1, 1, NEG)
                keep_where(wmaskT_f[:, 2], [[1, P]], 0, -1, NEG)
                keep_where(cmaskT_f[:], [[P, NT], [1, P]], 1 - CB, -CS_, NEG)
                keep_where(cmaskT_f[:], [[0, NT], [0, P]], NCMP - 1, -1, NEG)
                keep_where(maskT[:], [[1, P]], 0, -1, NEG)
                keep_where(bones[:].rearrange("p (b c) -> p b c", c=GH), [[-GH, P // GH], [0, GH]], 0, 1, 0.0)
                keep_where(bones[:].rearrange("p (b c) -> p b c", c=GH), [[GH, P // GH], [0, GH]], GH - 1, -1, 0.0)
                keep_where(sel[:], [[-1, MH], [0, P]], 0, 1, 1.0, ALU.not_equal)
                keep_where(sel2[:].rearrange("k a (b c) -> k a b c", b=2), [[-2, 2], [-1, 2], [0, HD]], 0, 1, 1.0,
                           ALU.not_equal)
                keep_where(keep[:].rearrange("k (a b) -> k a b", b=L), [[0, NT], [1, L]], 0, 0, 0.0, ALU.not_equal)
                link(pool.iota(stepi[:], [[1, L + 1]], base=0, channel_multiplier=0))

            N_POOL = 14 + 2 + ROT + 17 + 1

            @block.vector
            def _(dve):
                link = chain(dve, once["setup_steps"])
                dve.wait_ge(once["pool_made"], N_POOL)
                link(dve.tensor_copy(steps[:], stepi[:]))
                for parity in range(2):
                    link(dve.tensor_reduce(par[:, parity:parity + 1], bones[:, GH * parity:P:2 * GH], AX, ALU.add))
                link(dve.tensor_scalar(par[:, 0:2], par[:, 0:2], float(GH), None, ALU.mult))
                link(dve.tensor_scalar(par[:, 2:4], par[:, 0:2], -1.0, None, ALU.mult))
                link(dve.tensor_copy(identr[:], ident[:]))
                link(dve.tensor_scalar(onesr[:], ident[:], 0.0, 1.0, ALU.mult, ALU.add))
                link(dve.tensor_copy(wmaskT[:], wmaskT_f[:]))
                link(dve.tensor_copy(cmaskT[:], cmaskT_f[:]))
                dve.wait_ge(once["x_landed"], 32)
                link(dve.tensor_copy(posf[:], posi[:]))
                link(dve.tensor_tensor(sinr[:], posf[:].unsqueeze(2).to_broadcast([P, NT, ROT]),
                                       small[:, 0:1, :].to_broadcast([P, NT, ROT]), ALU.mult))
                reduce_angle(dve, link, sinr[:], sinr[:], cosr[:])
                absolute(dve, cosr[:], sinr[:]).then_inc(once["rope_ready"], 1)

            @block.scalar
            def _(act):
                act.wait_ge(once["rope_ready"], 1)
                act.activation(cosr[:], cosr[:], ACT.Sin, bias=consts[:, 0:1], scale=-1.0).then_inc(once["rope_trig"], 1)
                act.activation(sinr[:], sinr[:], ACT.Sin).then_inc(once["rope_trig"], 1)
                act.wait_ge(once["rope_trig"], 2)

        with nc.Fori(0, DEPTH) as layer:
            with nc.Block() as block:
                units, widths = weight_units(t, layer)
                splits = [n for n, unit in enumerate(units) if unit[1] == "split"]
                wholes = [n for n, unit in enumerate(units) if unit[1] == "whole"]
                order = {n: k for kind in (splits, wholes) for k, n in enumerate(kind)}
                N_SPLIT = len(splits)

                def unit_tile(n, ring=None):
                    return raw[:, n % NRAW, 0:units[n][2]]

                def landed(engine, n):
                    engine.wait_ge(raw_landed[n % NRAW], 16 * (n // NRAW + 1))

                blocks = []
                first = 0
                for n, width in enumerate(widths):
                    blocks.append((first, KD, n < 2, width))
                    first += KD
                for part in (("out",), ("up", "down"), ("up", "down")):
                    for what in part:
                        for _ in range(4 if what == "up" else 2):
                            deep = FF // 2 // P if what == "down" else KD
                            blocks.append((first, deep, what == "up", 512))
                            first += deep
                assert first == N_SPLIT
                B_IN, B_OUT = 0, 6
                B_UP, B_DOWN = (8, 14), (12, 18)
                N_IN = 6 * KD

                tile_of = [NT - 1 - v // NGR for v in range(NT * NGR)]
                att = [(v, kind, n) for v in range(NT * NGR) for kind, n in key_tiles(tile_of[v])]
                att_end = [sum(x[0] <= v for x in att) for v in range(NT * NGR)]
                LAG = 3
                begin = [0] + att_end[:-1]
                pace = (begin[-1] - 3) / (R * (NT * NGR - 1) - 1)
                maxima_after, diagonals_after = {}, {}
                for head in range(R * (NT * NGR - 1)):
                    n = int(head * pace)
                    v, r = 1 + head // R, head % R
                    maxima_after.setdefault(n, []).append((v, r))
                    if r == R - 1:
                        assert n <= begin[v] - 2
                        diagonals_after.setdefault(max(n, begin[v - 1]), []).append(v)
                N_VA = 4 + 1 + 2 * NT + 2

                @block.sync
                def _(sp):
                    def load(tile, src, slow=False):
                        params.append(sp.dma_start(tile, src, allow_slow_non_contiguous=slow).then_inc(s["params_landed"], 16))

                    params = []
                    for row, src in (
                        (R_PRE, t["ln_mix_pre"][layer].rearrange("(k p) -> k p", p=P)),
                        (R_MLP, t["ln_mlp_pre"][layer].rearrange("(k p) -> k p", p=P)),
                        (R_GN, t["gn_ssm"][layer].rearrange("(k p) -> k p", p=P)),
                        (R_GN + 2, t["gn_mlstm"][layer].rearrange("(k p) -> k p", p=P)),
                        (R_GN + 4, t["gn_nsa"][layer].rearrange("(k p) -> k p", p=P)),
                        (R_D, t["ssm_d"][layer].rearrange("(k p) -> k p", p=P)),
                        (R_CONV, t["mlstm_conv"][layer].rearrange("k (c p) -> (k c) p", p=P)),
                        (R_PEK, t["cmp_pe_k"][layer].rearrange("(j q) d -> j (q d)", q=2)),
                        (R_PEV, t["cmp_pe_v"][layer].rearrange("(j q) d -> j (q d)", q=2)),
                        (R_LR, t["ssm_lambda_re"][layer].rearrange("(j g) p -> j (g p)", g=2)),
                        (R_LI, t["ssm_lambda_im"][layer].rearrange("(j g) p -> j (g p)", g=2)),
                    ):
                        load(prow[row:row + src.shape[0], :], src)
                    load(dt8[R_DT:R_DT + NJ, :], t["ssm_log_dt"][layer].rearrange("(j g) -> j g", g=2), True)
                    load(bnat[:, 0], t["ssm_b_re"][layer].rearrange("(j g) p h -> (g p) j h", g=2))
                    load(bnat[:, 1], t["ssm_b_im"][layer].rearrange("(j g) p h -> (g p) j h", g=2))
                    load(cnat[:, 0], t["ssm_c_re"][layer].rearrange("(c g) h p -> (g h) c p", c=2))
                    load(cnat[:, 1], t["ssm_c_im"][layer].rearrange("(c g) h p -> (g h) c p", c=2))
                    load(gateb[:, 0:1], t["mlstm_b_i"][layer].unsqueeze(1), True)
                    load(gateb[:, 1:2], t["mlstm_b_f"][layer].unsqueeze(1), True)
                    load(wglu[:], t["ssm_w_glu"][layer].rearrange("(c p) n -> p c n", p=P))
                    load(w2c[:, 0], t["cmp_w2_k"][layer].rearrange("(c p) n -> p c n", p=P))
                    load(w2c[:, 1], t["cmp_w2_v"][layer].rearrange("(c p) n -> p c n", p=P))
                    load(gpost[:, 0], t["ln_mix_post"][layer].partition_broadcast(P))
                    load(gpost[:, 1], t["ln_mlp_post"][layer].partition_broadcast(P))
                    assert len(params) == N_PARAMS
                    for n, (src, kind, width) in enumerate(units):
                        if n >= NRAW:
                            before = n - NRAW
                            sp.wait_ge(s["w_lo" if units[before][1] == "split" else "whole_used"], order[before] + 1)
                        tile = unit_tile(n)
                        if kind == "whole":
                            tile = tile.rearrange("p (j c) -> p j c", j=2)
                        sp.dma_start(tile, src).then_inc(raw_landed[n % NRAW], 16)

                @block.gpsimd
                def _(pool):
                    def split_low(k):
                        pool.wait_ge(s["w_hi"], k + 1)
                        n = splits[k]
                        width = units[n][2]
                        pool.tensor_tensor(wl[:, k % NSPLIT, 0:width], unit_tile(n), wh[:, k % NSPLIT, 0:width].bitcast(F32),
                                           ALU.subtract).then_inc(s["w_lo"], 1)

                    pool.memset(qkr[:, :, 0:KCONV - 1], 0.0).then_inc(s["m_pad"], 1)
                    for k in range(N_IN):
                        split_low(k)
                    pool.wait_ge(s["s5_ypre"], 2)
                    pool.wait_ge(s["evacuated"], 6)
                    pool.memset(va[:], 1.0).then_inc(s["m_va"], 1)
                    pool.wait_ge(s["m_va"], 1)
                    for i in range(NT):
                        pool.tensor_copy(va[:, i, :, 0:HD], z[:, i, ZV:ZV + MLS].rearrange("p (h d) -> p h d", h=MH)).then_inc(
                            s["m_va"], 1)
                    pool_link = chain(pool, s["n_va"])
                    pool.wait_ge(s["n_rope"], 1)
                    for keys in (ksh, ksl, kch, kcl):
                        pool_link(pool.memset(keys[:].bitcast(F32), 0.0))
                    pool_link(pool.memset(vsw[:], 1.0))
                    for n, a in enumerate((ZVS, ZVW)):
                        for i in range(NT):
                            pool_link(pool.tensor_copy(vsw[:, n, i, :, 0:HD],
                                                       z[:, i, a:a + GW].rearrange("p (g d) -> p g d", g=NGR)))
                    pool_link(pool.memset(vca[:], 0.0))
                    pool_link(pool.memset(vca[0:NCMP, :, HD:HD + 1], 1.0))
                    def diagonals(v):
                        slot = v % 2
                        pool.wait_ge(s["n_max"], R * (v + 1))
                        if v >= 2:
                            pool.wait_ge(s["n_shifted"], att_end[v - 2])
                        for kind in (COMPRESSED, WINDOW):
                            shift = am[:, v % 4].rearrange("p (r k) -> p k r", k=3)[:, kind].unsqueeze(2)
                            pool.tensor_tensor(diag[:, slot, kind], nident[:].unsqueeze(1).to_broadcast([P, R, P]),
                                               shift.to_broadcast([P, R, P]), ALU.mult).then_inc(s["n_diag_rest"], 1)

                    def summed(v):
                        i, g = tile_of[v], v % NGR
                        to = ytok[:, i, MLS + g * R * HD:MLS + (g + 1) * R * HD].rearrange("p (r d) -> p r d", r=R)
                        pool.wait_ge(s["n_o"], v + 1)
                        pool.tensor_tensor(to, prod[:, v % 2, :, 0], prod[:, v % 2, :, 1], ALU.add).then_inc(s["n_y"], 1)
                        pool.wait_ge(s["n_y"], 2 * v + 1)
                        pool.tensor_tensor(to, to, prod[:, v % 2, :, 2], ALU.add).then_inc(s["n_y"], 1)

                    for k in range(N_IN, N_IN + NSPLIT - 1):
                        split_low(k)
                    diagonals(0)
                    for n in range(len(att) + LAG):
                        if n - LAG + 1 in att_end:
                            summed(att_end.index(n - LAG + 1))
                        for v in diagonals_after.get(n, ()):
                            diagonals(v)
                    for k in range(N_IN + NSPLIT - 1, N_SPLIT):
                        split_low(k)
                    for half in range(2):
                        for i in range(NT):
                            piece = fbuf[:, i, 512 * half:512 * half + 512]
                            pool.wait_ge(s["ssq"], 5 * NT + NT * half + i - NT + 1)
                            pool.tensor_tensor(piece, piece, gpost[:, 1, 512 * half:512 * half + 512],
                                               ALU.mult).then_inc(s["f_gain"], 1)

                @block.scalar
                def _(act):
                    link = chain(act, s["act_steps"])

                    def split_high(k):
                        n = splits[k]
                        width = units[n][2]
                        landed(act, n)
                        if k >= NSPLIT:
                            act.wait_ge(s["w_used"], k - NSPLIT + 1)
                        act.activation(wh[:, k % NSPLIT, 0:width], unit_tile(n), ACT.Copy).then_inc(s["w_hi"], 1)

                    def splits_for(block_numbers, evacuate, hooks=(), done=0):
                        start = blocks[block_numbers[0]][0]
                        end = blocks[block_numbers[-1]][0] + blocks[block_numbers[-1]][1]
                        after = {blocks[b][0] + blocks[b][1] + NSPLIT - 1: b for b in block_numbers}
                        hooks = dict(hooks)
                        for k in range(start, end):
                            if k - start >= done:
                                split_high(k)
                            if k in after:
                                evacuate(after.pop(k))
                            if k - start in hooks:
                                hooks[k - start]()
                        for k in sorted(after):
                            evacuate(after[k])

                    def product_done(engine, b):
                        engine.wait_ge(s["w_used"], blocks[b][0] + blocks[b][1])

                    squared = [0]

                    def square(src, into, squares=junk):
                        if squared[0]:
                            act.wait_ge(s["ssq"], squared[0])
                        act.activation(squares[:, 0:src.shape[-1]], src, ACT.Square, accum_out=into).then_inc(s["ssq"], 1)
                        squared[0] += 1

                    def root(n):
                        act.wait_ge(s["msq"], n + 1)
                        act.activation(stat[:, 2, :], stat[:, 1, :], ACT.Sqrt).then_inc(s["rms"], 1)

                    def mean_squares(n):
                        for i in range(NT):
                            if n:
                                act.wait_ge(s["h_new"], i + 1)
                            square(h[:, i], stat[:, 0, i:i + 1])
                        root(n)

                    def turned_high(first, gains, count0):
                        for k in range(KD):
                            act.wait_ge(s["turned"], first + k + 1)
                            act.activation(xh[:, k], ps[k][:], ACT.Identity, scale=pcol[:, gains + k:gains + k + 1]).then_inc(
                                s["x_hi"], 1)

                    def take_in(b):
                        product_done(act, b)
                        group = 4 * (b % 2)
                        last = None
                        if b == 0:
                            for n in range(2):
                                act.activation(su[:, n], ps[group + n][:], ACT.Copy)
                            for n in range(2):
                                last = act.activation(qkr[:, n, KCONV - 1:], ps[group + 2 + n][:], ACT.Copy)
                        elif b == 1:
                            for n in range(2):
                                last = act.activation(qkr[:, 2 + n, KCONV - 1:], ps[group + n][:], ACT.Copy)
                        else:
                            a = (b - 2) * 512
                            for i in range(NT):
                                last = act.activation(z[:, i, a:a + widths[b]], ps[group + i][:, 0:widths[b]], ACT.Copy)
                        last.then_inc(s["evacuated"], 1)

                    def take_half(b):
                        product_done(act, b)
                        for i in range(NT):
                            last = act.activation(fbuf[:, i, 512 * (b % 2):512 * (b % 2) + 512], ps[4 * (b % 2) + i][:], ACT.Copy)
                        last.then_inc(s["evacuated"], 1)

                    def s5_dt():
                        act.wait_ge(s["cols_ready"], 1)
                        act.activation(small[:, S_DT], pcol[:, R_DT:R_DT + NJ], ACT.Exp).then_inc(s["s5_dt"], 1)
                        act.wait_ge(s["s5_ang"], 1)
                        act.activation(small[:, S_MAG], small[:, S_X], ACT.Exp)
                        act.activation(small[:, S_SIN], small[:, S_R], ACT.Sin)
                        act.activation(small[:, S_COS], small[:, S_ABS], ACT.Sin, bias=consts[:, 0:1], scale=-1.0).then_inc(
                            s["s5_trig"], 1)

                    def s5_tables():
                        act.wait_ge(s["s5_phase"], 2)
                        act.activation(stab[:], tred[:], ACT.Sin).then_inc(s["s5_table"], 1)
                        act.activation(ctab[:], tang[:], ACT.Sin, bias=consts[:, 0:1], scale=-1.0).then_inc(s["s5_table"], 1)

                    mean_squares(0)
                    act.wait_ge(s["cols_ready"], 1)
                    turned_high(0, R_PRE, 0)
                    splits_for(range(B_IN, B_OUT), take_in, {14: s5_dt, 22: s5_tables})

                    for n in range(2):
                        act.wait_ge(s["s5_ypre"], n + 1)
                        act.activation(tmp[:, 2 + n], tmp[:, n], ACT.Gelu_apprx_tanh).then_inc(s["s5_gelu"], 1)
                    for n in range(2):
                        act.wait_ge(s["s5_glu"], n + 1)
                        act.activation(tmp[:, n], ps[6 + n][:], ACT.Sigmoid).then_inc(s["s5_sig"], 1)
                    for n in range(2):
                        act.wait_ge(s["s5_ms"], n + 1)
                        act.activation(tmp[:, n], ps[4 + n][:], ACT.Sqrt, bias=consts[:, 1:2]).then_inc(s["s5_rt"], 1)

                    for n in range(4):
                        act.wait_ge(s["m_conv"], n + 1)
                        act.activation(qk[:, n], qk[:, n], ACT.Silu).then_inc(s["m_qk"], 1)
                    act.activation(so[:], z[:, :, ZO:ZO + MLS], ACT.Sigmoid).then_inc(s["m_so"], 1)
                    act.wait_ge(s["m_fx"], 1)
                    link(act.activation(rows[:, 6], rows[:, 6], ACT.Exp, scale=-1.0))
                    act.activation(rows[:, 6], rows[:, 6], ACT.Ln, bias=1.0).then_inc(s["m_ln"], 1)
                    act.wait_ge(s["m_rows"], 1)
                    act.activation(rows[:, 5:8], rows[:, 5:8], ACT.Exp).then_inc(s["m_exp"], 1)
                    for head in range(MH):
                        act.wait_ge(s["m_arg"], head + 1)
                        act.activation(wT[:, head], wT[:, head], ACT.Exp).then_inc(s["m_w"], 1)

                    act.wait_ge(s["n_rope"], 1)
                    act.activation(gate[:], z[:, :, ZG:ZG + 3 * NH], ACT.Sigmoid).then_inc(s["n_gate"], 1)
                    for i in range(NT):
                        act.activation(qa[:, i].rearrange("p r g d -> p g r d"),
                                       z[:, i, ZQ:ZQ + NSA].rearrange("p (g r d) -> p g r d", g=NGR, r=R),
                                       ACT.Copy).then_inc(s["n_qa"], 1)
                    for r in range(R):
                        act.wait_ge(s["n_qT"], r + 1)
                        act.activation(qh[:, r], ps[r][:], ACT.Copy).then_inc(s["n_q"], 1)
                    for n in range(2):
                        act.wait_ge(s["n_kT"], n + 1)
                        act.wait_ge(s["n_va"], 4)
                        for g in range(NGR):
                            rows_ = slice(g * HD, (g + 1) * HD)
                            last = act.activation(ksh[rows_, n, g], ps[4 + n][rows_, :], ACT.Copy)
                        last.then_inc(s["n_kh"], 1)
                    for n in range(4):
                        act.wait_ge(s["whole_used"], len(wholes) // 2 * (n // 2 + 1))
                        act.activation(hg[:, n], ps[n][:, 0:NGR * NCMP], ACT.Gelu_apprx_tanh).then_inc(s["n_hid"], 1)

                    act.wait_ge(s["n_kcT"], 1)
                    act.wait_ge(s["n_va"], N_VA)
                    for g in range(NGR):
                        rows_ = slice(g * HD, (g + 1) * HD)
                        last = act.activation(kch[rows_, g, 0:NCMP], ps[4][rows_, 0:NCMP], ACT.Copy)
                    last.then_inc(s["n_kch"], 1)
                    def head_squares(v):
                        act.wait_ge(s["n_y"], 2 * (v + 1))
                        act.activation(gsq[:, tile_of[v]], ytok[:, tile_of[v]], ACT.Square).then_inc(s["g_sq"], 1)

                    for k in range(N_IN, N_IN + NSPLIT - 1):
                        split_high(k)
                    for n in range(len(att)):
                        act.wait_ge(s["n_shifted"], n + 1)
                        if n >= 4:
                            act.wait_ge(s["n_av"], n - 3)
                        act.activation(pT[:, n % 4], ps[2 + n % 4][:].rearrange("p (r q) -> p r q", r=R), ACT.Exp,
                                       scale=HD ** -0.5).then_inc(s["n_exp"], 1)
                        if n - LAG - 2 in att_end[1:-1:NGR]:
                            head_squares(att_end.index(n - LAG - 2))
                    head_squares(NT * NGR - 1)
                    act.wait_ge(s["g_ms"], 1)
                    act.activation(gst[:, 1], gst[:, 0], ACT.Sqrt).then_inc(s["g_rt"], 1)
                    for k in range(2):
                        act.activation(xh[:, k], su[:, k], ACT.Copy).then_inc(s["x_hi"], 1)
                    for k in range(2, KD):
                        act.wait_ge(s["turned"], KD + k - 1)
                        act.activation(xh[:, k], ps[k][:], ACT.Identity, scale=pcol[:, R_GN + k:R_GN + k + 1]).then_inc(
                            s["x_hi"], 1)

                    def take_out(b):
                        product_done(act, b)
                        half = b - B_OUT
                        for i in range(NT):
                            square(ps[4 * (b % 2) + i][:], stat[:, 3 * half, i:i + 1], junkz)
                        if half == 1:
                            root(1)
                            mean_squares(2)
                            turned_high(2 * KD - 2, R_MLP, 0)

                    def take_down(b):
                        half = b - B_DOWN[1]
                        for i in range(NT):
                            act.wait_ge(s["f_sum"], NT * half + i + 1)
                            square(fbuf[:, i, 512 * half:512 * half + 512], stat[:, 3 * half, i:i + 1])
                        if half == 1:
                            root(3)

                    def take_up(part):
                        def take(b):
                            product_done(act, b)
                            for n in range(4):
                                f = 4 * (b - B_UP[part]) + n
                                g = 16 * part + f
                                if g >= 2:
                                    act.wait_ge(s["f_sq"], g - 1)
                                act.activation(act_t[:, g % 2], ps[4 * (b % 2) + n][:], ACT.Relu).then_inc(s["f_relu"], 1)
                                if g >= 1 and f >= 1:
                                    high(g - 1)
                            if b == B_UP[part] + 3:
                                high(16 * part + 15)
                        return take

                    def high(g):
                        act.wait_ge(s["f_sq"], g + 1)
                        if g == 16:
                            product_done(act, B_DOWN[0] + 1)
                        act.activation(fh[:, g % 16], sq_t[:, g % 2], ACT.Copy).then_inc(s["f_hi"], 1)

                    def take(b):
                        if b < B_UP[0]:
                            take_out(b)
                        elif b < B_DOWN[0]:
                            take_up(0)(b)
                        elif b < B_UP[1]:
                            take_half(b)
                        elif b < B_DOWN[1]:
                            take_up(1)(b)
                        else:
                            take_down(b)

                    splits_for(range(B_OUT, len(blocks)), take, done=NSPLIT - 1)

                @block.vector
                def _(dve):
                    link = chain(dve, s["dve_steps"])

                    def tt(out_, a, b, op):
                        return dve.tensor_tensor(out_, a, b, op)

                    SQUARES = (NT, 3 * NT, 4 * NT, 6 * NT)

                    def root_mean(n):
                        dve.wait_ge(s["ssq"], SQUARES[n])
                        if n % 2:
                            link(tt(stat[:, 0, :], stat[:, 0, :], stat[:, 3, :], ALU.add))
                        dve.tensor_scalar(stat[:, 1, :], stat[:, 0, :], 1.0 / D, EPS, ALU.mult, ALU.add).then_inc(s["msq"], 1)
                        dve.wait_ge(s["rms"], n + 1)
                        link(dve.reciprocal(stat[:, 1, :], stat[:, 2, :]))

                    def pre_norm(n):
                        root_mean(n)
                        for i in range(NT):
                            dve.tensor_scalar(fbuf[:, i], h[:, i], stat[:, 1, i:i + 1], None, ALU.mult).then_inc(s["normed"], 1)

                    def turned_low(first, gains):
                        for k in range(KD):
                            dve.wait_ge(s["x_hi"], first + k + 1)
                            dve.scalar_tensor_tensor(xl[:, k], ps[k][:], pcol[:, gains + k:gains + k + 1], xh[:, k].bitcast(F32),
                                                     ALU.mult, ALU.subtract).then_inc(s["x_lo"], 1)

                    def post_norm(n, which):
                        root_mean(n)
                        for i in range(NT):
                            if which:
                                dve.wait_ge(s["f_gain"], NT + i + 1)
                            dve.scalar_tensor_tensor(h[:, i], fbuf[:, i], stat[:, 1, i:i + 1], h[:, i], ALU.mult,
                                                     ALU.add).then_inc(s["h_new"], 1)

                    def sm_(n):
                        return small[:, n]

                    dve.wait_ge(s["params_landed"], 16 * N_PARAMS)
                    dve.tensor_copy(prow[R_DT:R_DT + NJ, :].rearrange("j (g p) -> j g p", g=2),
                                    dt8[R_DT:R_DT + NJ, :].unsqueeze(2).to_broadcast([NJ, 2, NP_])).then_inc(s["cols_turned"], 1)
                    pre_norm(0)
                    dve.wait_ge(s["cols_turned"], 2)
                    dve.tensor_copy(pcol[:], ps[7][:, 0:NROW]).then_inc(s["cols_ready"], 1)
                    dve.wait_ge(s["cols_ready"], 1)
                    turned_low(0, R_PRE)

                    lr, li = pcol[:, R_LR:R_LR + NJ], pcol[:, R_LI:R_LI + NJ]
                    dve.wait_ge(s["s5_dt"], 1)
                    link(tt(sm_(S_X), lr, sm_(S_DT), ALU.mult))
                    link(tt(sm_(S_TH), li, sm_(S_DT), ALU.mult))
                    reduce_angle(dve, link, sm_(S_R), sm_(S_TH), sm_(S_T0))
                    absolute(dve, sm_(S_ABS), sm_(S_R)).then_inc(s["s5_ang"], 1)
                    link(dve.tensor_scalar(sm_(S_RHI), sm_(S_R), ROUND13, None, ALU.add))
                    link(dve.tensor_scalar(sm_(S_RHI), sm_(S_RHI), ROUND13, None, ALU.subtract))
                    link(tt(sm_(S_RLO), sm_(S_R), sm_(S_RHI), ALU.subtract))
                    table = [P, NJ, L + 1]
                    stepb = steps[:].unsqueeze(1).to_broadcast(table)
                    link(tt(tang[:], sm_(S_RHI).unsqueeze(2).to_broadcast(table), stepb, ALU.mult))
                    reduce_angle(dve, link, tred[:], tang[:], tnum[:])
                    link(tt(tang[:], sm_(S_RLO).unsqueeze(2).to_broadcast(table), stepb, ALU.mult))
                    link(tt(tred[:], tred[:], tang[:], ALU.add))
                    dve.tensor_scalar(tred[:], tred[:], PI_IN, -PI_IN, ALU.min, ALU.max).then_inc(s["s5_phase"], 1)
                    dve.wait_ge(s["s5_phase"], 1)
                    absolute(dve, tang[:], tred[:]).then_inc(s["s5_phase"], 1)
                    dve.wait_ge(s["s5_trig"], 1)
                    link(tt(sm_(S_ARE), sm_(S_MAG), sm_(S_COS), ALU.mult))
                    link(tt(sm_(S_AIM), sm_(S_MAG), sm_(S_SIN), ALU.mult))
                    link(tt(sm_(S_T0), lr, lr, ALU.mult))
                    link(tt(sm_(S_T1), li, li, ALU.mult))
                    link(tt(sm_(S_DEN), sm_(S_T0), sm_(S_T1), ALU.add))
                    link(dve.reciprocal(sm_(S_RDEN), sm_(S_DEN)))
                    link(dve.tensor_scalar(sm_(S_E), sm_(S_ARE), 1.0, None, ALU.subtract))
                    for out_, (a, b), op in ((S_GRE, (lr, li), ALU.add), (S_GIM, (li, lr), ALU.subtract)):
                        link(tt(sm_(S_T0), sm_(S_E), a, ALU.mult))
                        link(tt(sm_(S_T1), sm_(S_AIM), b, ALU.mult))
                        link(tt(sm_(S_T0), sm_(S_T0), sm_(S_T1), op))
                        link(tt(sm_(out_), sm_(S_T0), sm_(S_RDEN), ALU.mult))
                    link(dve.memset(bd[:], 0.0))
                    wide = [P, NJ, GH]
                    gre, gim = (sm_(n).unsqueeze(2).to_broadcast(wide) for n in (S_GRE, S_GIM))
                    t0 = tmp[:, 0, 0:NJ * GH].rearrange("p (j c) -> p j c", j=NJ)
                    t1 = tmp[:, 1, 0:NJ * GH].rearrange("p (j c) -> p j c", j=NJ)
                    for part, (a, b), op in ((0, (0, 1), ALU.add), (1, (1, 0), ALU.subtract)):
                        link(tt(t0, gre, bnat[:, a], ALU.mult))
                        link(tt(t1, gim, bnat[:, b], ALU.mult))
                        for g in range(2):
                            rows_ = slice(g * NP_, (g + 1) * NP_)
                            link(tt(bd[rows_, part, :, g * GH:(g + 1) * GH], t0[rows_], t1[rows_], op))
                    for part in range(2):
                        for c in range(2):
                            for g in range(2):
                                mine = par[:, 2 * part + g:2 * part + g + 1]
                                last = dve.tensor_scalar(cb[:, part, c, g * NP_:(g + 1) * NP_], cnat[:, part, c], mine, None,
                                                         ALU.mult)
                                if (part, c, g) != (1, 1, 1):
                                    link(last)
                    last.then_inc(s["s5_nat"], 1)
                    dve.wait_ge(s["s5_natT"], 2)
                    link(dve.tensor_copy(bT[:], ps[0][:].rearrange("p (n c) -> p n c", n=4)))
                    dve.tensor_copy(cT[:], ps[1][:].rearrange("p (a b c) -> p a b c", a=2, b=2)).then_inc(s["s5_mats"], 1)

                    dve.wait_ge(s["s5_table"], 2)
                    chunked = [P, NT, L]

                    def by_chunk(ap):
                        return ap.rearrange("p (c l) -> p c l", c=NT)

                    def cos_sin(j):
                        return (ctab[:, j, 0:L].unsqueeze(1).to_broadcast(chunked),
                                stab[:, j, 0:L].unsqueeze(1).to_broadcast(chunked))

                    for j in range(NJ):
                        cos_, sin_ = cos_sin(j)
                        dve.wait_ge(s["s5_bu"], j + 1)
                        re_, im_ = by_chunk(ps[2 * (j % 2)][:]), by_chunk(ps[2 * (j % 2) + 1][:])
                        tt(by_chunk(tmp[:, 0]), re_, cos_, ALU.mult)
                        tt(by_chunk(tmp[:, 1]), im_, sin_, ALU.mult)
                        tt(by_chunk(tmp[:, 2]), im_, cos_, ALU.mult)
                        tt(by_chunk(tmp[:, 3]), re_, sin_, ALU.mult).then_inc(s["s5_rot"], 1)
                        dve.wait_ge(s["s5_rot"], j + 1)
                        tt(vr[:, j], tmp[:, 0], tmp[:, 1], ALU.add)
                        link(tt(vi[:, j], tmp[:, 2], tmp[:, 3], ALU.subtract))
                    last_cos, last_sin = ctab[:, :, L], stab[:, :, L]
                    for c in range(NT):
                        for j in range(NJ):
                            decay = sm_(S_MAG)[:, j:j + 1].to_broadcast([P, L])
                            for v, start in ((vr, S_IRE), (vi, S_IIM)):
                                part = v[:, j, c * L:(c + 1) * L]
                                last = dve.tensor_tensor_scan(part, decay, part,
                                                              sm_(start)[:, j:j + 1] if c else 0.0, ALU.mult, ALU.add)
                        link(last)
                        if c < NT - 1:
                            er, ei = vr[:, :, (c + 1) * L - 1], vi[:, :, (c + 1) * L - 1]
                            tt(sm_(S_T0), last_cos, er, ALU.mult)
                            tt(sm_(S_T1), last_sin, ei, ALU.mult)
                            tt(sm_(S_T2), last_cos, ei, ALU.mult)
                            link(tt(sm_(S_T3), last_sin, er, ALU.mult))
                            tt(sm_(S_IRE), sm_(S_T0), sm_(S_T1), ALU.subtract)
                            link(tt(sm_(S_IIM), sm_(S_T2), sm_(S_T3), ALU.add))
                    for j in range(NJ):
                        cos_, sin_ = cos_sin(j)
                        re_, im_ = by_chunk(vr[:, j]), by_chunk(vi[:, j])
                        tt(by_chunk(tmp[:, 0]), re_, cos_, ALU.mult)
                        tt(by_chunk(tmp[:, 1]), im_, sin_, ALU.mult)
                        tt(by_chunk(tmp[:, 2]), im_, cos_, ALU.mult)
                        link(tt(by_chunk(tmp[:, 3]), re_, sin_, ALU.mult))
                        link(tt(vr[:, j], tmp[:, 0], tmp[:, 1], ALU.subtract))
                        tt(vi[:, j], tmp[:, 2], tmp[:, 3], ALU.add).then_inc(s["s5_x"], 1)
                        dve.wait_ge(s["s5_x"], j + 1)
                    dve.wait_ge(s["s5_x"], NJ)
                    for n in range(2):
                        dve.wait_ge(s["s5_y"], n + 1)
                        dve.scalar_tensor_tensor(tmp[:, n], su[:, n], pcol[:, R_D + n:R_D + n + 1], ps[4 + n][:], ALU.mult,
                                                 ALU.add).then_inc(s["s5_ypre"], 1)
                    for n in range(2):
                        dve.wait_ge(s["s5_sig"], n + 1)
                        link(tt(su[:, n], tmp[:, 2 + n], tmp[:, n], ALU.mult))
                        tt(tmp[:, n], su[:, n], su[:, n], ALU.mult).then_inc(s["s5_sq"], 1)
                    for n in range(2):
                        dve.wait_ge(s["s5_rt"], n + 1)
                        link(dve.reciprocal(tmp[:, 2 + n], tmp[:, n]))
                        link(dve.scalar_tensor_tensor(su[:, n], su[:, n], pcol[:, R_GN + n:R_GN + n + 1], tmp[:, 2 + n],
                                                      ALU.mult, ALU.mult))

                    dve.wait_ge(s["m_pad"], 1)
                    for n in range(4):
                        tap = lambda k: pcol[:, R_CONV + 4 * k + n:R_CONV + 4 * k + n + 1]
                        link(dve.tensor_scalar(qk[:, n], qkr[:, n, 0:T], tap(0), None, ALU.mult))
                        for k in range(1, KCONV):
                            last = dve.scalar_tensor_tensor(qk[:, n], qkr[:, n, k:k + T], tap(k), qk[:, n], ALU.mult, ALU.add)
                            if k < KCONV - 1:
                                link(last)
                        last.then_inc(s["m_conv"], 1)
                    dve.wait_ge(s["m_gateT"], 1)
                    link(dve.tensor_scalar(rows[:, 0], ps[0][0:MH, :], gateb[:, 0:1], None, ALU.add))
                    link(dve.tensor_scalar(rows[:, 5], ps[1][0:MH, :], gateb[:, 1:2], None, ALU.add))
                    absolute(dve, rows[:, 6], rows[:, 5]).then_inc(s["m_fx"], 1)
                    dve.wait_ge(s["m_ln"], 1)
                    link(dve.scalar_tensor_tensor(rows[:, 1], rows[:, 5], 0.0, rows[:, 6], ALU.min, ALU.subtract))
                    dve.tensor_tensor_scan(rows[:, 2], keep[:], rows[:, 1], 0.0, ALU.mult, ALU.add)
                    link(dve.tensor_tensor_scan(rows[:, 3], rows[:, 1], rows[:, 0], 0.0, ALU.add, ALU.max))
                    tt(rows[:, 4], rows[:, 2], rows[:, 3], ALU.subtract)
                    tt(rows[:, 0], rows[:, 0], rows[:, 2], ALU.subtract)
                    dve.memset(msr[:, 0:1], 0.0)
                    link(dve.tensor_copy(msr[:, 1:NT], rows[:, 3, L - 1:T - 1:L]))
                    crow = [MH, NT, L]
                    tt(by_chunk(rows[:, 5]), by_chunk(rows[:, 4]), msr[:].unsqueeze(2).to_broadcast(crow), ALU.add)
                    tt(by_chunk(rows[:, 6]), by_chunk(rows[:, 0]),
                       by_chunk(rows[:, 4])[:, :, L - 1:L].to_broadcast(crow), ALU.add)
                    dve.tensor_scalar(rows[:, 7], rows[:, 3], -1.0, None, ALU.mult).then_inc(s["m_rows"], 1)
                    dve.wait_ge(s["m_colT"], 1)
                    dve.tensor_copy(dec[:], ps[3][:, 0:2 * NT].rearrange("p (a c) -> p a c", a=2))
                    link(dve.tensor_copy(colt[:], ps[2][:, 0:4 * NT * MH].rearrange("p (a c n) -> p a c n", a=4, c=NT)))
                    dve.tensor_scalar(colt[:, 2], colt[:, 2], HD ** -0.5, None, ALU.mult).then_inc(s["m_cols"], 1)
                    dve.wait_ge(s["m_cols"], 1)
                    for head in range(MH):
                        dve.wait_ge(s["m_bc"], head + 1)
                        for c in range(NT):
                            span = slice(c * L, (c + 1) * L)
                            last = dve.scalar_tensor_tensor(wT[:, head, span], ps[4 + head][:, span],
                                                            colt[:, 0, c, head:head + 1], maskT[:], ALU.add, ALU.add)
                        last.then_inc(s["m_arg"], 1)
                    for n in range(2):
                        dve.wait_ge(s["m_kT"], n + 1)
                        tt(kw[:, :, 2 * n:2 * n + 2], ps[n][:].rearrange("p (c a d) -> p c a d", c=NT, a=2),
                           colt[:, 2, :, 2 * n:2 * n + 2].unsqueeze(3).to_broadcast([P, NT, 2, HD]), ALU.mult).then_inc(s["m_kw"], 1)
                    for head in range(MH):
                        dve.wait_ge(s["m_s"], head + 1)
                        dve.wait_ge(s["m_w"], head + 1)
                        dve.scalar_tensor_tensor(wT[:, head], ps[4 + head][:], HD ** -0.5, wT[:, head], ALU.mult,
                                                 ALU.mult).then_inc(s["m_p"], 1)
                    W1 = HD + 1
                    for c in range(NT):
                        dve.wait_ge(s["m_chunk"], c + 1)
                        if c == 0:
                            dve.tensor_copy(cst[:], ps[2][:, 0:2 * W1].rearrange("p (a d) -> p a d", a=2)).then_inc(s["m_state"], 1)
                            dve.tensor_copy(nu[:, 0], ps[0][:, 0:MH * W1].rearrange("p (n d) -> p n d", n=MH)).then_inc(s["m_nu"], 1)
                            continue
                        if c < NT - 1:
                            dve.wait_ge(s["m_state"], 2 * c - 1)
                            for a in range(2):
                                dve.scalar_tensor_tensor(cst[:, a], cst[:, a], dec[:, a, c:c + 1], ps[2][:, a * W1:(a + 1) * W1],
                                                         ALU.mult, ALU.add).then_inc(s["m_state"], 1)
                        for odd in range(2):
                            link(tt(mtmp[:, odd::2], ps[1 + 2 * odd][:, 0:2 * W1].rearrange("p (n d) -> p n d", n=2),
                                    colt[:, 1, c, odd::2].unsqueeze(2).to_broadcast([P, 2, W1]), ALU.mult))
                        tt(nu[:, c], mtmp[:], ps[0][:, 0:MH * W1].rearrange("p (n d) -> p n d", n=MH), ALU.add).then_inc(
                            s["m_nu"], 1)
                    dve.wait_ge(s["m_nu"], NT)
                    link(absolute(dve, mden[:, 0], nu[:, :, :, HD]))
                    link(tt(mden[:, 0], mden[:, 0], colt[:, 3], ALU.max))
                    link(dve.reciprocal(mden[:, 1], mden[:, 0]))
                    dve.wait_ge(s["m_so"], 1)
                    for i in range(NT):
                        yt = ytok[:, i, 0:MLS].rearrange("p (n d) -> p n d", n=MH)
                        link(tt(yt, nu[:, i, :, 0:HD], mden[:, 1, i].unsqueeze(2).to_broadcast([P, MH, HD]), ALU.mult))
                    for i in range(NT):
                        last = tt(ytok[:, i, 0:MLS], ytok[:, i, 0:MLS], so[:, i], ALU.mult)
                    link(last)

                    def rope(x, heads):
                        shape = [P, NT, heads, ROT]
                        size = NT * heads * ROT
                        ts = [rtmp[:, n, 0:size].rearrange("p (i a c) -> p i a c", i=NT, a=heads) for n in range(4)]
                        cos_, sin_ = (v[:].unsqueeze(2).to_broadcast(shape) for v in (cosr, sinr))
                        x1, x2 = x[:, :, :, 0:ROT], x[:, :, :, ROT:2 * ROT]
                        tt(ts[0], x1, cos_, ALU.mult)
                        tt(ts[1], x2, sin_, ALU.mult)
                        tt(ts[2], x2, cos_, ALU.mult)
                        link(tt(ts[3], x1, sin_, ALU.mult))
                        tt(x1, ts[0], ts[1], ALU.subtract)
                        return tt(x2, ts[2], ts[3], ALU.add)

                    link(rope(z[:, :, ZQ:ZQ + NSA].rearrange("p i (a d) -> p i a d", d=HD), NH))
                    for a in (ZKC, ZKS, ZKW):
                        last = rope(z[:, :, a:a + GW].rearrange("p i (a d) -> p i a d", d=HD), NGR)
                        if a != ZKW:
                            link(last)
                    last.then_inc(s["n_rope"], 1)
                    for r in range(R):
                        dve.wait_ge(s["n_q"], r + 1)
                        tt(ql[:, r], ps[r][:], qh[:, r].bitcast(F32), ALU.subtract).then_inc(s["n_ql"], 1)
                    for n in range(2):
                        dve.wait_ge(s["n_kh"], n + 1)
                        for g in range(NGR):
                            rows_ = slice(g * HD, (g + 1) * HD)
                            last = tt(ksl[rows_, n, g], ps[4 + n][rows_, :], ksh[rows_, n, g].bitcast(F32), ALU.subtract)
                        last.then_inc(s["n_k"], 1)
                    for kv, pe_row in ((0, R_PEK), (1, R_PEV)):
                        dve.wait_ge(s["n_kT"], 3 + kv)
                        for g in range(NGR):
                            src = ps[6 + kv][g * HD:(g + 1) * HD, :].rearrange("p (m q) -> p q m", q=CS_)
                            for q in range(2):
                                to = slice(q * HD, (q + 1) * HD)
                                for half in range(2):
                                    js = slice(half * 8, half * 8 + 8)
                                    last = tt(flat[to, kv, js, g, :], src[:, q::2, half:half + NCMP],
                                              pcol[to, pe_row + half * 8:pe_row + half * 8 + 8].unsqueeze(2).to_broadcast(
                                                  [HD, 8, NCMP]), ALU.add)
                        last.then_inc(s["n_flat"], 1)
                    dve.wait_ge(s["n_kch"], 1)
                    for g in range(NGR):
                        rows_ = slice(g * HD, (g + 1) * HD)
                        tt(kcl[rows_, g, 0:NCMP], ps[4][rows_, 0:NCMP], kch[rows_, g, 0:NCMP].bitcast(F32), ALU.subtract)
                    dve.tensor_copy(vca[0:NCMP, :, 0:HD], ps[5][0:NCMP, 0:GW].rearrange(
                        "p (g d) -> p g d", g=NGR)).then_inc(s["n_kc"], 1)
                    dve.wait_ge(s["n_gate"], 1)

                    def maxima(v, r):
                        i, slot = tile_of[v], v % 4
                        width = (i + 1) * P
                        if v >= 4 and r == 0:
                            dve.wait_ge(s["n_diag_rest"], 2 * (v - 3))
                            dve.wait_ge(s["n_diag"], v - 3)
                        n_win = min(i + 1, WIN // P + 1)
                        dve.wait_ge(s["n_score"], R * v + r + 1)
                        for kind, scores_, msk in (
                            (COMPRESSED, ps[1][:, 384:384 + NCMP], cmask[:, i, 0:NCMP]),
                            (WINDOW, ps[1][:, 0:n_win * P], wmask[:, 384 - n_win * P:384]),
                            (SELECTED, ps[0][:, 0:width], mask[:, 512 - width:512]),
                        ):
                            last = dve.tensor_tensor_reduce(scores_, scores_, msk, 1.0, 3 * NEG,
                                                            ALU.add, ALU.max, am[:, slot, 3 * r + kind:3 * r + kind + 1])
                        last.then_inc(s["n_max"], 1)

                    def diagonals(v):
                        slot = v % 2
                        if v >= 2:
                            dve.wait_ge(s["n_shifted"], att_end[v - 2])
                        dve.wait_ge(s["n_max"], R * (v + 1))
                        shift = am[:, v % 4].rearrange("p (r k) -> p k r", k=3)[:, SELECTED].unsqueeze(2)
                        tt(diag[:, slot, SELECTED], nident[:].unsqueeze(1).to_broadcast([P, R, P]),
                           shift.to_broadcast([P, R, P]), ALU.mult).then_inc(s["n_diag"], 1)

                    def gated(v):
                        i, g, slot = tile_of[v], v % NGR, v % 2
                        dve.wait_ge(s["n_av"], att_end[v])
                        if v >= 2:
                            dve.wait_ge(s["n_y"], 2 * (v - 1))
                        o = [ps[6 + n][:, 0:6 * (HD + 1)].rearrange("p (k d) -> p k d", d=HD + 1) for n in range(2)]
                        for n in range(2):
                            last = dve.reciprocal(cf[:, slot, 6 * n:6 * n + 6], o[n][:, :, HD])
                        link(last)
                        link(tt(cf[:, slot], cf[:, slot], gate[:, i, 3 * R * g:3 * R * (g + 1)], ALU.mult))
                        if i == 0:
                            for r in range(R):
                                one = cf[:, slot, 3 * r + COMPRESSED:3 * r + COMPRESSED + 1]
                                last = tt(one, one, cvalid[:], ALU.mult)
                            link(last)
                        for n in range(2):
                            last = tt(prod[:, slot, 2 * n:2 * n + 2].rearrange("p r k d -> p (r k) d"), o[n][:, :, 0:HD],
                                      cf[:, slot, 6 * n:6 * n + 6].unsqueeze(2).to_broadcast([P, 6, HD]), ALU.mult)
                        last.then_inc(s["n_o"], 1)

                    for r in range(R):
                        maxima(0, r)
                    diagonals(0)
                    for n in range(len(att) + LAG):
                        if n - LAG + 1 in att_end:
                            gated(att_end.index(n - LAG + 1))
                        for v, r in maxima_after.get(n, ()):
                            maxima(v, r)
                        for v in diagonals_after.get(n, ()):
                            diagonals(v)

                    heads = MH + NH
                    for n, i in enumerate(tile_of[::NGR]):
                        dve.wait_ge(s["g_sq"], n + 1)
                        last = dve.tensor_reduce(gst[:, 2, i], gsq[:, i].rearrange("p (n d) -> p n d", d=HD), AX, ALU.add)
                    link(last)
                    dve.tensor_scalar(gst[:, 0], gst[:, 2], 1.0 / HD, EPS, ALU.mult, ALU.add).then_inc(s["g_ms"], 1)
                    dve.wait_ge(s["g_rt"], 1)
                    link(dve.reciprocal(gst[:, 2], gst[:, 1]))
                    for i in tile_of[::NGR]:
                        yt = ytok[:, i].rearrange("p (n d) -> p n d", d=HD)
                        tt(yt, yt, gst[:, 2, i].unsqueeze(2).to_broadcast([P, heads, HD]), ALU.mult).then_inc(s["g_y"], 1)
                    for k in range(2):
                        dve.wait_ge(s["x_hi"], KD + k + 1)
                        tt(xl[:, k], su[:, k], xh[:, k].bitcast(F32), ALU.subtract).then_inc(s["x_lo"], 1)
                    for k in range(2, KD):
                        dve.wait_ge(s["x_hi"], KD + k + 1)
                        dve.scalar_tensor_tensor(xl[:, k], ps[k][:], pcol[:, R_GN + k:R_GN + k + 1], xh[:, k].bitcast(F32),
                                                 ALU.mult, ALU.subtract).then_inc(s["x_lo"], 1)

                    for half in range(2):
                        b = B_OUT + half
                        for i in range(NT):
                            dve.wait_ge(s["ssq"], NT * (1 + half) + i + 1)
                            cols = slice(512 * half, 512 * half + 512)
                            last = tt(fbuf[:, i, cols], ps[4 * (b % 2) + i][:], gpost[:, 0, cols], ALU.mult)
                    link(last)
                    post_norm(1, 0)
                    dve.wait_ge(s["h_new"], NT)
                    pre_norm(2)
                    turned_low(2 * KD, R_MLP)
                    for part in range(2):
                        for g in range(16 * part, 16 * part + 16):
                            b, n = B_UP[part] + g % 16 // 4, g % 4
                            dve.wait_ge(s["f_relu"], g + 1)
                            if g >= 2:
                                dve.wait_ge(s["f_lo"], g - 1)
                            dve.scalar_tensor_tensor(sq_t[:, g % 2], ps[4 * (b % 2) + n][:], 0.0, act_t[:, g % 2], ALU.max,
                                                     ALU.mult).then_inc(s["f_sq"], 1)
                            if g % 16:
                                low(dve, g - 1, fl, fh, sq_t, s)
                        low(dve, 16 * part + 15, fl, fh, sq_t, s)
                    for half in range(2):
                        b = B_DOWN[1] + half
                        dve.wait_ge(s["w_used"], blocks[b][0] + blocks[b][1])
                        for i in range(NT):
                            into = fbuf[:, i, 512 * half:512 * half + 512]
                            tt(into, into, ps[4 * (b % 2) + i][:], ALU.add).then_inc(s["f_sum"], 1)
                    post_norm(3, 1)

                @block.tensor
                def _(pe):
                    def product(b, inputs=None):
                        first, deep, on_features, width = blocks[b]
                        group = 4 * (b % 2)
                        hi, lo = (fh, fl) if b in (B_DOWN[0], B_DOWN[0] + 1, B_DOWN[1], B_DOWN[1] + 1) else (xh, xl)
                        for k in range(deep):
                            unit = first + k
                            slot = unit % NSPLIT
                            pe.wait_ge(s["w_lo"], unit + 1)
                            if inputs:
                                pe.wait_ge(s[inputs[0]], inputs[1] + max(k + 1, inputs[2]))
                            if on_features:
                                for n in range(width // P):
                                    cols = slice(n * P, (n + 1) * P)
                                    for m, (w, x) in enumerate(((wh, hi), (wh, lo), (wl, hi))):
                                        last = pe.matmul(ps[group + n][:], w[:, slot, cols], x[:, k], start=k == 0 and m == 0,
                                                         stop=k == deep - 1 and m == 2)
                            else:
                                for i in range(NT):
                                    rows_ = slice(i * P, (i + 1) * P)
                                    for m, (x, w) in enumerate(((hi, wh), (hi, wl), (lo, wh))):
                                        last = pe.matmul(ps[group + i][:, 0:width], x[:, k, rows_], w[:, slot, 0:width],
                                                         start=k == 0 and m == 0, stop=k == deep - 1 and m == 2)
                            last.then_inc(s["w_used"], 1)

                    def turn(src, bank, count, ready, before, order=range(NT)):
                        for n, i in enumerate(order):
                            pe.wait_ge(s[ready], before + n + 1)
                            for k in range(count):
                                last = pe.transpose(ps[bank + k][:, i * P:(i + 1) * P], src[:, i, k * P:(k + 1) * P], ident[:])
                                if n == NT - 1:
                                    last.then_inc(s["turned"], 1)

                    pe.wait_ge(s["cols_turned"], 1)
                    pe.transpose(ps[7][:, 0:NROW], prow[:], ident[0:NROW, 0:NROW]).then_inc(s["cols_turned"], 1)
                    pe.wait_ge(s["cols_ready"], 1)
                    turn(fbuf, 0, KD, "normed", 0)
                    for b in range(B_OUT):
                        if b >= 2:
                            pe.wait_ge(s["evacuated"], b - 1)
                        product(b, ("x_lo", 0, 4) if b == 0 else None)

                    pe.wait_ge(s["evacuated"], B_OUT)
                    pe.wait_ge(s["s5_nat"], 1)
                    for n in range(4):
                        last = pe.transpose(ps[0][:, n * P:(n + 1) * P],
                                            bd[:, n // 2, 4 * (n % 2):4 * (n % 2) + 4].rearrange("p j c -> p (j c)"), ident[:])
                    last.then_inc(s["s5_natT"], 1)
                    for n in range(4):
                        last = pe.transpose(ps[1][:, n * P:(n + 1) * P], cb[:, n // 2, n % 2], ident[:])
                    last.then_inc(s["s5_natT"], 1)
                    pe.wait_ge(s["s5_mats"], 1)
                    for j in range(NJ):
                        if j >= 2:
                            pe.wait_ge(s["s5_rot"], j - 1)
                        rows_ = slice(32 * (j % 4), 32 * (j % 4) + 32)
                        for part in range(2):
                            last = pe.matmul(ps[2 * (j % 2) + part][:], bT[rows_, 2 * part + j // 4], su[rows_, j // 4],
                                             start=True, stop=True)
                        last.then_inc(s["s5_bu"], 1)
                    for n in range(2):
                        for q in range(4):
                            rows_ = slice(32 * q, 32 * q + 32)
                            pe.wait_ge(s["s5_x"], 4 * n + q + 1)
                            for part, v in enumerate((vr, vi)):
                                last = pe.matmul(ps[4 + n][rows_, :], cT[:, part, n, rows_], v[:, 4 * n + q], start=part == 0,
                                                 stop=part == 1)
                        last.then_inc(s["s5_y"], 1)
                    pe.wait_ge(s["s5_gelu"], 2)
                    for m in range(2):
                        for c in range(2):
                            last = pe.matmul(ps[6 + m][:], wglu[:, c, m * P:(m + 1) * P], tmp[:, 2 + c], start=c == 0, stop=c == 1)
                        last.then_inc(s["s5_glu"], 1)
                    for m in range(2):
                        pe.wait_ge(s["s5_sq"], m + 1)
                        pe.matmul(ps[4 + m][:], bones[:], tmp[:, m], start=True, stop=True).then_inc(s["s5_ms"], 1)

                    for n, a in enumerate((ZI, ZFG)):
                        for i in range(NT):
                            last = pe.transpose(ps[n][0:MH, i * P:(i + 1) * P], z[:, i, a:a + MH], ident[:])
                    last.then_inc(s["m_gateT"], 1)
                    pe.wait_ge(s["m_exp"], 1)
                    for a, row in enumerate((0, 5, 6, 7)):
                        for c in range(NT):
                            col = (a * NT + c) * MH
                            pe.transpose(ps[2][:, col:col + MH], rows[:, row, c * L:(c + 1) * L], ident[0:MH, 0:MH])
                    for a in range(2):
                        last = pe.matmul(ps[3][:, a * NT:(a + 1) * NT], sel2[:, a], rows[:, 5, L - 1:T:L], start=True, stop=True)
                    last.then_inc(s["m_colT"], 1)
                    pe.wait_ge(s["s5_rt"], 2)
                    for head in range(MH):
                        pe.matmul(ps[4 + head][:], sel[:, head], rows[:, 4], start=True, stop=True).then_inc(s["m_bc"], 1)
                    pe.wait_ge(s["m_qk"], 4)
                    for n in range(2):
                        for c in range(NT):
                            last = pe.transpose(ps[n][:, c * L:(c + 1) * L], qk[:, 2 + n, c * L:(c + 1) * L], ident[:])
                        last.then_inc(s["m_kT"], 1)
                    for head in range(MH):
                        pe.wait_ge(s["m_arg"], head + 1)
                        rows_ = slice(HD * (head % 2), HD * (head % 2) + HD)
                        for c in range(NT):
                            span = slice(c * L, (c + 1) * L)
                            last = pe.matmul(ps[4 + head][:, span], qk[rows_, 2 + head // 2, span], qk[rows_, head // 2, span],
                                             start=True, stop=True)
                        last.then_inc(s["m_s"], 1)
                    W1 = HD + 1
                    pe.wait_ge(s["m_kw"], 2)
                    pe.wait_ge(s["m_va"], 1 + NT)
                    pe.wait_ge(s["m_cols"], 1)
                    for c in range(NT):
                        span = slice(c * L, (c + 1) * L)
                        if c:
                            pe.wait_ge(s["m_nu"], c)
                            pe.wait_ge(s["m_state"], 2 * c - 1)
                        for head in range(MH):
                            if c == 0:
                                pe.wait_ge(s["m_p"], head + 1)
                            rows_ = slice(HD * (head % 2), HD * (head % 2) + HD)
                            cols = slice(head * W1, (head + 1) * W1)
                            last = pe.matmul(ps[0][:, cols], wT[:, head, span], va[:, c, head], start=True, stop=True)
                            if c:
                                cols = slice(head // 2 * W1, (head // 2 + 1) * W1)
                                last = pe.matmul(ps[1 + 2 * (head % 2)][:, cols], qk[rows_, head // 2, span],
                                                 cst[rows_, head // 2], start=True, stop=True)
                            if c < NT - 1:
                                a = head // 2
                                last = pe.matmul(ps[2][rows_, a * W1:(a + 1) * W1], kw[:, c, head], va[:, c, head], start=True,
                                                 stop=True)
                        last.then_inc(s["m_chunk"], 1)

                    pe.wait_ge(s["n_rope"], 1)
                    for r in range(R):
                        for i in range(NT):
                            if r == 0:
                                pe.wait_ge(s["n_qa"], i + 1)
                            last = pe.transpose(ps[r][:, i * P:(i + 1) * P], qa[:, i, r].rearrange("p g d -> p (g d)"), ident[:])
                        last.then_inc(s["n_qT"], 1)
                    for n, a in enumerate((ZKS, ZKW, ZKC, ZVC)):
                        for i in range(NT):
                            last = pe.transpose(ps[4 + n][:, i * P:(i + 1) * P], z[:, i, a:a + GW], ident[:])
                        last.then_inc(s["n_kT"], 1)
                    for k, n in enumerate(wholes):
                        kv, j0 = k // (len(wholes) // 2), 2 * (k % (len(wholes) // 2))
                        pe.wait_ge(raw_landed[n % NRAW], 16 * (n // NRAW + 1))
                        if j0 == 0:
                            pe.wait_ge(s["n_flat"], kv + 1)
                            pe.wait_ge(s["n_ql"], 2 * kv + 2)
                        for jj in range(2):
                            for c in range(2):
                                last = pe.matmul(ps[2 * kv + c][:, 0:NGR * NCMP],
                                                 raw[:, n % NRAW, jj * CHID + c * P:jj * CHID + (c + 1) * P],
                                                 flat[:, kv, j0 + jj].rearrange("p g n -> p (g n)"),
                                                 start=j0 + jj == 0, stop=j0 + jj == CB // 2 - 1)
                        last.then_inc(s["whole_used"], 1)
                    pe.wait_ge(s["n_hid"], 4)
                    pe.wait_ge(s["n_k"], 2)
                    for g in range(NGR):
                        blocks_ = slice(g * NCMP, (g + 1) * NCMP)
                        for c in range(2):
                            pe.matmul(ps[4][g * HD:(g + 1) * HD, 0:NCMP], w2c[:, 0, c], hg[:, c, blocks_], start=c == 0, stop=c == 1)
                        for c in range(2):
                            last = pe.matmul(ps[5][0:NCMP, g * HD:(g + 1) * HD], hg[:, 2 + c, blocks_], w2c[:, 1, c],
                                             start=c == 0, stop=c == 1)
                    last.then_inc(s["n_kcT"], 1)
                    pe.wait_ge(s["n_kc"], 1)

                    def scores(v, r):
                        i, g = tile_of[v], v % NGR
                        n_win = min(i + 1, WIN // P + 1)
                        if v or r:
                            pe.wait_ge(s["n_max"], R * v + r)
                        q = qh[:, r, i * P:(i + 1) * P]
                        pe.matmul(ps[0][:, 0:(i + 1) * P], q, ksh[:, 0, g, 0:(i + 1) * P], start=True, stop=True)
                        pe.matmul(ps[1][:, 0:n_win * P], q, ksh[:, 1, g, (i + 1 - n_win) * P:(i + 1) * P], start=True,
                                  stop=True)
                        pe.matmul(ps[1][:, 384:384 + 32], q, kch[:, g, 0:32], start=True, stop=True).then_inc(
                            s["n_score"], 1)

                    def shifted(n):
                        v, kind, tile = att[n]
                        i, g, slot = tile_of[v], v % NGR, v % 2
                        cols = slice(tile * P, (tile + 1) * P)
                        if kind == SELECTED:
                            pe.wait_ge(s["n_diag"], v + 1)
                        else:
                            pe.wait_ge(s["n_diag_rest"], 2 * v + (1 if kind == COMPRESSED else 2))
                        if n >= 4:
                            pe.wait_ge(s["n_exp"], n - 3)
                        bank = ps[2 + n % 4][:].rearrange("p (r q) -> p r q", r=R)
                        if kind == COMPRESSED:
                            kh, kl = kch[:, g], kcl[:, g]
                        else:
                            kh, kl = (x[:, kind - SELECTED, g, cols] for x in (ksh, ksl))
                        q_high, q_low = (x[:, :, i * P:(i + 1) * P] for x in (qh, ql))
                        pe.matmul(bank, kh, q_high, start=True, stop=False)
                        pe.matmul(bank, kh, q_low, start=False, stop=False)
                        pe.matmul(bank, kl, q_high, start=False, stop=False)
                        msk = None
                        if kind == COMPRESSED:
                            msk = cmaskT[:, i]
                        elif tile == i:
                            msk = wmaskT[:, 2]
                        elif kind == WINDOW and tile == i - WIN // P:
                            msk = wmaskT[:, 0]
                        if msk is not None:
                            pe.matmul(bank, identr[:], msk.unsqueeze(1).to_broadcast([P, R, P]), start=False, stop=False)
                        pe.matmul(bank, onesr[:], diag[:, slot, kind], start=False, stop=True).then_inc(
                            s["n_shifted"], 1)

                    def values(n):
                        v, kind, tile = att[n]
                        g = v % NGR
                        pe.wait_ge(s["n_exp"], n + 1)
                        first = n == 0 or att[n - 1][0] != v
                        if first and v:
                            pe.wait_ge(s["n_o"], v)
                        final = n + 1 == att_end[v]
                        val = vca[:, g] if kind == COMPRESSED else vsw[:, kind - SELECTED, tile, g]
                        for r in range(R):
                            col = (3 * (r % 2) + kind) * (HD + 1)
                            last = pe.matmul(ps[6 + r // 2][:, col:col + HD + 1], pT[:, n % 4, r], val,
                                             start=first and r % 2 == 0, stop=final and r % 2 == 1,
                                             skip_group_check=True)
                        last.then_inc(s["n_av"], 1)

                    pe.wait_ge(s["n_va"], N_VA)
                    for r in range(R):
                        scores(0, r)
                    for n in range(len(att) + LAG):
                        if n < len(att):
                            shifted(n)
                        under_way = n < len(att) and n >= LAG and att[n - LAG][0] == att[n][0]
                        if under_way:
                            for v, r in maxima_after.get(n, ()):
                                scores(v, r)
                        if n >= LAG:
                            values(n - LAG)
                        if not under_way:
                            for v, r in maxima_after.get(n, ()):
                                scores(v, r)

                    turn(ytok, 2, KD - 2, "g_y", 0, tile_of[::NGR])
                    for b in range(B_OUT, B_OUT + 2):
                        product(b, ("x_lo", KD, 4) if b == B_OUT else None)
                    turn(fbuf, 0, KD, "normed", NT)
                    for part in range(2):
                        for n in range(4):
                            b = B_UP[part] + n
                            if part and n < 2:
                                pe.wait_ge(s["evacuated"], B_OUT + n + 1)
                            elif n >= 2:
                                pe.wait_ge(s["f_sq"], 16 * part + 4 * (n - 1))
                            product(b, ("x_lo", 2 * KD, 4) if b == B_UP[0] else None)
                        pe.wait_ge(s["f_sq"], 16 * part + 12)
                        product(B_DOWN[part], ("f_lo", 16 * part, 0))
                        product(B_DOWN[part] + 1)
            nc.multi_engine_barrier(list(nc.engines), sems_to_clear=layer_sems)

        with nc.Block() as block:
            @block.sync
            def _(sp):
                sp.dma_start(out[0].rearrange("(i p) d -> p i d", p=P), h[:]).then_inc(once["stored"], 16)
                sp.wait_ge(once["stored"], 16)


def kernel(**inputs):
    import concourse.bacc as bacc
    import numpy as np
    from concourse.bass_utils import run_bass_kernel_spmd

    nc = bacc.Bacc("TRN2", target_bir_lowering=False, num_devices=1)
    arrays, tensors = {}, {}
    for name, value in inputs.items():
        a = np.ascontiguousarray(value)
        arrays[f"in_{name}"] = a
        tensors[name] = nc.dram_tensor(f"in_{name}", a.shape, mybir.dt.from_np(a.dtype), kind="ExternalInput").ap()
    out = nc.dram_tensor("out", (1, T, D), F32, kind="ExternalOutput").ap()
    build(nc, tensors, out)
    result = run_bass_kernel_spmd(nc, [arrays], core_ids=[0])
    return result.results[0]["out"]
```

```python
from contextlib import ExitStack

import concourse.bass as bass
from concourse import mybir

F32 = mybir.dt.float32
F32R = mybir.dt.float32r
I32 = mybir.dt.int32
ALU = mybir.AluOpType
ACT = mybir.ActivationFunctionType
AX = mybir.AxisListType.X

P = 128
DEPTH, D, T = 2, 1024, 512
NT = T // P
KD = D // P
SSM, MLS, NSA = D // 4, D // 4, D // 2
NG, GH, NP_ = 16, 16, 64
NJ = NG * NP_ // P
L = P
MH, HD, KCONV = 4, 64, 4
NH, NGR = NSA // HD, 2
R = NH // NGR
CB, CS_, CHID = 32, 16, 256
NCMP = T // CS_ - CB // CS_ + 1
WIN = 256
FF = 4 * D
EPS = 1e-6
NEG = -2.0 ** 99
THETA, ROT = 500000.0, HD // 8
D_IN = SSM + 4 * MLS + 2 * MH + NSA + 6 * NGR * HD + 3 * NH

ZF = SSM + 2 * MLS
ZT = D_IN - ZF
ZV, ZO, ZI, ZFG, ZQ = 0, MLS, 2 * MLS, 2 * MLS + MH, 2 * MLS + 2 * MH
ZKC = ZQ + NSA
GW = NGR * HD
ZVC, ZKS, ZVS, ZKW, ZVW = (ZKC + n * GW for n in range(1, 6))
ZG = ZKC + 6 * GW

R_PRE, R_MLP, R_GN, R_D, R_CONV = 0, 8, 16, 24, 26
R_PEK, R_PEV = R_CONV + 4 * KCONV, R_CONV + 4 * KCONV + CB // 2
R_LR = R_PEV + CB // 2
R_LI = R_LR + NJ
R_DT = 96
NROW = R_DT + NJ

TWO_PI = 6.283185307179586
C1 = 6.28125
C2 = round((TWO_PI - C1) * 2 ** 22) / 2 ** 22
C3 = TWO_PI - C1 - C2
ROUND = 1.5 * 2.0 ** 23
ROUND13 = 1.5 * 2.0 ** 10
PI_IN = 3.1415925

NRAW, NSPLIT = 6, 4


(S_DT, S_X, S_MAG, S_TH, S_R, S_ABS, S_SIN, S_COS, S_ARE, S_AIM, S_DEN, S_RDEN, S_E, S_GRE, S_GIM, S_RHI, S_RLO,
 S_IRE, S_IIM, S_T0, S_T1, S_T2, S_T3) = range(23)
N_PARAMS = 9
COMPRESSED, SELECTED, WINDOW = range(3)


def key_tiles(i):
    return ([(SELECTED, n) for n in range(i + 1)] + [(WINDOW, n) for n in range(max(0, i - WIN // P), i + 1)]
            + [(COMPRESSED, 0)])


def reduce_angle(dve, link, out, angle, whole):
    link(dve.tensor_scalar(whole, angle, 1.0 / TWO_PI, ROUND, ALU.mult, ALU.add))
    link(dve.tensor_scalar(whole, whole, ROUND, None, ALU.subtract))
    for c in (C1, C2, C3):
        link(dve.scalar_tensor_tensor(out, whole, -c, angle, ALU.mult, ALU.add))
        angle = out
    link(dve.tensor_scalar(out, out, PI_IN, -PI_IN, ALU.min, ALU.max))


def absolute(dve, out, x):
    return dve.scalar_tensor_tensor(out, x, -1.0, x, ALU.mult, ALU.max)


def low(dve, g, fl, fh, sq_t, s):
    dve.wait_ge(s["f_hi"], g + 1)
    dve.tensor_tensor(fl[:, g % 16], sq_t[:, g % 2], fh[:, g % 16].bitcast(F32), ALU.subtract).then_inc(s["f_lo"], 1)


def weight_units(t, layer):
    units = []
    cols = [(0, 512), (512, ZF)] + [(ZF + a, min(ZF + a + 512, D_IN)) for a in range(0, ZT, 512)]
    for a, b in cols:
        for k in range(KD):
            units.append((t["w_in"][layer, k * P:(k + 1) * P, a:b], "split", b - a))
    for name in ("cmp_w1_k", "cmp_w1_v"):
        for j in range(CB // 4):
            src = t[name][layer, 2 * j * P:(2 * j + 2) * P, :].rearrange("(j p) c -> p j c", p=P)
            units.append((src, "whole", 2 * CHID))
    for half in range(2):
        for k in range(KD):
            units.append((t["w_out"][layer, k * P:(k + 1) * P, half * 512:half * 512 + 512], "split", 512))
    for part in range(2):
        for c in range(4):
            for k in range(KD):
                a = part * FF // 2 + c * 512
                units.append((t["mlp_w1"][layer, k * P:(k + 1) * P, a:a + 512], "split", 512))
        for half in range(2):
            for k in range(FF // 2 // P):
                a = part * FF // 2 + k * P
                units.append((t["mlp_w2"][layer, a:a + P, half * 512:half * 512 + 512], "split", 512))
    return units, [b - a for a, b in cols]


def build(nc, t, out):
    ctx = ExitStack()
    with ctx:
        at = [nc.sbuf_base]
        place = {}

        def over(name, shape, under, dt=F32):
            return nc.alloc_sbuf_tensor_at(name, shape, dt, offset=place[under])

        def sb(name, shape, dt=F32):
            place[name] = at[0]
            size = 4
            for n in shape[1:]:
                size *= n
            size = (size + 31) // 32 * 32
            tensor = nc.alloc_sbuf_tensor_at(name, shape, dt, offset=at[0])
            at[0] += size
            return tensor

        at[0] = (at[0] + 31) // 32 * 32
        h = sb("h", [P, NT, D])
        xh = sb("xh", [P, KD, T], F32R)
        xl = sb("xl", [P, KD, T], F32R)
        raw = sb("raw", [P, NRAW, 512])
        wh = sb("wh", [P, NSPLIT, 512], F32R)
        wl = sb("wl", [P, NSPLIT, 512], F32R)
        fbuf = sb("fbuf", [P, NT, D])
        gpost = sb("gpost", [P, 2, D])
        junk = over("junk", [P, D], "xl")
        ident = sb("ident", [P, P])
        mask = sb("mask", [P, 512])
        wmask = sb("wmask", [P, 384])
        cmask = sb("cmask", [P, NT, 32])
        cvalid = sb("cvalid", [P, 1])
        nident = sb("nident", [P, P])
        identr = sb("identr", [P, P], F32R)
        onesr = sb("onesr", [P, P], F32R)
        wmaskT = sb("wmaskT", [P, 3, P], F32R)
        cmaskT = sb("cmaskT", [P, NT, P], F32R)
        maskT = sb("maskT", [P, P])
        bones = sb("bones", [P, P])
        par = sb("par", [P, 4])
        sel = sb("sel", [MH, MH, P])
        sel2 = sb("sel2", [MH, 2, P])
        keep = sb("keep", [MH, T])
        steps = sb("steps", [P, L + 1])
        stepi = sb("stepi", [P, L + 1], I32)
        consts = sb("consts", [P, 2])
        posi = sb("posi", [P, NT], I32)
        posf = sb("posf", [P, NT])
        cosr = sb("cosr", [P, NT, ROT])
        sinr = sb("sinr", [P, NT, ROT])
        pcol = sb("pcol", [P, NROW])
        pcols = sb("pcols", [P, DEPTH, NROW])
        gateb = sb("gateb", [MH, 2])
        wglu = sb("wglu", [P, 2, SSM])
        w2c = sb("w2c", [P, 2, 2, HD])
        bnat = sb("bnat", [P, 2, NJ, GH])
        cnat = sb("cnat", [P, 2, 2, NP_])
        stat = sb("stat", [P, 4, NT])
        small = sb("small", [P, 24, NJ])
        shared = at[0]
        z = sb("z", [P, NT, ZT])
        su = sb("su", [P, 2, T])
        qkr = sb("qkr", [P, 4, KCONV - 1 + T])
        ytok = over("ytok", [P, NT, MLS + NSA], "fbuf")
        work = at[0]
        vr = sb("vr", [P, NJ, T])
        vi = over("vi", [P, NJ, T], "fbuf")
        ctab = sb("ctab", [P, NJ, L + 1])
        stab = sb("stab", [P, NJ, L + 1])
        bd = sb("bd", [P, 2, NJ, 32])
        bT = sb("bT", [P, 4, P], F32R)
        bTl = over("bTl", [P, 4, P], "bd", F32R)
        place["behind gpost"] = place["gpost"] + 2 * T * 4
        suh = over("suh", [P, 2, T], "gpost", F32R)
        sul = over("sul", [P, 2, T], "behind gpost", F32R)
        cb = sb("cb", [P, 2, 2, P])
        cT = sb("cT", [P, 2, 2, P])
        tmp = sb("tmp", [P, 4, T])
        s5_end = at[0]
        at[0] = work
        tang = sb("tang", [P, NJ, L + 1])
        tnum = sb("tnum", [P, NJ, L + 1])
        assert at[0] <= work + NJ * T * 4
        tred = over("tred", [P, NJ, L + 1], "fbuf")
        at[0] = work
        qk = sb("qk", [P, 4, T])
        wT = sb("wT", [P, MH, T])
        ctmp = over("ctmp", [P, T], "wT")
        kw = sb("kw", [P, NT, MH, HD])
        va = sb("va", [P, NT, MH, HD + 1])
        nu = sb("nu", [P, NT, MH, HD + 1])
        so = sb("so", [P, NT, MLS])
        rows = over("rows", [MH, 8, T], "xl")
        msr = sb("msr", [MH, NT])
        colt = sb("colt", [P, 4, NT, MH])
        cst = sb("cst", [P, 2, HD + 1])
        dec = sb("dec", [P, 2, NT])
        mden = sb("mden", [P, 2, NT, MH])
        mtmp = sb("mtmp", [P, MH, HD + 1])
        mls_end = at[0]
        at[0] = work
        qa = over("qa", [P, NT, R, NGR, HD], "xh")
        flat = over("flat", [P, 2, CB // 2, NGR, NCMP], "wl")
        qh = sb("qh", [P, R, T], F32R)
        ql = sb("ql", [P, R, T], F32R)
        ksh = over("ksh", [P, 2, NGR, T], "qkr", F32R)
        ksl = sb("ksl", [P, 2, NGR, T], F32R)
        place["behind mlstm"] = mls_end
        vsw = over("vsw", [P, 2, NT, NGR, HD + 1], "behind mlstm")
        vca = sb("vca", [P, NGR, HD + 1])
        place["behind qa"] = place["xh"] + NT * NSA * 4
        rtmp = over("rtmp", [P, 4, NT * NH * ROT], "behind qa")
        place["behind ytok"] = place["fbuf"] + NT * (MLS + NSA) * 4
        hg = over("hg", [P, 4, NGR * NCMP], "behind ytok")
        place["behind rtmp"] = place["behind qa"] + 4 * NT * NH * ROT * 4
        gate = over("gate", [P, NT, 3 * NH], "behind rtmp")
        am = sb("am", [P, 4, 12])
        cf = sb("cf", [P, 2, 12])
        diag = over("diag", [P, 2, 3, R, P], "xl", F32R)
        place["behind diag"] = place["xl"] + 2 * 3 * R * P * 4
        kch = over("kch", [P, NGR, P], "behind diag", F32R)
        place["behind kch"] = place["behind diag"] + NGR * P * 4
        kcl = over("kcl", [P, NGR, P], "behind kch", F32R)
        pT = over("pT", [P, 4, R, P], "xh")
        prod = sb("prod", [P, 2, R, 3, HD])
        junkz = over("junkz", [P, 512], "z")
        gsq = over("gsq", [P, NT, MLS + NSA], "z")
        gst = sb("gst", [P, 3, NT, 12])
        nsa_end = at[0]
        assert nsa_end <= mls_end
        at[0] = shared
        fh = sb("fh", [P, FF // 2 // P, T], F32R)
        fl = sb("fl", [P, FF // 2 // P, T], F32R)
        act_t = sb("act_t", [P, 2, T])
        sq_t = sb("sq_t", [P, 2, T])
        mlp_end = at[0]
        ps = [ctx.enter_context(nc.psum_tensor(f"ps{n}", [P, 512], F32)) for n in range(8)]


        def sems(text):
            made = {name: ctx.enter_context(nc.semaphore(name)) for name in text.split()}
            numbers = [x.num for x in made.values()]
            assert numbers == list(range(numbers[0], numbers[0] + len(numbers)))
            return made, range(numbers[0], numbers[0] + len(numbers))

        once, _ = sems("""x_landed rows_landed rows_ready rows_turned x_squared pool_made rope_ready rope_trig
            setup_steps stored""")
        s, layer_sems = sems("""
            params_landed raw_landed0 raw_landed1 raw_landed2 raw_landed3 raw_landed4 raw_landed5
            w_hi w_lo w_used whole_used evacuated f_sum f_gain
            act_steps dve_steps cols_ready ssq msq rms normed turned x_hi x_lo h_new
            f_relu f_sq f_hi f_lo
            gains_landed bank_done bank_out s5_dt s5_ang s5_trig s5_phase s5_table s5_nat s5_natT s5_mats s5_bu s5_rot s5_x s5_y
            s5_ypre s5_gelu s5_glu s5_sig s5_sq s5_ms s5_rt s5_done
            m_pad conv_steps m_conv m_conv_k m_qk m_gateT m_fx m_ln m_rows m_exp m_colT m_bc m_cols m_arg m_w m_s m_p m_kT m_kw
            m_va n_va m_chunk m_state m_nu m_so m_out
            n_rope n_qa n_qT n_q n_ql n_kT n_kh n_k n_flat n_hid n_kcT n_kch n_kc n_gate
            n_score n_max n_diag n_diag_rest n_shifted n_exp n_av n_o n_y
            g_sq g_ms g_rt g_y""")
        raw_landed = [s[f"raw_landed{n}"] for n in range(NRAW)]

        def chain(engine, semaphore):
            count = [0]

            def link(instruction):
                count[0] += 1
                instruction.then_inc(semaphore, 1)
                engine.wait_ge(semaphore, count[0])
            return link

        prow = over("prow", [NROW, DEPTH, P], "xh")
        dt8 = over("dt8", [NROW, DEPTH, 2], "wh")
        wmaskT_f = over("wmaskT_f", [P, 3, P], "z")
        cmaskT_f = over("cmaskT_f", [P, NT, P], "su")
        with nc.Block() as block:
            @block.sync
            def _(sp):
                sp.dma_start(h[:], t["x"][0].rearrange("(i p) d -> p i d", p=P)).then_inc(once["x_landed"], 16)
                sp.dma_start(posi[:], t["positions"][0].rearrange("(i p) -> p i", p=P),
                             allow_slow_non_contiguous=True).then_inc(once["x_landed"], 16)
                sp.wait_ge(once["pool_made"], 1)
                for row, src in (
                    (R_PRE, t["ln_mix_pre"].rearrange("l (k p) -> k l p", p=P)),
                    (R_MLP, t["ln_mlp_pre"].rearrange("l (k p) -> k l p", p=P)),
                    (R_GN, t["gn_ssm"].rearrange("l (k p) -> k l p", p=P)),
                    (R_GN + 2, t["gn_mlstm"].rearrange("l (k p) -> k l p", p=P)),
                    (R_GN + 4, t["gn_nsa"].rearrange("l (k p) -> k l p", p=P)),
                    (R_D, t["ssm_d"].rearrange("l (k p) -> k l p", p=P)),
                    (R_PEK, t["cmp_pe_k"].rearrange("l (j q) d -> j l (q d)", q=2)),
                    (R_PEV, t["cmp_pe_v"].rearrange("l (j q) d -> j l (q d)", q=2)),
                    (R_LR, t["ssm_lambda_re"].rearrange("l (j g) p -> j l (g p)", g=2)),
                    (R_LI, t["ssm_lambda_im"].rearrange("l (j g) p -> j l (g p)", g=2)),
                ):
                    sp.dma_start(prow[row:row + src.shape[0], :, :], src).then_inc(once["rows_landed"], 16)
                for one in range(DEPTH):
                    conv = t["mlstm_conv"][one].rearrange("k (c p) -> (k c) p", p=P)
                    sp.dma_start(prow[R_CONV:R_CONV + conv.shape[0], one, :], conv).then_inc(once["rows_landed"], 16)
                sp.dma_start(dt8[R_DT:R_DT + NJ, :, :], t["ssm_log_dt"].rearrange("l (j g) -> j l g", g=2),
                             allow_slow_non_contiguous=True).then_inc(once["rows_landed"], 16)
                sp.wait_ge(once["x_landed"], 32)

            @block.gpsimd
            def _(pool):
                link = chain(pool, once["pool_made"])

                def keep_where(tile, pattern, base, mult, fill, op=ALU.is_ge):
                    link(pool.affine_select(out=tile, in_=tile, pattern=pattern, base=base,
                                            channel_multiplier=mult, compare_op=op, fill=fill))

                for tile, value in ((prow, 0.0), (ident, 0.0), (mask, 0.0), (wmask, 0.0), (cmask, 0.0), (cvalid, 1.0), (nident, 0.0),
                                    (maskT, 0.0), (bones, 1.0 / GH), (sel, 0.0), (sel2, 0.0), (keep, 1.0),
                                    (wmaskT_f, 0.0), (cmaskT_f, 0.0)):
                    link(pool.memset(tile[:], value))
                link(pool.memset(consts[:, 0:1], TWO_PI / 4))
                link(pool.memset(consts[:, 1:2], EPS))
                for n in range(ROT):
                    link(pool.memset(small[:, 0, n:n + 1], THETA ** (-2.0 * n / (2 * ROT))))
                keep_where(ident[:], [[-1, P]], 0, 1, 1.0, ALU.not_equal)
                keep_where(mask[:, 384:512], [[-1, P]], 0, 1, NEG)
                keep_where(wmask[:, 256:384], [[-1, P]], 0, 1, NEG)
                keep_where(wmask[:, 0:128], [[1, P]], -1, -1, NEG)
                keep_where(cmask[:], [[P, NT], [-CS_, 32]], 1 - CB, 1, NEG)
                keep_where(cvalid[:], [[0, 1]], 1 - CB, 1, 0.0)
                keep_where(nident[:], [[-1, P]], 0, 1, -1.0, ALU.not_equal)
                keep_where(wmaskT_f[:, 0], [[-1, P]], -1, 1, NEG)
                keep_where(wmaskT_f[:, 2], [[1, P]], 0, -1, NEG)
                keep_where(cmaskT_f[:], [[P, NT], [1, P]], 1 - CB, -CS_, NEG)
                keep_where(cmaskT_f[:], [[0, NT], [0, P]], NCMP - 1, -1, NEG)
                keep_where(maskT[:], [[1, P]], 0, -1, NEG)
                keep_where(bones[:].rearrange("p (b c) -> p b c", c=GH), [[-GH, P // GH], [0, GH]], 0, 1, 0.0)
                keep_where(bones[:].rearrange("p (b c) -> p b c", c=GH), [[GH, P // GH], [0, GH]], GH - 1, -1, 0.0)
                keep_where(sel[:], [[-1, MH], [0, P]], 0, 1, 1.0, ALU.not_equal)
                keep_where(sel2[:].rearrange("k a (b c) -> k a b c", b=2), [[-2, 2], [-1, 2], [0, HD]], 0, 1, 1.0,
                           ALU.not_equal)
                keep_where(keep[:].rearrange("k (a b) -> k a b", b=L), [[0, NT], [1, L]], 0, 0, 0.0, ALU.not_equal)
                link(pool.iota(stepi[:], [[1, L + 1]], base=0, channel_multiplier=0))

            N_POOL = 14 + 2 + ROT + 17 + 1

            @block.vector
            def _(dve):
                link = chain(dve, once["setup_steps"])
                dve.wait_ge(once["pool_made"], N_POOL)
                link(dve.tensor_copy(steps[:], stepi[:]))
                for parity in range(2):
                    link(dve.tensor_reduce(par[:, parity:parity + 1], bones[:, GH * parity:P:2 * GH], AX, ALU.add))
                link(dve.tensor_scalar(par[:, 0:2], par[:, 0:2], float(GH), None, ALU.mult))
                link(dve.tensor_scalar(par[:, 2:4], par[:, 0:2], -1.0, None, ALU.mult))
                link(dve.tensor_copy(identr[:], ident[:]))
                link(dve.tensor_scalar(onesr[:], ident[:], 0.0, 1.0, ALU.mult, ALU.add))
                link(dve.tensor_copy(wmaskT[:], wmaskT_f[:]))
                link(dve.tensor_copy(cmaskT[:], cmaskT_f[:]))
                dve.wait_ge(once["x_landed"], 32)
                link(dve.tensor_copy(posf[:], posi[:]))
                link(dve.tensor_tensor(sinr[:], posf[:].unsqueeze(2).to_broadcast([P, NT, ROT]),
                                       small[:, 0:1, :].to_broadcast([P, NT, ROT]), ALU.mult))
                reduce_angle(dve, link, sinr[:], sinr[:], cosr[:])
                absolute(dve, cosr[:], sinr[:]).then_inc(once["rope_ready"], 1)
                dve.wait_ge(once["rows_landed"], 16 * (11 + DEPTH))
                dve.tensor_copy(prow[R_DT:R_DT + NJ, :, :].rearrange("j l (g p) -> j l g p", g=2),
                                dt8[R_DT:R_DT + NJ, :, :].unsqueeze(3).to_broadcast([NJ, DEPTH, 2, NP_])).then_inc(
                    once["rows_ready"], 1)
                dve.wait_ge(once["rows_turned"], 1)
                link(dve.tensor_copy(pcols[:], ps[7][:, 0:DEPTH * NROW].rearrange("p (l n) -> p l n", l=DEPTH)))

            @block.tensor
            def _(pe):
                pe.wait_ge(once["rows_ready"], 1)
                for one in range(DEPTH):
                    last = pe.transpose(ps[7][:, one * NROW:(one + 1) * NROW], prow[:, one], ident[0:NROW, 0:NROW])
                last.then_inc(once["rows_turned"], 1)

            @block.scalar
            def _(act):
                act.wait_ge(once["rope_ready"], 1)
                act.activation(cosr[:], cosr[:], ACT.Sin, bias=consts[:, 0:1], scale=-1.0).then_inc(once["rope_trig"], 1)
                act.activation(sinr[:], sinr[:], ACT.Sin).then_inc(once["rope_trig"], 1)
                act.wait_ge(once["rope_trig"], 2)
                act.wait_ge(once["x_landed"], 32)
                for i in range(NT):
                    act.activation(junk[:], h[:, i], ACT.Square, accum_out=stat[:, 0, i:i + 1]).then_inc(once["x_squared"], 1)
                    act.wait_ge(once["x_squared"], i + 1)

        with nc.Fori(0, DEPTH) as layer:
            with nc.Block() as block:
                units, widths = weight_units(t, layer)
                splits = [n for n, unit in enumerate(units) if unit[1] == "split"]
                wholes = [n for n, unit in enumerate(units) if unit[1] == "whole"]
                order = {n: k for kind in (splits, wholes) for k, n in enumerate(kind)}
                N_SPLIT = len(splits)

                def unit_tile(n):
                    return raw[:, n % NRAW, 0:units[n][2]]

                def landed(engine, n):
                    engine.wait_ge(raw_landed[n % NRAW], 16 * (n // NRAW + 1))

                blocks = []
                first = 0
                for n, width in enumerate(widths):
                    blocks.append((first, KD, n < 2, width))
                    first += KD
                for part in (("out",), ("up", "down"), ("up", "down")):
                    for what in part:
                        for _ in range(4 if what == "up" else 2):
                            deep = FF // 2 // P if what == "down" else KD
                            blocks.append((first, deep, what == "up", 512))
                            first += deep
                assert first == N_SPLIT
                B_IN, B_OUT = 0, 6
                in_banks = [4, 2, 4, 4, 4, 4]
                B_UP, B_DOWN = (8, 14), (12, 18)
                N_IN = 6 * KD
                CHUNK_BANK = (0, 4, 5, 6)

                tile_of = [NT - 1 - v // NGR for v in range(NT * NGR)]
                att = [(v, kind, n) for v in range(NT * NGR) for kind, n in key_tiles(tile_of[v])]
                att_end = [sum(x[0] <= v for x in att) for v in range(NT * NGR)]
                LAG = 4
                begin = [0] + att_end[:-1]
                pace = (begin[-1] - 3) / (R * (NT * NGR - 1) - 1)
                maxima_after, diagonals_after = {}, {}
                for head in range(R * (NT * NGR - 1)):
                    n = int(head * pace)
                    v, r = 1 + head // R, head % R
                    maxima_after.setdefault(n, []).append((v, r))
                    if r == R - 1:
                        assert n <= begin[v] - 2
                        diagonals_after.setdefault(max(n, begin[v - 1]), []).append(v)
                N_VA = 4 + 1 + 2 * NT + 2

                @block.sync
                def _(sp):
                    def load(tile, src, slow=False, landed="params_landed"):
                        params.append(sp.dma_start(tile, src, allow_slow_non_contiguous=slow).then_inc(s[landed], 16))

                    def load_unit(n):
                        src, kind, width = units[n]
                        tile = unit_tile(n)
                        if kind == "whole":
                            tile = tile.rearrange("p (j c) -> p j c", j=2)
                        sp.dma_start(tile, src).then_inc(raw_landed[n % NRAW], 16)

                    params = []
                    for n in range(NRAW):
                        load_unit(n)
                    load(bnat[:, 0], t["ssm_b_re"][layer].rearrange("(j g) p h -> (g p) j h", g=2))
                    load(bnat[:, 1], t["ssm_b_im"][layer].rearrange("(j g) p h -> (g p) j h", g=2))
                    load(cnat[:, 0], t["ssm_c_re"][layer].rearrange("(c g) h p -> (g h) c p", c=2))
                    load(cnat[:, 1], t["ssm_c_im"][layer].rearrange("(c g) h p -> (g h) c p", c=2))
                    load(gateb[:, 0:1], t["mlstm_b_i"][layer].unsqueeze(1), True)
                    load(gateb[:, 1:2], t["mlstm_b_f"][layer].unsqueeze(1), True)
                    load(wglu[:], t["ssm_w_glu"][layer].rearrange("(c p) n -> p c n", p=P))
                    load(w2c[:, 0], t["cmp_w2_k"][layer].rearrange("(c p) n -> p c n", p=P))
                    load(w2c[:, 1], t["cmp_w2_v"][layer].rearrange("(c p) n -> p c n", p=P))
                    assert len(params) == N_PARAMS
                    for n in range(NRAW, len(units)):
                        before = n - NRAW
                        sp.wait_ge(s["w_lo" if units[before][1] == "split" else "whole_used"], order[before] + 1)
                        if n == N_IN:
                            sp.wait_ge(s["s5_bu"], NJ)
                            for a, gains in enumerate(("ln_mix_post", "ln_mlp_post")):
                                sp.dma_start(gpost[:, a], t[gains][layer].partition_broadcast(P)).then_inc(s["gains_landed"], 16)
                        load_unit(n)

                @block.gpsimd
                def _(pool):
                    def split_low(k):
                        pool.wait_ge(s["w_hi"], k + 1)
                        n = splits[k]
                        width = units[n][2]
                        pool.tensor_tensor(wl[:, k % NSPLIT, 0:width], unit_tile(n), wh[:, k % NSPLIT, 0:width].bitcast(F32),
                                           ALU.subtract).then_inc(s["w_lo"], 1)

                    pool.memset(qkr[:, :, 0:KCONV - 1], 0.0).then_inc(s["m_pad"], 1)
                    for k in range(N_IN):
                        split_low(k)
                    pool.wait_ge(s["s5_ypre"], 2)
                    conv_link = chain(pool, s["conv_steps"])
                    for n in range(2, 4):
                        for k in range(KCONV):
                            tap = pcol[:, R_CONV + 4 * k + n:R_CONV + 4 * k + n + 1].to_broadcast([P, T])
                            into = ctmp[:] if k else qk[:, n]
                            conv_link(pool.tensor_tensor(into, qkr[:, n, k:k + T], tap, ALU.mult))
                            if k:
                                last = pool.tensor_tensor(qk[:, n], qk[:, n], ctmp[:], ALU.add)
                                if k < KCONV - 1:
                                    conv_link(last)
                        last.then_inc(s["m_conv_k"], 1)
                        pool.wait_ge(s["m_conv_k"], n - 1)
                    pool.wait_ge(s["bank_out"], sum(in_banks))
                    pool.memset(va[:], 1.0).then_inc(s["m_va"], 1)
                    pool.wait_ge(s["m_va"], 1)
                    for i in range(NT):
                        pool.tensor_copy(va[:, i, :, 0:HD], z[:, i, ZV:ZV + MLS].rearrange("p (h d) -> p h d", h=MH)).then_inc(
                            s["m_va"], 1)
                    pool_link = chain(pool, s["n_va"])
                    pool.wait_ge(s["m_conv"], 2)
                    pool_link(pool.memset(ksh[:].bitcast(F32), 0.0))
                    pool.wait_ge(s["s5_done"], 2)
                    pool_link(pool.memset(vsw[:], 1.0))
                    for n, a in enumerate((ZVS, ZVW)):
                        for i in range(NT):
                            pool_link(pool.tensor_copy(vsw[:, n, i, :, 0:HD],
                                                       z[:, i, a:a + GW].rearrange("p (g d) -> p g d", g=NGR)))
                    pool.wait_ge(s["m_out"], 1)
                    for keys in (kch, kcl):
                        pool_link(pool.memset(keys[:].bitcast(F32), 0.0))
                    pool_link(pool.memset(vca[:], 0.0))
                    pool_link(pool.memset(vca[0:NCMP, :, HD:HD + 1], 1.0))
                    pool_link(pool.memset(ksl[:].bitcast(F32), 0.0))
                    def diagonals(v):
                        slot = v % 2
                        pool.wait_ge(s["n_max"], R * (v + 1))
                        if v >= 2:
                            pool.wait_ge(s["n_shifted"], att_end[v - 2])
                        for kind in (COMPRESSED, WINDOW):
                            shift = am[:, v % 4].rearrange("p (r k) -> p k r", k=3)[:, kind].unsqueeze(2)
                            pool.tensor_tensor(diag[:, slot, kind], nident[:].unsqueeze(1).to_broadcast([P, R, P]),
                                               shift.to_broadcast([P, R, P]), ALU.mult).then_inc(s["n_diag_rest"], 1)

                    def summed(v):
                        i, g = tile_of[v], v % NGR
                        to = ytok[:, i, MLS + g * R * HD:MLS + (g + 1) * R * HD].rearrange("p (r d) -> p r d", r=R)
                        pool.wait_ge(s["n_o"], v + 1)
                        pool.tensor_tensor(to, prod[:, v % 2, :, 0], prod[:, v % 2, :, 1], ALU.add).then_inc(s["n_y"], 1)
                        pool.wait_ge(s["n_y"], 2 * v + 1)
                        pool.tensor_tensor(to, to, prod[:, v % 2, :, 2], ALU.add).then_inc(s["n_y"], 1)

                    for k in range(N_IN, N_IN + NSPLIT - 1):
                        split_low(k)
                    diagonals(0)
                    for n in range(len(att) + LAG):
                        if n - LAG + 1 in att_end:
                            summed(att_end.index(n - LAG + 1))
                        for v in diagonals_after.get(n, ()):
                            diagonals(v)
                    for k in range(N_IN + NSPLIT - 1, N_SPLIT):
                        split_low(k)
                    pool.wait_ge(s["gains_landed"], 32)
                    for half in range(2):
                        for i in range(NT):
                            piece = fbuf[:, i, 512 * half:512 * half + 512]
                            pool.wait_ge(s["ssq"], 3 * NT + NT * half + i + 1)
                            pool.tensor_tensor(piece, piece, gpost[:, 1, 512 * half:512 * half + 512],
                                               ALU.mult).then_inc(s["f_gain"], 1)

                @block.scalar
                def _(act):
                    link = chain(act, s["act_steps"])

                    def split_high(k):
                        n = splits[k]
                        width = units[n][2]
                        landed(act, n)
                        if k >= NSPLIT:
                            act.wait_ge(s["w_used"], k - NSPLIT + 1)
                        act.activation(wh[:, k % NSPLIT, 0:width], unit_tile(n), ACT.Copy).then_inc(s["w_hi"], 1)

                    def splits_for(block_numbers, evacuate, hooks=(), done=0):
                        start = blocks[block_numbers[0]][0]
                        end = blocks[block_numbers[-1]][0] + blocks[block_numbers[-1]][1]
                        after = {blocks[b][0] + blocks[b][1] + NSPLIT - 1: b for b in block_numbers}
                        hooks = dict(hooks)
                        for k in range(start, end):
                            if k - start >= done:
                                split_high(k)
                            if k in after:
                                evacuate(after.pop(k))
                            if k - start in hooks:
                                hooks[k - start]()
                        for k in sorted(after):
                            evacuate(after[k])

                    def product_done(engine, b):
                        engine.wait_ge(s["w_used"], blocks[b][0] + blocks[b][1])

                    squared = [0]

                    def square(src, into, squares=junk):
                        if squared[0]:
                            act.wait_ge(s["ssq"], squared[0])
                        act.activation(squares[:, 0:src.shape[-1]], src, ACT.Square, accum_out=into).then_inc(s["ssq"], 1)
                        squared[0] += 1

                    def root(n):
                        act.wait_ge(s["msq"], n + 1)
                        act.activation(stat[:, 2, :], stat[:, 1, :], ACT.Sqrt).then_inc(s["rms"], 1)

                    def stream_squares(before):
                        for i in range(NT):
                            act.wait_ge(s["h_new"], before + i + 1)
                            square(h[:, i], stat[:, 0, i:i + 1])

                    def turned_high(first, gains):
                        for k in range(KD):
                            act.wait_ge(s["turned"], first + k + 1)
                            act.activation(xh[:, k], ps[k][:], ACT.Identity, scale=pcol[:, gains + k:gains + k + 1]).then_inc(
                                s["x_hi"], 1)

                    def take_in(b):
                        for n in range(in_banks[b]):
                            if n < in_banks[b] - 1:
                                act.wait_ge(s["bank_done"], sum(in_banks[:b]) - b + n + 1)
                            else:
                                product_done(act, b)
                            if b == 0 and n < 2:
                                act.activation(su[:, n], ps[n][:], ACT.Copy)
                                last = act.activation(suh[:, n], ps[n][:], ACT.Copy)
                            elif b < 2:
                                last = act.activation(qkr[:, 2 * b + n % 2, KCONV - 1:], ps[n][:], ACT.Copy)
                            else:
                                a = (b - 2) * 512
                                last = act.activation(z[:, n, a:a + widths[b]], ps[n][:, 0:widths[b]], ACT.Copy)
                            last.then_inc(s["bank_out"], 1)

                    def take_half(b):
                        product_done(act, b)
                        for i in range(NT):
                            last = act.activation(fbuf[:, i, 512 * (b % 2):512 * (b % 2) + 512], ps[4 * (b % 2) + i][:], ACT.Copy)
                        last.then_inc(s["evacuated"], 1)

                    def s5_dt():
                        act.activation(small[:, S_DT], pcol[:, R_DT:R_DT + NJ], ACT.Exp).then_inc(s["s5_dt"], 1)

                    def s5_trig():
                        act.wait_ge(s["s5_ang"], 1)
                        act.activation(small[:, S_MAG], small[:, S_X], ACT.Exp)
                        act.activation(small[:, S_SIN], small[:, S_R], ACT.Sin)
                        act.activation(small[:, S_COS], small[:, S_ABS], ACT.Sin, bias=consts[:, 0:1], scale=-1.0).then_inc(
                            s["s5_trig"], 1)

                    def s5_tables():
                        act.wait_ge(s["s5_phase"], 2)
                        act.activation(stab[:], tred[:], ACT.Sin).then_inc(s["s5_table"], 1)
                        act.activation(ctab[:], tang[:], ACT.Sin, bias=consts[:, 0:1], scale=-1.0).then_inc(s["s5_table"], 1)

                    root(0)
                    for k in range(NSPLIT - 1):
                        split_high(k)
                    act.wait_ge(s["cols_ready"], 1)
                    turned_high(0, R_PRE)
                    s5_dt()
                    splits_for(range(B_IN, B_OUT), take_in, {6: s5_trig, 12: s5_tables}, done=NSPLIT - 1)

                    for n in range(2):
                        act.wait_ge(s["s5_ypre"], n + 1)
                        act.activation(tmp[:, 2 + n], tmp[:, n], ACT.Gelu_apprx_tanh).then_inc(s["s5_gelu"], 1)
                    for n in range(2):
                        act.wait_ge(s["s5_glu"], n + 1)
                        act.activation(tmp[:, n], ps[6 + n][:], ACT.Sigmoid).then_inc(s["s5_sig"], 1)
                    for n in range(2):
                        act.wait_ge(s["s5_ms"], n + 1)
                        act.activation(tmp[:, n], ps[4 + n][:], ACT.Sqrt, bias=consts[:, 1:2]).then_inc(s["s5_rt"], 1)

                    act.wait_ge(s["m_fx"], 1)
                    link(act.activation(rows[:, 6], rows[:, 6], ACT.Exp, scale=-1.0))
                    act.activation(rows[:, 6], rows[:, 6], ACT.Ln, bias=1.0).then_inc(s["m_ln"], 1)
                    act.wait_ge(s["m_rows"], 1)
                    act.activation(rows[:, 5:8], rows[:, 5:8], ACT.Exp).then_inc(s["m_exp"], 1)
                    for n in range(4):
                        act.wait_ge(s["whole_used"], len(wholes))
                        act.activation(hg[:, n], ps[6][:, n * NGR * NCMP:(n + 1) * NGR * NCMP], ACT.Gelu_apprx_tanh).then_inc(s["n_hid"], 1)
                    for n in range(4):
                        act.wait_ge(s["m_conv" if n < 2 else "m_conv_k"], n % 2 + 1)
                        act.activation(qk[:, n], qk[:, n], ACT.Silu).then_inc(s["m_qk"], 1)
                    act.wait_ge(s["s5_done"], 2)
                    act.activation(so[:], z[:, :, ZO:ZO + MLS], ACT.Sigmoid).then_inc(s["m_so"], 1)
                    act.activation(gate[:], z[:, :, ZG:ZG + 3 * NH], ACT.Sigmoid).then_inc(s["n_gate"], 1)
                    for head in range(MH):
                        act.wait_ge(s["m_arg"], head + 1)
                        act.activation(wT[:, head], wT[:, head], ACT.Exp).then_inc(s["m_w"], 1)

                    act.wait_ge(s["n_rope"], 2)
                    for i in range(NT):
                        act.activation(qa[:, i].rearrange("p r g d -> p g r d"),
                                       z[:, i, ZQ:ZQ + NSA].rearrange("p (g r d) -> p g r d", g=NGR, r=R),
                                       ACT.Copy).then_inc(s["n_qa"], 1)
                    for r in range(R):
                        act.wait_ge(s["n_qT"], r + 1)
                        act.activation(qh[:, r], ps[r][:], ACT.Copy).then_inc(s["n_q"], 1)
                    for n in range(2):
                        act.wait_ge(s["n_kT"], n + 3)
                        act.wait_ge(s["n_va"], 1)
                        for g in range(NGR):
                            rows_ = slice(g * HD, (g + 1) * HD)
                            last = act.activation(ksh[rows_, n, g], ps[5 + n][rows_, :], ACT.Copy)
                        last.then_inc(s["n_kh"], 1)
                    act.wait_ge(s["n_kcT"], 1)
                    act.wait_ge(s["n_va"], N_VA - 1)
                    for g in range(NGR):
                        rows_ = slice(g * HD, (g + 1) * HD)
                        last = act.activation(kch[rows_, g, 0:NCMP], ps[7][rows_, 0:NCMP], ACT.Copy)
                    last.then_inc(s["n_kch"], 1)
                    def head_squares(v):
                        act.wait_ge(s["n_y"], 2 * (v + 1))
                        act.activation(gsq[:, tile_of[v]], ytok[:, tile_of[v]], ACT.Square).then_inc(s["g_sq"], 1)

                    for k in range(N_IN, N_IN + NSPLIT - 1):
                        split_high(k)
                    for n in range(len(att)):
                        act.wait_ge(s["n_shifted"], n + 1)
                        if n >= 4:
                            act.wait_ge(s["n_av"], n - 3)
                        act.activation(pT[:, n % 4], ps[2 + n % 4][:].rearrange("p (r q) -> p r q", r=R), ACT.Exp,
                                       scale=HD ** -0.5).then_inc(s["n_exp"], 1)
                        if n - LAG - 2 in att_end[1::NGR]:
                            head_squares(att_end.index(n - LAG - 2))
                    for v in range(1, NT * NGR, NGR):
                        if att_end[v] + LAG + 2 >= len(att):
                            head_squares(v)
                    act.wait_ge(s["g_ms"], 1)
                    act.activation(gst[:, 1], gst[:, 0], ACT.Sqrt).then_inc(s["g_rt"], 1)
                    for k in range(2):
                        act.activation(xh[:, k], su[:, k], ACT.Copy).then_inc(s["x_hi"], 1)
                    for k in range(2, KD):
                        act.wait_ge(s["turned"], KD + k - 1)
                        act.activation(xh[:, k], ps[k][:], ACT.Identity, scale=pcol[:, R_GN + k:R_GN + k + 1]).then_inc(
                            s["x_hi"], 1)

                    def take_out(b):
                        product_done(act, b)
                        half = b - B_OUT
                        for i in range(NT):
                            square(ps[4 * (b % 2) + i][:], stat[:, 3 * half, i:i + 1], junkz)
                        if half == 1:
                            root(1)
                            stream_squares(0)
                            root(2)
                            turned_high(2 * KD - 2, R_MLP)

                    def take_down(b):
                        half = b - B_DOWN[1]
                        for i in range(NT):
                            act.wait_ge(s["f_sum"], NT * half + i + 1)
                            square(fbuf[:, i, 512 * half:512 * half + 512], stat[:, 3 * half, i:i + 1])
                        if half == 1:
                            root(3)

                    def take_up(part):
                        def take(b):
                            product_done(act, b)
                            for n in range(4):
                                f = 4 * (b - B_UP[part]) + n
                                g = 16 * part + f
                                if g >= 2:
                                    act.wait_ge(s["f_sq"], g - 1)
                                act.activation(act_t[:, g % 2], ps[4 * (b % 2) + n][:], ACT.Relu).then_inc(s["f_relu"], 1)
                                if g >= 1 and f >= 1:
                                    high(g - 1)
                            if b == B_UP[part] + 3:
                                high(16 * part + 15)
                        return take

                    def high(g):
                        act.wait_ge(s["f_sq"], g + 1)
                        if g == 16:
                            product_done(act, B_DOWN[0] + 1)
                        act.activation(fh[:, g % 16], sq_t[:, g % 2], ACT.Copy).then_inc(s["f_hi"], 1)

                    def take(b):
                        if b < B_UP[0]:
                            take_out(b)
                        elif b < B_DOWN[0]:
                            take_up(0)(b)
                        elif b < B_UP[1]:
                            take_half(b)
                        elif b < B_DOWN[1]:
                            take_up(1)(b)
                        else:
                            take_down(b)

                    splits_for(range(B_OUT, len(blocks)), take, done=NSPLIT - 1)
                    stream_squares(NT)
                    act.wait_ge(s["ssq"], squared[0])

                @block.vector
                def _(dve):
                    link = chain(dve, s["dve_steps"])

                    def tt(out_, a, b, op):
                        return dve.tensor_tensor(out_, a, b, op)

                    SQUARES = (0, 2 * NT, 3 * NT, 5 * NT)

                    def root_mean(n):
                        if n:
                            dve.wait_ge(s["ssq"], SQUARES[n])
                        if n % 2:
                            link(tt(stat[:, 0, :], stat[:, 0, :], stat[:, 3, :], ALU.add))
                        dve.tensor_scalar(stat[:, 1, :], stat[:, 0, :], 1.0 / D, EPS, ALU.mult, ALU.add).then_inc(s["msq"], 1)
                        dve.wait_ge(s["rms"], n + 1)
                        link(dve.reciprocal(stat[:, 1, :], stat[:, 2, :]))

                    def pre_norm(n):
                        root_mean(n)
                        for i in range(NT):
                            dve.tensor_scalar(fbuf[:, i], h[:, i], stat[:, 1, i:i + 1], None, ALU.mult).then_inc(s["normed"], 1)

                    def turned_low(first, gains):
                        for k in range(KD):
                            dve.wait_ge(s["x_hi"], first + k + 1)
                            dve.scalar_tensor_tensor(xl[:, k], ps[k][:], pcol[:, gains + k:gains + k + 1], xh[:, k].bitcast(F32),
                                                     ALU.mult, ALU.subtract).then_inc(s["x_lo"], 1)

                    def post_norm(n, which):
                        root_mean(n)
                        for i in range(NT):
                            if which:
                                dve.wait_ge(s["f_gain"], NT + i + 1)
                            dve.scalar_tensor_tensor(h[:, i], fbuf[:, i], stat[:, 1, i:i + 1], h[:, i], ALU.mult,
                                                     ALU.add).then_inc(s["h_new"], 1)

                    def sm_(n):
                        return small[:, n]

                    dve.tensor_copy(pcol[:], pcols[:, layer]).then_inc(s["cols_ready"], 1)
                    pre_norm(0)
                    dve.wait_ge(s["cols_ready"], 1)
                    turned_low(0, R_PRE)

                    lr, li = pcol[:, R_LR:R_LR + NJ], pcol[:, R_LI:R_LI + NJ]
                    dve.wait_ge(s["s5_dt"], 1)
                    link(tt(sm_(S_X), lr, sm_(S_DT), ALU.mult))
                    link(tt(sm_(S_TH), li, sm_(S_DT), ALU.mult))
                    reduce_angle(dve, link, sm_(S_R), sm_(S_TH), sm_(S_T0))
                    absolute(dve, sm_(S_ABS), sm_(S_R)).then_inc(s["s5_ang"], 1)
                    link(dve.tensor_scalar(sm_(S_RHI), sm_(S_R), ROUND13, None, ALU.add))
                    link(dve.tensor_scalar(sm_(S_RHI), sm_(S_RHI), ROUND13, None, ALU.subtract))
                    link(tt(sm_(S_RLO), sm_(S_R), sm_(S_RHI), ALU.subtract))
                    table = [P, NJ, L + 1]
                    stepb = steps[:].unsqueeze(1).to_broadcast(table)
                    link(tt(tang[:], sm_(S_RHI).unsqueeze(2).to_broadcast(table), stepb, ALU.mult))
                    reduce_angle(dve, link, tred[:], tang[:], tnum[:])
                    link(tt(tang[:], sm_(S_RLO).unsqueeze(2).to_broadcast(table), stepb, ALU.mult))
                    link(tt(tred[:], tred[:], tang[:], ALU.add))
                    dve.tensor_scalar(tred[:], tred[:], PI_IN, -PI_IN, ALU.min, ALU.max).then_inc(s["s5_phase"], 1)
                    dve.wait_ge(s["s5_phase"], 1)
                    absolute(dve, tang[:], tred[:]).then_inc(s["s5_phase"], 1)
                    dve.wait_ge(s["s5_trig"], 1)
                    link(tt(sm_(S_ARE), sm_(S_MAG), sm_(S_COS), ALU.mult))
                    link(tt(sm_(S_AIM), sm_(S_MAG), sm_(S_SIN), ALU.mult))
                    link(tt(sm_(S_T0), lr, lr, ALU.mult))
                    link(tt(sm_(S_T1), li, li, ALU.mult))
                    link(tt(sm_(S_DEN), sm_(S_T0), sm_(S_T1), ALU.add))
                    link(dve.reciprocal(sm_(S_RDEN), sm_(S_DEN)))
                    link(dve.tensor_scalar(sm_(S_E), sm_(S_ARE), 1.0, None, ALU.subtract))
                    for out_, (a, b), op in ((S_GRE, (lr, li), ALU.add), (S_GIM, (li, lr), ALU.subtract)):
                        link(tt(sm_(S_T0), sm_(S_E), a, ALU.mult))
                        link(tt(sm_(S_T1), sm_(S_AIM), b, ALU.mult))
                        link(tt(sm_(S_T0), sm_(S_T0), sm_(S_T1), op))
                        link(tt(sm_(out_), sm_(S_T0), sm_(S_RDEN), ALU.mult))
                    dve.wait_ge(s["params_landed"], 16 * N_PARAMS)
                    link(dve.memset(bd[:], 0.0))
                    wide = [P, NJ, GH]
                    gre, gim = (sm_(n).unsqueeze(2).to_broadcast(wide) for n in (S_GRE, S_GIM))
                    t0 = tmp[:, 0, 0:NJ * GH].rearrange("p (j c) -> p j c", j=NJ)
                    t1 = tmp[:, 1, 0:NJ * GH].rearrange("p (j c) -> p j c", j=NJ)
                    for part, (a, b), op in ((0, (0, 1), ALU.add), (1, (1, 0), ALU.subtract)):
                        link(tt(t0, gre, bnat[:, a], ALU.mult))
                        link(tt(t1, gim, bnat[:, b], ALU.mult))
                        for g in range(2):
                            rows_ = slice(g * NP_, (g + 1) * NP_)
                            link(tt(bd[rows_, part, :, g * GH:(g + 1) * GH], t0[rows_], t1[rows_], op))
                    for part in range(2):
                        for c in range(2):
                            for g in range(2):
                                mine = par[:, 2 * part + g:2 * part + g + 1]
                                last = dve.tensor_scalar(cb[:, part, c, g * NP_:(g + 1) * NP_], cnat[:, part, c], mine, None,
                                                         ALU.mult)
                                if (part, c, g) != (1, 1, 1):
                                    link(last)
                    last.then_inc(s["s5_nat"], 1)
                    dve.wait_ge(s["s5_natT"], 2)
                    bt = ps[4][:].rearrange("p (n c) -> p n c", n=4)
                    link(dve.tensor_copy(bT[:], bt))
                    tt(bTl[:], bt, bT[:].bitcast(F32), ALU.subtract)
                    dve.wait_ge(s["bank_out"], 2)
                    for n in range(2):
                        tt(sul[:, n], su[:, n], suh[:, n].bitcast(F32), ALU.subtract)
                    dve.tensor_copy(cT[:], ps[5][:].rearrange("p (a b c) -> p a b c", a=2, b=2)).then_inc(s["s5_mats"], 1)

                    dve.wait_ge(s["s5_table"], 2)
                    chunked = [P, NT, L]

                    def by_chunk(ap):
                        return ap.rearrange("p (c l) -> p c l", c=NT)

                    def cos_sin(j):
                        return (ctab[:, j, 0:L].unsqueeze(1).to_broadcast(chunked),
                                stab[:, j, 0:L].unsqueeze(1).to_broadcast(chunked))

                    for j in range(NJ):
                        cos_, sin_ = cos_sin(j)
                        dve.wait_ge(s["s5_bu"], j + 1)
                        re_, im_ = by_chunk(ps[4 + 2 * (j % 2)][:]), by_chunk(ps[5 + 2 * (j % 2)][:])
                        tt(by_chunk(tmp[:, 0]), re_, cos_, ALU.mult)
                        tt(by_chunk(tmp[:, 1]), im_, sin_, ALU.mult)
                        tt(by_chunk(tmp[:, 2]), im_, cos_, ALU.mult)
                        tt(by_chunk(tmp[:, 3]), re_, sin_, ALU.mult).then_inc(s["s5_rot"], 1)
                        dve.wait_ge(s["s5_rot"], j + 1)
                        tt(vr[:, j], tmp[:, 0], tmp[:, 1], ALU.add)
                        link(tt(vi[:, j], tmp[:, 2], tmp[:, 3], ALU.subtract))
                    last_cos, last_sin = ctab[:, :, L], stab[:, :, L]
                    for c in range(NT):
                        for j in range(NJ):
                            decay = sm_(S_MAG)[:, j:j + 1].to_broadcast([P, L])
                            for v, start in ((vr, S_IRE), (vi, S_IIM)):
                                part = v[:, j, c * L:(c + 1) * L]
                                last = dve.tensor_tensor_scan(part, decay, part,
                                                              sm_(start)[:, j:j + 1] if c else 0.0, ALU.mult, ALU.add)
                        link(last)
                        if c < NT - 1:
                            er, ei = vr[:, :, (c + 1) * L - 1], vi[:, :, (c + 1) * L - 1]
                            tt(sm_(S_T0), last_cos, er, ALU.mult)
                            tt(sm_(S_T1), last_sin, ei, ALU.mult)
                            tt(sm_(S_T2), last_cos, ei, ALU.mult)
                            link(tt(sm_(S_T3), last_sin, er, ALU.mult))
                            tt(sm_(S_IRE), sm_(S_T0), sm_(S_T1), ALU.subtract)
                            link(tt(sm_(S_IIM), sm_(S_T2), sm_(S_T3), ALU.add))
                    for j in range(NJ):
                        cos_, sin_ = cos_sin(j)
                        re_, im_ = by_chunk(vr[:, j]), by_chunk(vi[:, j])
                        tt(by_chunk(tmp[:, 0]), re_, cos_, ALU.mult)
                        tt(by_chunk(tmp[:, 1]), im_, sin_, ALU.mult)
                        tt(by_chunk(tmp[:, 2]), im_, cos_, ALU.mult)
                        link(tt(by_chunk(tmp[:, 3]), re_, sin_, ALU.mult))
                        link(tt(vr[:, j], tmp[:, 0], tmp[:, 1], ALU.subtract))
                        tt(vi[:, j], tmp[:, 2], tmp[:, 3], ALU.add).then_inc(s["s5_x"], 1)
                        dve.wait_ge(s["s5_x"], j + 1)
                    dve.wait_ge(s["s5_x"], NJ)

                    def rope(x, heads):
                        shape = [P, NT, heads, ROT]
                        size = NT * heads * ROT
                        ts = [rtmp[:, n, 0:size].rearrange("p (i a c) -> p i a c", i=NT, a=heads) for n in range(4)]
                        cos_, sin_ = (v[:].unsqueeze(2).to_broadcast(shape) for v in (cosr, sinr))
                        x1, x2 = x[:, :, :, 0:ROT], x[:, :, :, ROT:2 * ROT]
                        tt(ts[0], x1, cos_, ALU.mult)
                        tt(ts[1], x2, sin_, ALU.mult)
                        tt(ts[2], x2, cos_, ALU.mult)
                        link(tt(ts[3], x1, sin_, ALU.mult))
                        tt(x1, ts[0], ts[1], ALU.subtract)
                        return tt(x2, ts[2], ts[3], ALU.add)

                    dve.wait_ge(s["bank_out"], sum(in_banks))
                    rope(z[:, :, ZKC:ZKC + GW].rearrange("p i (a d) -> p i a d", d=HD), NGR).then_inc(s["n_rope"], 1)
                    dve.wait_ge(s["n_rope"], 1)
                    for n in range(2):
                        dve.wait_ge(s["s5_y"], n + 1)
                        dve.scalar_tensor_tensor(tmp[:, n], su[:, n], pcol[:, R_D + n:R_D + n + 1], ps[4 + n][:], ALU.mult,
                                                 ALU.add).then_inc(s["s5_ypre"], 1)
                    for kv, pe_row in ((0, R_PEK), (1, R_PEV)):
                        dve.wait_ge(s["n_kT"], 1 + kv)
                        for g in range(NGR):
                            src = ps[2 + kv][g * HD:(g + 1) * HD, :].rearrange("p (m q) -> p q m", q=CS_)
                            for q in range(2):
                                to = slice(q * HD, (q + 1) * HD)
                                for half in range(2):
                                    js = slice(half * 8, half * 8 + 8)
                                    last = tt(flat[to, kv, js, g, :], src[:, q::2, half:half + NCMP],
                                              pcol[to, pe_row + half * 8:pe_row + half * 8 + 8].unsqueeze(2).to_broadcast(
                                                  [HD, 8, NCMP]), ALU.add)
                        last.then_inc(s["n_flat"], 1)
                    for n in range(2):
                        dve.wait_ge(s["s5_sig"], n + 1)
                        link(tt(su[:, n], tmp[:, 2 + n], tmp[:, n], ALU.mult))
                        tt(tmp[:, n], su[:, n], su[:, n], ALU.mult).then_inc(s["s5_sq"], 1)
                    dve.wait_ge(s["m_gateT"], 1)
                    link(dve.tensor_scalar(rows[:, 0], ps[0][0:MH, :], gateb[:, 0:1], None, ALU.add))
                    link(dve.tensor_scalar(rows[:, 5], ps[1][0:MH, :], gateb[:, 1:2], None, ALU.add))
                    absolute(dve, rows[:, 6], rows[:, 5]).then_inc(s["m_fx"], 1)
                    for n in range(2):
                        dve.wait_ge(s["s5_rt"], n + 1)
                        link(dve.reciprocal(tmp[:, 2 + n], tmp[:, n]))
                        dve.scalar_tensor_tensor(su[:, n], su[:, n], pcol[:, R_GN + n:R_GN + n + 1], tmp[:, 2 + n], ALU.mult,
                                                 ALU.mult).then_inc(s["s5_done"], 1)

                    dve.wait_ge(s["m_ln"], 1)
                    link(dve.scalar_tensor_tensor(rows[:, 1], rows[:, 5], 0.0, rows[:, 6], ALU.min, ALU.subtract))
                    dve.tensor_tensor_scan(rows[:, 2], keep[:], rows[:, 1], 0.0, ALU.mult, ALU.add)
                    link(dve.tensor_tensor_scan(rows[:, 3], rows[:, 1], rows[:, 0], 0.0, ALU.add, ALU.max))
                    tt(rows[:, 4], rows[:, 2], rows[:, 3], ALU.subtract)
                    tt(rows[:, 0], rows[:, 0], rows[:, 2], ALU.subtract)
                    dve.memset(msr[:, 0:1], 0.0)
                    link(dve.tensor_copy(msr[:, 1:NT], rows[:, 3, L - 1:T - 1:L]))
                    crow = [MH, NT, L]
                    tt(by_chunk(rows[:, 5]), by_chunk(rows[:, 4]), msr[:].unsqueeze(2).to_broadcast(crow), ALU.add)
                    tt(by_chunk(rows[:, 6]), by_chunk(rows[:, 0]),
                       by_chunk(rows[:, 4])[:, :, L - 1:L].to_broadcast(crow), ALU.add)
                    dve.tensor_scalar(rows[:, 7], rows[:, 3], -1.0, None, ALU.mult).then_inc(s["m_rows"], 1)
                    dve.wait_ge(s["m_pad"], 1)
                    for n in range(2):
                        tap = lambda k: pcol[:, R_CONV + 4 * k + n:R_CONV + 4 * k + n + 1]
                        link(dve.tensor_scalar(qk[:, n], qkr[:, n, 0:T], tap(0), None, ALU.mult))
                        for k in range(1, KCONV):
                            last = dve.scalar_tensor_tensor(qk[:, n], qkr[:, n, k:k + T], tap(k), qk[:, n], ALU.mult, ALU.add)
                            if k < KCONV - 1:
                                link(last)
                        last.then_inc(s["m_conv"], 1)
                    dve.wait_ge(s["m_colT"], 1)
                    dve.tensor_copy(dec[:], ps[3][:, 0:2 * NT].rearrange("p (a c) -> p a c", a=2))
                    link(dve.tensor_copy(colt[:], ps[2][:, 0:4 * NT * MH].rearrange("p (a c n) -> p a c n", a=4, c=NT)))
                    dve.tensor_scalar(colt[:, 2], colt[:, 2], HD ** -0.5, None, ALU.mult).then_inc(s["m_cols"], 1)
                    dve.wait_ge(s["m_cols"], 1)
                    dve.wait_ge(s["m_conv_k"], 2)
                    for head in range(MH):
                        dve.wait_ge(s["m_bc"], head + 1)
                        for c in range(NT):
                            span = slice(c * L, (c + 1) * L)
                            last = dve.scalar_tensor_tensor(wT[:, head, span], ps[4 + head][:, span],
                                                            colt[:, 0, c, head:head + 1], maskT[:], ALU.add, ALU.add)
                        last.then_inc(s["m_arg"], 1)
                    for n in range(2):
                        dve.wait_ge(s["m_kT"], n + 1)
                        tt(kw[:, :, 2 * n:2 * n + 2], ps[n][:].rearrange("p (c a d) -> p c a d", c=NT, a=2),
                           colt[:, 2, :, 2 * n:2 * n + 2].unsqueeze(3).to_broadcast([P, NT, 2, HD]), ALU.mult).then_inc(s["m_kw"], 1)
                    for head in range(MH):
                        dve.wait_ge(s["m_s"], head + 1)
                        dve.wait_ge(s["m_w"], head + 1)
                        dve.scalar_tensor_tensor(wT[:, head], ps[4 + head][:], HD ** -0.5, wT[:, head], ALU.mult,
                                                 ALU.mult).then_inc(s["m_p"], 1)
                    W1 = HD + 1
                    for c in range(NT):
                        dve.wait_ge(s["m_chunk"], c + 1)
                        if c == 0:
                            dve.tensor_copy(cst[:], ps[2][:, 0:2 * W1].rearrange("p (a d) -> p a d", a=2)).then_inc(s["m_state"], 1)
                            dve.tensor_copy(nu[:, 0], ps[0][:, 0:MH * W1].rearrange("p (n d) -> p n d", n=MH)).then_inc(s["m_nu"], 1)
                            link(rope(z[:, :, ZQ:ZQ + NSA].rearrange("p i (a d) -> p i a d", d=HD), NH))
                            continue
                        if c < NT - 1:
                            dve.wait_ge(s["m_state"], 2 * c - 1)
                            for a in range(2):
                                dve.scalar_tensor_tensor(cst[:, a], cst[:, a], dec[:, a, c:c + 1], ps[2][:, a * W1:(a + 1) * W1],
                                                         ALU.mult, ALU.add).then_inc(s["m_state"], 1)
                        for odd in range(2):
                            link(tt(mtmp[:, odd::2], ps[1 + 2 * odd][:, 0:2 * W1].rearrange("p (n d) -> p n d", n=2),
                                    colt[:, 1, c, odd::2].unsqueeze(2).to_broadcast([P, 2, W1]), ALU.mult))
                        tt(nu[:, c], mtmp[:], ps[CHUNK_BANK[c]][:, 0:MH * W1].rearrange("p (n d) -> p n d", n=MH), ALU.add).then_inc(
                            s["m_nu"], 1)
                        if c == 1:
                            link(rope(z[:, :, ZKS:ZKS + GW].rearrange("p i (a d) -> p i a d", d=HD), NGR))
                            rope(z[:, :, ZKW:ZKW + GW].rearrange("p i (a d) -> p i a d", d=HD), NGR).then_inc(s["n_rope"], 1)
                    dve.wait_ge(s["m_nu"], NT)
                    link(absolute(dve, mden[:, 0], nu[:, :, :, HD]))
                    link(tt(mden[:, 0], mden[:, 0], colt[:, 3], ALU.max))
                    link(dve.reciprocal(mden[:, 1], mden[:, 0]))
                    dve.wait_ge(s["m_so"], 1)
                    for i in range(NT):
                        yt = ytok[:, i, 0:MLS].rearrange("p (n d) -> p n d", n=MH)
                        link(tt(yt, nu[:, i, :, 0:HD], mden[:, 1, i].unsqueeze(2).to_broadcast([P, MH, HD]), ALU.mult))
                    for i in range(NT):
                        last = tt(ytok[:, i, 0:MLS], ytok[:, i, 0:MLS], so[:, i], ALU.mult)
                    last.then_inc(s["m_out"], 1)

                    for r in range(R):
                        dve.wait_ge(s["n_q"], r + 1)
                        tt(ql[:, r], ps[r][:], qh[:, r].bitcast(F32), ALU.subtract).then_inc(s["n_ql"], 1)
                    dve.wait_ge(s["n_va"], N_VA)
                    for n in range(2):
                        dve.wait_ge(s["n_kh"], n + 1)
                        for g in range(NGR):
                            rows_ = slice(g * HD, (g + 1) * HD)
                            last = tt(ksl[rows_, n, g], ps[5 + n][rows_, :], ksh[rows_, n, g].bitcast(F32), ALU.subtract)
                        last.then_inc(s["n_k"], 1)
                    dve.wait_ge(s["n_kch"], 1)
                    for g in range(NGR):
                        rows_ = slice(g * HD, (g + 1) * HD)
                        tt(kcl[rows_, g, 0:NCMP], ps[7][rows_, 0:NCMP], kch[rows_, g, 0:NCMP].bitcast(F32), ALU.subtract)
                    dve.tensor_copy(vca[0:NCMP, :, 0:HD], ps[4][0:NCMP, 0:GW].rearrange(
                        "p (g d) -> p g d", g=NGR)).then_inc(s["n_kc"], 1)
                    dve.wait_ge(s["n_gate"], 1)

                    def maxima(v, r):
                        i, slot = tile_of[v], v % 4
                        width = (i + 1) * P
                        bank = 0 if v else 2 * r
                        if v >= 4 and r == 0:
                            dve.wait_ge(s["n_diag_rest"], 2 * (v - 3))
                            dve.wait_ge(s["n_diag"], v - 3)
                        n_win = min(i + 1, WIN // P + 1)
                        dve.wait_ge(s["n_score"], R * v + r + 1)
                        for kind, scores_, msk in (
                            (COMPRESSED, ps[bank + 1][:, 384:384 + NCMP], cmask[:, i, 0:NCMP]),
                            (WINDOW, ps[bank + 1][:, 0:n_win * P], wmask[:, 384 - n_win * P:384]),
                            (SELECTED, ps[bank][:, 0:width], mask[:, 512 - width:512]),
                        ):
                            last = dve.tensor_tensor_reduce(scores_, scores_, msk, 1.0, 3 * NEG,
                                                            ALU.add, ALU.max, am[:, slot, 3 * r + kind:3 * r + kind + 1])
                        last.then_inc(s["n_max"], 1)

                    def diagonals(v):
                        slot = v % 2
                        if v >= 2:
                            dve.wait_ge(s["n_shifted"], att_end[v - 2])
                        dve.wait_ge(s["n_max"], R * (v + 1))
                        shift = am[:, v % 4].rearrange("p (r k) -> p k r", k=3)[:, SELECTED].unsqueeze(2)
                        tt(diag[:, slot, SELECTED], nident[:].unsqueeze(1).to_broadcast([P, R, P]),
                           shift.to_broadcast([P, R, P]), ALU.mult).then_inc(s["n_diag"], 1)

                    def gated(v):
                        i, g, slot = tile_of[v], v % NGR, v % 2
                        dve.wait_ge(s["n_av"], att_end[v])
                        if v >= 2:
                            dve.wait_ge(s["n_y"], 2 * (v - 1))
                        o = [ps[6 + n][:, 0:6 * (HD + 1)].rearrange("p (k d) -> p k d", d=HD + 1) for n in range(2)]
                        for n in range(2):
                            last = dve.reciprocal(cf[:, slot, 6 * n:6 * n + 6], o[n][:, :, HD])
                        link(last)
                        link(tt(cf[:, slot], cf[:, slot], gate[:, i, 3 * R * g:3 * R * (g + 1)], ALU.mult))
                        if i == 0:
                            for r in range(R):
                                one = cf[:, slot, 3 * r + COMPRESSED:3 * r + COMPRESSED + 1]
                                last = tt(one, one, cvalid[:], ALU.mult)
                            link(last)
                        for n in range(2):
                            last = tt(prod[:, slot, 2 * n:2 * n + 2].rearrange("p r k d -> p (r k) d"), o[n][:, :, 0:HD],
                                      cf[:, slot, 6 * n:6 * n + 6].unsqueeze(2).to_broadcast([P, 6, HD]), ALU.mult)
                        last.then_inc(s["n_o"], 1)

                    for r in range(R):
                        maxima(0, r)
                    diagonals(0)
                    for n in range(len(att) + LAG):
                        if n - LAG + 1 in att_end:
                            gated(att_end.index(n - LAG + 1))
                        for v, r in maxima_after.get(n, ()):
                            maxima(v, r)
                        for v in diagonals_after.get(n, ()):
                            diagonals(v)

                    heads = MH + NH
                    for n, i in enumerate(tile_of[::NGR]):
                        dve.wait_ge(s["g_sq"], n + 1)
                        last = dve.tensor_reduce(gst[:, 2, i], gsq[:, i].rearrange("p (n d) -> p n d", d=HD), AX, ALU.add)
                    link(last)
                    dve.tensor_scalar(gst[:, 0], gst[:, 2], 1.0 / HD, EPS, ALU.mult, ALU.add).then_inc(s["g_ms"], 1)
                    dve.wait_ge(s["g_rt"], 1)
                    link(dve.reciprocal(gst[:, 2], gst[:, 1]))
                    for i in tile_of[::NGR]:
                        yt = ytok[:, i].rearrange("p (n d) -> p n d", d=HD)
                        tt(yt, yt, gst[:, 2, i].unsqueeze(2).to_broadcast([P, heads, HD]), ALU.mult).then_inc(s["g_y"], 1)
                    for k in range(2):
                        dve.wait_ge(s["x_hi"], KD + k + 1)
                        tt(xl[:, k], su[:, k], xh[:, k].bitcast(F32), ALU.subtract).then_inc(s["x_lo"], 1)
                    for k in range(2, KD):
                        dve.wait_ge(s["x_hi"], KD + k + 1)
                        dve.scalar_tensor_tensor(xl[:, k], ps[k][:], pcol[:, R_GN + k:R_GN + k + 1], xh[:, k].bitcast(F32),
                                                 ALU.mult, ALU.subtract).then_inc(s["x_lo"], 1)

                    dve.wait_ge(s["gains_landed"], 32)
                    for half in range(2):
                        b = B_OUT + half
                        for i in range(NT):
                            dve.wait_ge(s["ssq"], NT * half + i + 1)
                            cols = slice(512 * half, 512 * half + 512)
                            last = tt(fbuf[:, i, cols], ps[4 * (b % 2) + i][:], gpost[:, 0, cols], ALU.mult)
                    link(last)
                    post_norm(1, 0)
                    dve.wait_ge(s["h_new"], NT)
                    pre_norm(2)
                    turned_low(2 * KD, R_MLP)
                    for part in range(2):
                        for g in range(16 * part, 16 * part + 16):
                            b, n = B_UP[part] + g % 16 // 4, g % 4
                            dve.wait_ge(s["f_relu"], g + 1)
                            if g >= 2:
                                dve.wait_ge(s["f_lo"], g - 1)
                            dve.scalar_tensor_tensor(sq_t[:, g % 2], ps[4 * (b % 2) + n][:], 0.0, act_t[:, g % 2], ALU.max,
                                                     ALU.mult).then_inc(s["f_sq"], 1)
                            if g % 16:
                                low(dve, g - 1, fl, fh, sq_t, s)
                        low(dve, 16 * part + 15, fl, fh, sq_t, s)
                    for half in range(2):
                        b = B_DOWN[1] + half
                        dve.wait_ge(s["w_used"], blocks[b][0] + blocks[b][1])
                        for i in range(NT):
                            into = fbuf[:, i, 512 * half:512 * half + 512]
                            tt(into, into, ps[4 * (b % 2) + i][:], ALU.add).then_inc(s["f_sum"], 1)
                    post_norm(3, 1)

                @block.tensor
                def _(pe):
                    def product(b, inputs=None, between=()):
                        first, deep, on_features, width = blocks[b]
                        group = 4 * (b % 2) if b >= B_OUT else 0
                        between = dict(between)

                        def bank_free(k, n):
                            if inputs and k == 0 and n < inputs[2]:
                                pe.wait_ge(s[inputs[0]], inputs[1] + n + 1)
                            if 0 < b < B_OUT and k == 0:
                                pe.wait_ge(s["bank_out"], sum(in_banks[:b - 1]) + min(n, in_banks[b - 1] - 1) + 1)

                        def bank_done(k, n, last):
                            if b < B_OUT and k == deep - 1 and n < in_banks[b] - 1:
                                last.then_inc(s["bank_done"], 1)

                        hi, lo = (fh, fl) if b in (B_DOWN[0], B_DOWN[0] + 1, B_DOWN[1], B_DOWN[1] + 1) else (xh, xl)
                        for k in range(deep):
                            unit = first + k
                            slot = unit % NSPLIT
                            pe.wait_ge(s["w_lo"], unit + 1)
                            if inputs:
                                pe.wait_ge(s[inputs[0]], inputs[1] + k + 1)
                            if on_features:
                                for n in range(width // P):
                                    cols = slice(n * P, (n + 1) * P)
                                    bank_free(k, n)
                                    for m, (w, x) in enumerate(((wh, hi), (wh, lo), (wl, hi))):
                                        last = pe.matmul(ps[group + n][:], w[:, slot, cols], x[:, k], start=k == 0 and m == 0,
                                                         stop=k == deep - 1 and m == 2)
                                    bank_done(k, n, last)
                            else:
                                for i in range(NT):
                                    rows_ = slice(i * P, (i + 1) * P)
                                    bank_free(k, i)
                                    for m, (x, w) in enumerate(((hi, wh), (hi, wl), (lo, wh))):
                                        last = pe.matmul(ps[group + i][:, 0:width], x[:, k, rows_], w[:, slot, 0:width],
                                                         start=k == 0 and m == 0, stop=k == deep - 1 and m == 2)
                                    bank_done(k, i, last)
                            last.then_inc(s["w_used"], 1)
                            if k in between:
                                between[k]()

                    def turn(src, bank, count, ready, before, order=range(NT)):
                        for n, i in enumerate(order):
                            pe.wait_ge(s[ready], before + n + 1)
                            for k in range(count):
                                last = pe.transpose(ps[bank + k][:, i * P:(i + 1) * P], src[:, i, k * P:(k + 1) * P], ident[:])
                                if n == NT - 1:
                                    last.then_inc(s["turned"], 1)

                    turn(fbuf, 0, KD, "normed", 0)

                    def s5_turn():
                        pe.wait_ge(s["x_lo"], KD)
                        pe.wait_ge(s["s5_nat"], 1)
                        for n in range(4):
                            last = pe.transpose(ps[4][:, n * P:(n + 1) * P],
                                                bd[:, n // 2, 4 * (n % 2):4 * (n % 2) + 4].rearrange("p j c -> p (j c)"),
                                                ident[:])
                        last.then_inc(s["s5_natT"], 1)
                        for n in range(4):
                            last = pe.transpose(ps[5][:, n * P:(n + 1) * P], cb[:, n // 2, n % 2], ident[:])
                        last.then_inc(s["s5_natT"], 1)

                    def s5_input(j):
                        def run():
                            if j == 0:
                                pe.wait_ge(s["s5_mats"], 1)
                            if j >= 2:
                                pe.wait_ge(s["s5_rot"], j - 1)
                            rows_ = slice(32 * (j % 4), 32 * (j % 4) + 32)
                            for part in range(2):
                                mat = slice(2 * part + j // 4, 2 * part + j // 4 + 1)
                                for m, (w, x) in enumerate(((bT, suh), (bT, sul), (bTl, suh))):
                                    last = pe.matmul(ps[4 + 2 * (j % 2) + part][:], w[rows_, mat.start], x[rows_, j // 4],
                                                     start=m == 0, stop=m == 2)
                            last.then_inc(s["s5_bu"], 1)
                        return run

                    s5_steps = {2 * KD - 1: s5_turn}
                    s5_steps.update({2 * KD + 1 + j: s5_input(j) for j in range(NJ)})
                    for b in range(B_OUT):
                        product(b, ("x_lo", 0, 4) if b == 0 else None,
                                {k - b * KD: step for k, step in s5_steps.items() if k // KD == b})

                    for n in range(2):
                        for q in range(4):
                            rows_ = slice(32 * q, 32 * q + 32)
                            pe.wait_ge(s["s5_x"], 4 * n + q + 1)
                            for part, v in enumerate((vr, vi)):
                                last = pe.matmul(ps[4 + n][rows_, :], cT[:, part, n, rows_], v[:, 4 * n + q], start=part == 0,
                                                 stop=part == 1)
                        last.then_inc(s["s5_y"], 1)
                    pe.wait_ge(s["bank_out"], sum(in_banks))
                    for n, a in enumerate((ZI, ZFG)):
                        for i in range(NT):
                            last = pe.transpose(ps[n][0:MH, i * P:(i + 1) * P], z[:, i, a:a + MH], ident[:])
                    last.then_inc(s["m_gateT"], 1)

                    def keys_turned(bank, a):
                        for i in range(NT):
                            last = pe.transpose(ps[bank][:, i * P:(i + 1) * P], z[:, i, a:a + GW], ident[:])
                        last.then_inc(s["n_kT"], 1)

                    pe.wait_ge(s["n_rope"], 1)
                    keys_turned(2, ZKC)
                    keys_turned(3, ZVC)
                    pe.wait_ge(s["s5_gelu"], 2)
                    for m in range(2):
                        for c in range(2):
                            last = pe.matmul(ps[6 + m][:], wglu[:, c, m * P:(m + 1) * P], tmp[:, 2 + c], start=c == 0, stop=c == 1)
                        last.then_inc(s["s5_glu"], 1)
                    for m in range(2):
                        pe.wait_ge(s["s5_sq"], m + 1)
                        pe.matmul(ps[4 + m][:], bones[:], tmp[:, m], start=True, stop=True).then_inc(s["s5_ms"], 1)

                    pe.wait_ge(s["s5_sig"], 2)
                    pe.wait_ge(s["n_flat"], 2)
                    for k, n in enumerate(wholes):
                        kv, j0 = k // (len(wholes) // 2), 2 * (k % (len(wholes) // 2))
                        pe.wait_ge(raw_landed[n % NRAW], 16 * (n // NRAW + 1))
                        for jj in range(2):
                            for c in range(2):
                                col = (2 * kv + c) * NGR * NCMP
                                last = pe.matmul(ps[6][:, col:col + NGR * NCMP],
                                                 raw[:, n % NRAW, jj * CHID + c * P:jj * CHID + (c + 1) * P],
                                                 flat[:, kv, j0 + jj].rearrange("p g n -> p (g n)"),
                                                 start=k == 0 and jj == 0 and c == 0, stop=j0 + jj == CB // 2 - 1,
                                                 skip_group_check=True)
                        last.then_inc(s["whole_used"], 1)

                    pe.wait_ge(s["m_exp"], 1)
                    for a, row in enumerate((0, 5, 6, 7)):
                        for c in range(NT):
                            col = (a * NT + c) * MH
                            pe.transpose(ps[2][:, col:col + MH], rows[:, row, c * L:(c + 1) * L], ident[0:MH, 0:MH])
                    for a in range(2):
                        last = pe.matmul(ps[3][:, a * NT:(a + 1) * NT], sel2[:, a], rows[:, 5, L - 1:T:L], start=True, stop=True)
                    last.then_inc(s["m_colT"], 1)
                    pe.wait_ge(s["s5_rt"], 2)
                    pe.wait_ge(s["n_hid"], 4)
                    for head in range(MH):
                        pe.matmul(ps[4 + head][:], sel[:, head], rows[:, 4], start=True, stop=True).then_inc(s["m_bc"], 1)
                    pe.wait_ge(s["m_qk"], 4)
                    for n in range(2):
                        for c in range(NT):
                            last = pe.transpose(ps[n][:, c * L:(c + 1) * L], qk[:, 2 + n, c * L:(c + 1) * L], ident[:])
                        last.then_inc(s["m_kT"], 1)
                    for head in range(MH):
                        pe.wait_ge(s["m_arg"], head + 1)
                        rows_ = slice(HD * (head % 2), HD * (head % 2) + HD)
                        for c in range(NT):
                            span = slice(c * L, (c + 1) * L)
                            last = pe.matmul(ps[4 + head][:, span], qk[rows_, 2 + head // 2, span], qk[rows_, head // 2, span],
                                             start=True, stop=True)
                        last.then_inc(s["m_s"], 1)
                    W1 = HD + 1
                    pe.wait_ge(s["m_kw"], 2)
                    pe.wait_ge(s["m_va"], 1 + NT)
                    pe.wait_ge(s["m_cols"], 1)
                    for c in range(NT):
                        span = slice(c * L, (c + 1) * L)
                        if c:
                            pe.wait_ge(s["m_state"], 2 * c - 1)
                        for head in range(MH):
                            if c == 0:
                                pe.wait_ge(s["m_p"], head + 1)
                            rows_ = slice(HD * (head % 2), HD * (head % 2) + HD)
                            cols = slice(head * W1, (head + 1) * W1)
                            last = pe.matmul(ps[CHUNK_BANK[c]][:, cols], wT[:, head, span], va[:, c, head], start=True, stop=True)
                            if c < NT - 1:
                                a = head // 2
                                last = pe.matmul(ps[2][rows_, a * W1:(a + 1) * W1], kw[:, c, head], va[:, c, head], start=True,
                                                 stop=True)
                        if c:
                            pe.wait_ge(s["m_nu"], c)
                            for head in range(MH):
                                rows_ = slice(HD * (head % 2), HD * (head % 2) + HD)
                                cols = slice(head // 2 * W1, (head // 2 + 1) * W1)
                                last = pe.matmul(ps[1 + 2 * (head % 2)][:, cols], qk[rows_, head // 2, span],
                                                 cst[rows_, head // 2], start=True, stop=True)
                        last.then_inc(s["m_chunk"], 1)

                    pe.wait_ge(s["n_rope"], 2)
                    pe.wait_ge(s["m_nu"], NT)
                    for g in range(NGR):
                        blocks_ = slice(g * NCMP, (g + 1) * NCMP)
                        for c in range(2):
                            pe.matmul(ps[7][g * HD:(g + 1) * HD, 0:NCMP], w2c[:, 0, c], hg[:, c, blocks_], start=c == 0, stop=c == 1)
                        for c in range(2):
                            last = pe.matmul(ps[4][0:NCMP, g * HD:(g + 1) * HD], hg[:, 2 + c, blocks_], w2c[:, 1, c],
                                             start=c == 0, stop=c == 1)
                    last.then_inc(s["n_kcT"], 1)
                    for r in range(R):
                        for i in range(NT):
                            if r == 0:
                                pe.wait_ge(s["n_qa"], i + 1)
                            last = pe.transpose(ps[r][:, i * P:(i + 1) * P], qa[:, i, r].rearrange("p g d -> p (g d)"), ident[:])
                        last.then_inc(s["n_qT"], 1)
                    keys_turned(5, ZKS)
                    keys_turned(6, ZKW)
                    pe.wait_ge(s["n_kc"], 1)
                    pe.wait_ge(s["n_k"], 2)

                    def scores(v, r):
                        i, g = tile_of[v], v % NGR
                        n_win = min(i + 1, WIN // P + 1)
                        bank = 0 if v else 2 * r
                        if v:
                            pe.wait_ge(s["n_max"], R * v + r)
                        q = qh[:, r, i * P:(i + 1) * P]
                        pe.matmul(ps[bank][:, 0:(i + 1) * P], q, ksh[:, 0, g, 0:(i + 1) * P], start=True, stop=True)
                        pe.matmul(ps[bank + 1][:, 0:n_win * P], q, ksh[:, 1, g, (i + 1 - n_win) * P:(i + 1) * P], start=True,
                                  stop=True)
                        pe.matmul(ps[bank + 1][:, 384:384 + 32], q, kch[:, g, 0:32], start=True, stop=True).then_inc(
                            s["n_score"], 1)

                    def shifted(n):
                        v, kind, tile = att[n]
                        i, g, slot = tile_of[v], v % NGR, v % 2
                        cols = slice(tile * P, (tile + 1) * P)
                        if kind == SELECTED:
                            pe.wait_ge(s["n_diag"], v + 1)
                        else:
                            pe.wait_ge(s["n_diag_rest"], 2 * v + (1 if kind == COMPRESSED else 2))
                        if n >= 4:
                            pe.wait_ge(s["n_exp"], n - 3)
                        bank = ps[2 + n % 4][:].rearrange("p (r q) -> p r q", r=R)
                        if kind == COMPRESSED:
                            kh, kl = kch[:, g], kcl[:, g]
                        else:
                            kh, kl = (x[:, kind - SELECTED, g, cols] for x in (ksh, ksl))
                        q_high, q_low = (x[:, :, i * P:(i + 1) * P] for x in (qh, ql))
                        pe.matmul(bank, kh, q_high, start=True, stop=False)
                        pe.matmul(bank, kh, q_low, start=False, stop=False)
                        pe.matmul(bank, kl, q_high, start=False, stop=False)
                        msk = None
                        if kind == COMPRESSED:
                            msk = cmaskT[:, i]
                        elif tile == i:
                            msk = wmaskT[:, 2]
                        elif kind == WINDOW and tile == i - WIN // P:
                            msk = wmaskT[:, 0]
                        if msk is not None:
                            pe.matmul(bank, identr[:], msk.unsqueeze(1).to_broadcast([P, R, P]), start=False, stop=False)
                        pe.matmul(bank, onesr[:], diag[:, slot, kind], start=False, stop=True).then_inc(
                            s["n_shifted"], 1)

                    def values(n):
                        v, kind, tile = att[n]
                        g = v % NGR
                        pe.wait_ge(s["n_exp"], n + 1)
                        first = n == 0 or att[n - 1][0] != v
                        if first and v:
                            pe.wait_ge(s["n_o"], v)
                        final = n + 1 == att_end[v]
                        val = vca[:, g] if kind == COMPRESSED else vsw[:, kind - SELECTED, tile, g]
                        for r in range(R):
                            col = (3 * (r % 2) + kind) * (HD + 1)
                            last = pe.matmul(ps[6 + r // 2][:, col:col + HD + 1], pT[:, n % 4, r], val,
                                             start=first and r % 2 == 0, stop=final and r % 2 == 1,
                                             skip_group_check=True)
                        last.then_inc(s["n_av"], 1)

                    pe.wait_ge(s["n_va"], N_VA)
                    for r in range(R):
                        scores(0, r)
                    for n in range(len(att) + LAG):
                        if n < len(att):
                            shifted(n)
                        under_way = n < len(att) and n >= LAG and att[n - LAG][0] == att[n][0]
                        if under_way:
                            for v, r in maxima_after.get(n, ()):
                                scores(v, r)
                        if n >= LAG:
                            values(n - LAG)
                        if not under_way:
                            for v, r in maxima_after.get(n, ()):
                                scores(v, r)

                    turn(ytok, 2, KD - 2, "g_y", 0, tile_of[::NGR])
                    for b in range(B_OUT, B_OUT + 2):
                        product(b, ("x_lo", KD, 4) if b == B_OUT else None)
                    turn(fbuf, 0, KD, "normed", NT)
                    for part in range(2):
                        for n in range(4):
                            b = B_UP[part] + n
                            if part and n < 2:
                                pe.wait_ge(s["evacuated"], n + 1)
                            elif n >= 2:
                                pe.wait_ge(s["f_sq"], 16 * part + 4 * (n - 1))
                            product(b, ("x_lo", 2 * KD, 4) if b == B_UP[0] else None)
                        pe.wait_ge(s["f_sq"], 16 * part + 12)
                        product(B_DOWN[part], ("f_lo", 16 * part, 0))
                        product(B_DOWN[part] + 1)
            nc.multi_engine_barrier(list(nc.engines), sems_to_clear=layer_sems)

        with nc.Block() as block:
            @block.sync
            def _(sp):
                sp.dma_start(out[0].rearrange("(i p) d -> p i d", p=P), h[:]).then_inc(once["stored"], 16)
                sp.wait_ge(once["stored"], 16)


def kernel(**inputs):
    import concourse.bacc as bacc
    import numpy as np
    from concourse.bass_utils import run_bass_kernel_spmd

    nc = bacc.Bacc("TRN2", target_bir_lowering=False, num_devices=1)
    arrays, tensors = {}, {}
    for name, value in inputs.items():
        a = np.ascontiguousarray(value)
        arrays[f"in_{name}"] = a
        tensors[name] = nc.dram_tensor(f"in_{name}", a.shape, mybir.dt.from_np(a.dtype), kind="ExternalInput").ap()
    out = nc.dram_tensor("out", (1, T, D), F32, kind="ExternalOutput").ap()
    build(nc, tensors, out)
    result = run_bass_kernel_spmd(nc, [arrays], core_ids=[0])
    return result.results[0]["out"]
```
